# Optimizing a Trainium2 kernel written in Bass

```python
import math
import jax, jax.numpy as jnp
from jax import lax
import numpy as np

D_MODEL = 1024
BATCH = 1
SEQ = 256
DEPTH = 2

N_A_LAYERS = DEPTH // 2
N_B_LAYERS = DEPTH - N_A_LAYERS
PLE_DIM = 256
SSM_DIM = D_MODEL
SSM_GROUP_DIM = 16
SSM_GROUPS = SSM_DIM // SSM_GROUP_DIM
SSM_STATE = 64
SSM_CHUNK = 128
N_HEADS = 8
HEAD_DIM = 64
Q_BLOCK = 128
REL_BUCKETS = 32
REL_MAX_EXACT = REL_BUCKETS // 2
REL_MAX_DIST = 128
D_FF = 2816
CONV_WIDTH = 3
NEG_INF = -1e30
EPS = 1e-6


def rms_norm(x, g):
    xf = x.astype(jnp.float32)
    y = xf * lax.rsqrt(jnp.mean(xf * xf, axis=-1, keepdims=True) + EPS)
    return (y * g.astype(jnp.float32)).astype(x.dtype)

def _ssm_combine(e_i, e_j):
    ar_i, ai_i, br_i, bi_i = e_i
    ar_j, ai_j, br_j, bi_j = e_j
    return (ar_j * ar_i - ai_j * ai_i,
            ar_j * ai_i + ai_j * ar_i,
            ar_j * br_i - ai_j * bi_i + br_j,
            ar_j * bi_i + ai_j * br_i + bi_j)

def s5_mixer(h, w_in, log_dt, lam_re, lam_im, b_re, b_im, c_re, c_im, d_skip, w_glu):
    f32 = jnp.float32
    bsz, seqlen, _ = h.shape
    u = h @ w_in
    dt = jnp.exp(log_dt.astype(f32))[:, None]
    lr = lam_re.astype(f32)
    li = lam_im.astype(f32)
    mag = jnp.exp(lr * dt)
    ab_r = mag * jnp.cos(li * dt)
    ab_i = mag * jnp.sin(li * dt)
    den = lr * lr + li * li
    f_r = ((ab_r - 1.0) * lr + ab_i * li) / den
    f_i = (ab_i * lr - (ab_r - 1.0) * li) / den
    br = b_re.astype(f32)
    bi = b_im.astype(f32)
    bb_r = f_r[..., None] * br - f_i[..., None] * bi
    bb_i = f_r[..., None] * bi + f_i[..., None] * br
    cr = c_re.astype(f32)
    ci = c_im.astype(f32)
    n_chunks = seqlen // SSM_CHUNK
    uc = u.astype(f32).reshape(bsz, n_chunks, SSM_CHUNK, SSM_GROUPS, SSM_GROUP_DIM)
    uc = uc.transpose(1, 2, 0, 3, 4)
    a_shape = (SSM_CHUNK, bsz, SSM_GROUPS, SSM_STATE)
    a_r = jnp.broadcast_to(ab_r, a_shape)
    a_i = jnp.broadcast_to(ab_i, a_shape)

    def chunk_step(carry, u_chunk):
        x_r0, x_i0 = carry
        bu_r = jnp.einsum("tbgc,gpc->tbgp", u_chunk, bb_r)
        bu_i = jnp.einsum("tbgc,gpc->tbgp", u_chunk, bb_i)
        pw_r, pw_i, s_r, s_i = lax.associative_scan(
            _ssm_combine, (a_r, a_i, bu_r, bu_i), axis=0)
        x_r = s_r + pw_r * x_r0 - pw_i * x_i0
        x_i = s_i + pw_r * x_i0 + pw_i * x_r0
        y = (jnp.einsum("tbgp,gcp->tbgc", x_r, cr)
             - jnp.einsum("tbgp,gcp->tbgc", x_i, ci))
        return (x_r[-1], x_i[-1]), y

    zeros = jnp.zeros((bsz, SSM_GROUPS, SSM_STATE), f32)
    _, ys = lax.scan(chunk_step, (zeros, zeros), uc)
    y = ys.transpose(2, 0, 1, 3, 4).reshape(bsz, seqlen, SSM_DIM)
    y = y + d_skip.astype(f32) * u.astype(f32)
    g = jax.nn.gelu(y).astype(h.dtype)
    val, gate = jnp.split(g @ w_glu, 2, axis=-1)
    return val * jax.nn.sigmoid(gate)

def t5_causal_bucket(rel):
    n = jnp.maximum(-rel, 0)
    nf = jnp.maximum(n, REL_MAX_EXACT).astype(jnp.float32)
    large = REL_MAX_EXACT + (jnp.log(nf / REL_MAX_EXACT)
                             / math.log(REL_MAX_DIST / REL_MAX_EXACT)
                             * (REL_BUCKETS - REL_MAX_EXACT)).astype(jnp.int32)
    large = jnp.minimum(large, REL_BUCKETS - 1)
    return jnp.where(n < REL_MAX_EXACT, n, large)

def shared_kv(x, kv_norm, kv_w, k_norm):
    bsz, seqlen, _ = x.shape
    kv = rms_norm(x, kv_norm) @ kv_w
    nk = 2 * N_HEADS * HEAD_DIM
    k = rms_norm(kv[..., :nk].reshape(bsz, seqlen, N_HEADS, 2, HEAD_DIM), k_norm)
    v = kv[..., nk:].reshape(bsz, seqlen, N_HEADS, 2 * HEAD_DIM)
    return k, v

def diff_attention(h, k, v, rel_bias, w_q, q_norm, lq1, lk1, lq2, lk2, subln, w_o, lam_init):
    f32 = jnp.float32
    bsz, seqlen, _ = h.shape
    q = rms_norm((h @ w_q).reshape(bsz, seqlen, N_HEADS, 2, HEAD_DIM), q_norm)
    lam = (jnp.exp(jnp.sum(lq1.astype(f32) * lk1.astype(f32)))
           - jnp.exp(jnp.sum(lq2.astype(f32) * lk2.astype(f32))) + lam_init)
    scale = HEAD_DIM ** -0.5
    n_blocks = seqlen // Q_BLOCK
    qb = q.reshape(bsz, n_blocks, Q_BLOCK, N_HEADS, 2, HEAD_DIM).transpose(1, 0, 2, 3, 4, 5)
    k_pos = jnp.arange(seqlen)

    def block(args):
        idx, qc = args
        q_pos = idx * Q_BLOCK + jnp.arange(Q_BLOCK)
        rel = k_pos[None, :] - q_pos[:, None]
        bias = rel_bias[t5_causal_bucket(rel)].astype(f32).transpose(2, 0, 1)
        s = jnp.einsum("bqhcd,bkhcd->bhcqk", qc, k).astype(f32) * scale
        s = s + bias[None, :, None]
        s = jnp.where(rel <= 0, s, NEG_INF)
        pm = jax.nn.softmax(s, axis=-1)
        attn = pm[:, :, 0] - lam * pm[:, :, 1]
        return jnp.einsum("bhqk,bkhe->bqhe", attn.astype(v.dtype), v)

    o = lax.map(block, (jnp.arange(n_blocks), qb))
    o = o.transpose(1, 0, 2, 3, 4).reshape(bsz, seqlen, N_HEADS, 2 * HEAD_DIM)
    o = rms_norm(o, subln) * (1.0 - lam_init)
    return o.reshape(bsz, seqlen, N_HEADS * 2 * HEAD_DIM) @ w_o

def conv_ffn(h, w_up, conv_w, conv_b, w_down):
    up = h @ w_up
    seqlen = up.shape[1]
    padded = jnp.pad(up, ((0, 0), (CONV_WIDTH - 1, 0), (0, 0)))
    c = conv_b
    for j in range(CONV_WIDTH):
        c = c + conv_w[j] * padded[:, j:j + seqlen]
    g, val = jnp.split(c, 2, axis=-1)
    return (jax.nn.gelu(g) * val) @ w_down

def first_inputs(seed: int = 0) -> dict:
    key = jax.random.key(seed)
    ks = iter(jax.random.split(key, 40))
    f32 = jnp.float32

    def nrm(shape, scale):
        return jax.random.normal(next(ks), shape, f32) * scale

    def gain(shape):
        return 1.0 + nrm(shape, 0.05)

    na, nb = N_A_LAYERS, N_B_LAYERS
    lam_im = jnp.pi * jnp.arange(SSM_STATE, dtype=f32)
    return {
        "x": nrm((BATCH, SEQ, D_MODEL), 1.0),
        "p": nrm((DEPTH, BATCH, SEQ, PLE_DIM), 1.0),
        "ssm_norm": gain((na, D_MODEL)),
        "ssm_w_in": nrm((na, D_MODEL, SSM_DIM), D_MODEL ** -0.5),
        "ssm_log_dt": jax.random.uniform(next(ks), (na, SSM_GROUPS), f32,
                                         math.log(1e-3), math.log(1e-1)),
        "ssm_lambda_re": -0.5 + nrm((na, SSM_GROUPS, SSM_STATE), 0.01),
        "ssm_lambda_im": lam_im + nrm((na, SSM_GROUPS, SSM_STATE), 0.01),
        "ssm_b_re": nrm((na, SSM_GROUPS, SSM_STATE, SSM_GROUP_DIM), SSM_GROUP_DIM ** -0.5),
        "ssm_b_im": nrm((na, SSM_GROUPS, SSM_STATE, SSM_GROUP_DIM), SSM_GROUP_DIM ** -0.5),
        "ssm_c_re": nrm((na, SSM_GROUPS, SSM_GROUP_DIM, SSM_STATE), SSM_STATE ** -0.5),
        "ssm_c_im": nrm((na, SSM_GROUPS, SSM_GROUP_DIM, SSM_STATE), SSM_STATE ** -0.5),
        "ssm_d": nrm((na, SSM_DIM), 0.5),
        "ssm_w_glu": nrm((na, SSM_DIM, 2 * D_MODEL), SSM_DIM ** -0.5),
        "kv_norm": gain((D_MODEL,)),
        "kv_w": nrm((D_MODEL, 2 * N_HEADS * HEAD_DIM + N_HEADS * 2 * HEAD_DIM), D_MODEL ** -0.5),
        "k_norm": gain((HEAD_DIM,)),
        "attn_norm": gain((nb, D_MODEL)),
        "attn_w_q": nrm((nb, D_MODEL, 2 * N_HEADS * HEAD_DIM), D_MODEL ** -0.5),
        "q_norm": gain((nb, HEAD_DIM)),
        "lambda_q1": nrm((nb, HEAD_DIM), 0.1),
        "lambda_k1": nrm((nb, HEAD_DIM), 0.1),
        "lambda_q2": nrm((nb, HEAD_DIM), 0.1),
        "lambda_k2": nrm((nb, HEAD_DIM), 0.1),
        "subln": gain((nb, 2 * HEAD_DIM)),
        "attn_w_o": nrm((nb, N_HEADS * 2 * HEAD_DIM, D_MODEL), (N_HEADS * 2 * HEAD_DIM) ** -0.5),
        "rel_bias": nrm((REL_BUCKETS, N_HEADS), 0.5),
        "ffn_norm": gain((DEPTH, D_MODEL)),
        "ffn_w_up": nrm((DEPTH, D_MODEL, 2 * D_FF), D_MODEL ** -0.5),
        "ffn_conv_w": nrm((DEPTH, CONV_WIDTH, 2 * D_FF), CONV_WIDTH ** -0.5),
        "ffn_conv_b": nrm((DEPTH, 2 * D_FF), 0.02),
        "ffn_w_down": nrm((DEPTH, D_FF, D_MODEL), D_FF ** -0.5),
        "ple_norm": gain((DEPTH, D_MODEL)),
        "ple_w_gate": nrm((DEPTH, D_MODEL, D_MODEL), D_MODEL ** -0.5),
        "ple_w_proj": nrm((DEPTH, PLE_DIM, D_MODEL), PLE_DIM ** -0.5),
    }

def first_block(x, p, ssm_norm, ssm_w_in, ssm_log_dt, ssm_lambda_re, ssm_lambda_im,
              ssm_b_re, ssm_b_im, ssm_c_re, ssm_c_im, ssm_d, ssm_w_glu,
              kv_norm, kv_w, k_norm, attn_norm, attn_w_q, q_norm,
              lambda_q1, lambda_k1, lambda_q2, lambda_k2, subln, attn_w_o, rel_bias,
              ffn_norm, ffn_w_up, ffn_conv_w, ffn_conv_b, ffn_w_down,
              ple_norm, ple_w_gate, ple_w_proj):
    k = v = None
    for i in range(DEPTH):
        if i < N_A_LAYERS:
            h = rms_norm(x, ssm_norm[i])
            x = x + s5_mixer(h, ssm_w_in[i], ssm_log_dt[i], ssm_lambda_re[i], ssm_lambda_im[i],
                             ssm_b_re[i], ssm_b_im[i], ssm_c_re[i], ssm_c_im[i],
                             ssm_d[i], ssm_w_glu[i])
        else:
            if i == N_A_LAYERS:
                k, v = shared_kv(x, kv_norm, kv_w, k_norm)
            j = i - N_A_LAYERS
            lam_init = 0.8 - 0.6 * math.exp(-0.3 * i)
            h = rms_norm(x, attn_norm[j])
            x = x + diff_attention(h, k, v, rel_bias, attn_w_q[j], q_norm[j],
                                   lambda_q1[j], lambda_k1[j], lambda_q2[j], lambda_k2[j],
                                   subln[j], attn_w_o[j], lam_init)
        h = rms_norm(x, ffn_norm[i])
        x = x + conv_ffn(h, ffn_w_up[i], ffn_conv_w[i], ffn_conv_b[i], ffn_w_down[i])
        gate = jax.nn.sigmoid(rms_norm(x, ple_norm[i]) @ ple_w_gate[i])
        x = x + gate * (p[i] @ ple_w_proj[i])
    return x


A_HEADS = 8
A_KV_HEADS = 2
A_WIDTH = A_HEADS * HEAD_DIM
A_KV_WIDTH = A_KV_HEADS * HEAD_DIM
IDX_HEADS = 4
IDX_DIM = 64
IDX_SCALE = (IDX_HEADS * IDX_DIM) ** -0.5
TOPK_MAX = 256
POOL_WINDOWS = (2, 4, 8, 16)
POOL_GROUP = 128
POOL_WIDTH = POOL_GROUP * len(POOL_WINDOWS)
EVEN_MIX_WIDTH = A_WIDTH + POOL_WIDTH
EVEN_IN_COLS = A_WIDTH + 2 * A_KV_WIDTH + IDX_HEADS * IDX_DIM + IDX_DIM + IDX_HEADS + POOL_WIDTH
C_HEADS = 16
C_WIDTH = C_HEADS * HEAD_DIM
D_FF_2 = -(-8 * D_MODEL // (3 * 256)) * 256
N_EVEN = (DEPTH + 1) // 2
N_ODD = DEPTH // 2


def rms_norm_2(x, g):
    x32 = x.astype(jnp.float32)
    y = x32 * lax.rsqrt(jnp.mean(x32 * x32, axis=-1, keepdims=True) + EPS)
    return (y * g.astype(jnp.float32)).astype(x.dtype)

def to_blocks(a):
    b, t = a.shape[:2]
    a = a.reshape((b, t // Q_BLOCK, Q_BLOCK) + a.shape[2:])
    return jnp.moveaxis(a, 1, 0)

def from_blocks(a):
    a = jnp.moveaxis(a, 0, 1)
    return a.reshape((a.shape[0], a.shape[1] * a.shape[2]) + a.shape[3:])

def dsa_attention(q, k, v, q_idx, k_idx, w_idx):
    b, t = q.shape[:2]
    n_sel = min(TOPK_MAX, t // 4)
    rep = A_HEADS // A_KV_HEADS
    key_pos = jnp.arange(t)
    gather = jax.vmap(lambda kv, ids: kv[ids])

    def block(args):
        qb, qib, wb, start = args
        q_pos = start + jnp.arange(Q_BLOCK)
        causal = key_pos[None, :] <= q_pos[:, None]
        rel = jax.nn.relu(jnp.einsum('bthd,bsd->bths', qib, k_idx).astype(jnp.float32))
        score = jnp.einsum('bths,bth->bts', rel, wb.astype(jnp.float32)) * IDX_SCALE
        score = jnp.where(causal[None], score, -jnp.inf)
        _, sel = lax.top_k(score, n_sel)
        k_sel = gather(k, sel)
        v_sel = gather(v, sel)
        valid = sel <= q_pos[None, :, None]
        qg = qb.reshape(b, Q_BLOCK, A_KV_HEADS, rep, HEAD_DIM)
        logits = jnp.einsum('btgrd,btkgd->btgrk', qg, k_sel).astype(jnp.float32) * (HEAD_DIM ** -0.5)
        logits = jnp.where(valid[:, :, None, None, :], logits, -jnp.inf)
        p = jax.nn.softmax(logits, axis=-1).astype(v.dtype)
        o = jnp.einsum('btgrk,btkgd->btgrd', p, v_sel)
        return o.reshape(b, Q_BLOCK, A_WIDTH)

    starts = jnp.arange(t // Q_BLOCK) * Q_BLOCK
    out = lax.map(block, (to_blocks(q), to_blocks(q_idx), to_blocks(w_idx), starts))
    return from_blocks(out)

def multiscale_pool(u, pool_w, pool_scale):
    b, t, _ = u.shape
    groups = u.astype(jnp.float32).reshape(b, t, len(POOL_WINDOWS), POOL_GROUP)
    c0 = jnp.pad(jnp.cumsum(groups, axis=1), ((0, 0), (1, 0), (0, 0), (0, 0)))
    pos = jnp.arange(1, t + 1, dtype=jnp.float32)
    outs = []
    for g, w in enumerate(POOL_WINDOWS):
        cg = c0[:, :, g]
        hi = cg[:, 1:]
        lo = jnp.pad(cg[:, :t + 1 - w], ((0, 0), (w - 1, 0), (0, 0)))
        count = jnp.minimum(pos, float(w))[None, :, None]
        outs.append((hi - lo) / count - groups[:, :, g])
    mixed = jnp.stack(outs, axis=2)
    y = jnp.einsum('btgc,gcd->btgd', mixed, pool_w.astype(jnp.float32))
    return (y.reshape(b, t, POOL_WIDTH) * pool_scale.astype(jnp.float32)).astype(u.dtype)

def stick_breaking_attention(q, k, v):
    b, t = q.shape[:2]
    key_pos = jnp.arange(t)

    def block(args):
        qb, start = args
        q_pos = start + jnp.arange(Q_BLOCK)
        strict = key_pos[None, :] < q_pos[:, None]
        z = jnp.einsum('bthd,bshd->bhts', qb, k).astype(jnp.float32) * (HEAD_DIM ** -0.5)
        brk = jnp.where(strict, jax.nn.softplus(z), 0.0)
        later = jnp.pad(brk[..., 1:], ((0, 0), (0, 0), (0, 0), (0, 1)))
        remain = lax.cumsum(later, axis=3, reverse=True)
        log_a = jax.nn.log_sigmoid(z) - remain
        a = jnp.where(strict, jnp.exp(log_a), 0.0).astype(v.dtype)
        o = jnp.einsum('bhts,bshd->bthd', a, v)
        return o.reshape(b, Q_BLOCK, C_WIDTH)

    starts = jnp.arange(t // Q_BLOCK) * Q_BLOCK
    out = lax.map(block, (to_blocks(q), starts))
    return from_blocks(out)

def even_mixer(h, w_in, w_out, q_g, k_g, pool_w, pool_scale):
    b, t, _ = h.shape
    proj = h @ w_in
    sizes = [A_WIDTH, A_KV_WIDTH, A_KV_WIDTH, IDX_HEADS * IDX_DIM, IDX_DIM, IDX_HEADS]
    offsets = np.cumsum(sizes).tolist()
    q, k, v, qi, ki, wi, u = jnp.split(proj, offsets, axis=-1)
    q = rms_norm_2(q.reshape(b, t, A_HEADS, HEAD_DIM), q_g)
    k = rms_norm_2(k.reshape(b, t, A_KV_HEADS, HEAD_DIM), k_g)
    v = v.reshape(b, t, A_KV_HEADS, HEAD_DIM)
    attn = dsa_attention(q, k, v, qi.reshape(b, t, IDX_HEADS, IDX_DIM), ki, wi)
    pooled = multiscale_pool(u, pool_w, pool_scale)
    return jnp.concatenate([attn, pooled], axis=-1) @ w_out

def odd_mixer(h, w_qkv, w_out):
    b, t, _ = h.shape
    q, k, v = jnp.split((h @ w_qkv).reshape(b, t, 3, C_HEADS, HEAD_DIM), 3, axis=2)
    o = stick_breaking_attention(q[:, :, 0], k[:, :, 0], v[:, :, 0])
    return o @ w_out

def swiglu(h, w1, w3, w2):
    return (jax.nn.silu(h @ w1) * (h @ w3)) @ w2

def second_inputs(seed: int = 0) -> dict:
    key = jax.random.key(seed)
    ks = jax.random.split(key, 16)
    f32 = jnp.float32

    def dense(k, shape):
        return jax.random.normal(k, shape, f32) * (shape[-2] ** -0.5)

    def gain(k, shape, s):
        return 1.0 + s * jax.random.normal(k, shape, f32)

    return {
        'x': jax.random.normal(ks[0], (BATCH, SEQ, D_MODEL), f32),
        'norm_mix_g': gain(ks[1], (DEPTH, D_MODEL), 0.05),
        'norm_ffn_g': gain(ks[2], (DEPTH, D_MODEL), 0.05),
        'ev_w_in': dense(ks[3], (N_EVEN, D_MODEL, EVEN_IN_COLS)),
        'ev_w_out': dense(ks[4], (N_EVEN, EVEN_MIX_WIDTH, D_MODEL)),
        'ev_q_norm_g': gain(ks[5], (N_EVEN, HEAD_DIM), 0.05),
        'ev_k_norm_g': gain(ks[6], (N_EVEN, HEAD_DIM), 0.05),
        'ev_pool_w': dense(ks[7], (N_EVEN, len(POOL_WINDOWS), POOL_GROUP, POOL_GROUP)),
        'ev_pool_scale': gain(ks[8], (N_EVEN, POOL_WIDTH), 0.1),
        'od_w_qkv': dense(ks[9], (N_ODD, D_MODEL, 3 * C_WIDTH)),
        'od_w_out': dense(ks[10], (N_ODD, C_WIDTH, D_MODEL)),
        'ffn_w1': dense(ks[11], (DEPTH, D_MODEL, D_FF_2)),
        'ffn_w3': dense(ks[12], (DEPTH, D_MODEL, D_FF_2)),
        'ffn_w2': dense(ks[13], (DEPTH, D_FF_2, D_MODEL)),
    }

def second_block(x, norm_mix_g, norm_ffn_g, ev_w_in, ev_w_out, ev_q_norm_g, ev_k_norm_g,
              ev_pool_w, ev_pool_scale, od_w_qkv, od_w_out, ffn_w1, ffn_w3, ffn_w2):
    for layer in range(DEPTH):
        i = layer // 2
        h = rms_norm_2(x, norm_mix_g[layer])
        if layer % 2 == 0:
            x = x + even_mixer(h, ev_w_in[i], ev_w_out[i], ev_q_norm_g[i], ev_k_norm_g[i],
                               ev_pool_w[i], ev_pool_scale[i])
        else:
            x = x + odd_mixer(h, od_w_qkv[i], od_w_out[i])
        h = rms_norm_2(x, norm_ffn_g[layer])
        x = x + swiglu(h, ffn_w1[layer], ffn_w3[layer], ffn_w2[layer])
    return x


def setup_inputs(seed=0):
    out = dict(first_inputs(seed))
    for name, value in second_inputs(seed + 1).items():
        if name != "x":
            out[name + "_2"] = value
    return out


def reference(
    x, p, ssm_norm, ssm_w_in, ssm_log_dt, ssm_lambda_re, ssm_lambda_im, ssm_b_re, ssm_b_im,
    ssm_c_re, ssm_c_im, ssm_d, ssm_w_glu, kv_norm, kv_w, k_norm, attn_norm, attn_w_q, q_norm,
    lambda_q1, lambda_k1, lambda_q2, lambda_k2, subln, attn_w_o, rel_bias, ffn_norm, ffn_w_up,
    ffn_conv_w, ffn_conv_b, ffn_w_down, ple_norm, ple_w_gate, ple_w_proj, norm_mix_g_2,
    norm_ffn_g_2, ev_w_in_2, ev_w_out_2, ev_q_norm_g_2, ev_k_norm_g_2, ev_pool_w_2,
    ev_pool_scale_2, od_w_qkv_2, od_w_out_2, ffn_w1_2, ffn_w3_2, ffn_w2_2,
):
    x = first_block(
        x, p, ssm_norm, ssm_w_in, ssm_log_dt, ssm_lambda_re, ssm_lambda_im, ssm_b_re, ssm_b_im,
        ssm_c_re, ssm_c_im, ssm_d, ssm_w_glu, kv_norm, kv_w, k_norm, attn_norm, attn_w_q,
        q_norm, lambda_q1, lambda_k1, lambda_q2, lambda_k2, subln, attn_w_o, rel_bias, ffn_norm,
        ffn_w_up, ffn_conv_w, ffn_conv_b, ffn_w_down, ple_norm, ple_w_gate, ple_w_proj,
    )
    return second_block(
        x, norm_mix_g_2, norm_ffn_g_2, ev_w_in_2, ev_w_out_2, ev_q_norm_g_2, ev_k_norm_g_2,
        ev_pool_w_2, ev_pool_scale_2, od_w_qkv_2, od_w_out_2, ffn_w1_2, ffn_w3_2, ffn_w2_2,
    )


_drawn_inputs = setup_inputs


def setup_inputs(seed=0):
    import zlib

    import numpy as np

    out = dict(_drawn_inputs(seed))
    spreads = {}
    factors = {'ssm_norm': 3.835,
     'ssm_lambda_re': 8.0,
     'lambda_q1': 3.418,
     'lambda_k1': 4.62,
     'lambda_q2': 2.94,
     'lambda_k2': 4.326,
     'ple_norm': 3.691,
     'ev_q_norm_g_2': 8.0,
     'ev_k_norm_g_2': 8.0}
    for name, (base, spread) in spreads.items():
        noise = np.random.default_rng([zlib.crc32(name.encode()), seed]).standard_normal(out[name].shape)
        drawn = base * np.exp(spread * noise) if base else spread * noise
        out[name] = __import__('jax').numpy.asarray(drawn.astype(out[name].dtype))
    for name, factor in factors.items():
        out[name] = (out[name] * factor).astype(out[name].dtype)
    return out
```

```python
import math
from contextlib import ExitStack

import numpy as np

import concourse.bass as bass
from concourse import mybir

P = 128
D = 1024
T = 256
KT = D // P
TT = T // P
FF = 2816
STEPS = FF // (2 * P)
GROUPS, GDIM, STATE = 64, 16, 64
PAIRS = GROUPS // 2
HEADS, HD = 8, 64
SEL = 64
STICKS = 16
EPS = 1e-6
NEG = -1e30
TAKEN = -3e38
ROUND = 1.5 * 2.0 ** 23
LAM_INIT = 0.8 - 0.6 * math.exp(-0.3)
TWO_PI = 6.2831850

RING = 6
SPLIT = 3
STAGES = [("w_in", 4), ("glu", 8), ("ffn0", 3 * STEPS), ("ple0", 5), ("kvq", 12), ("wo", 4),
          ("ffn1", 3 * STEPS), ("ple1", 5), ("evin", 7), ("evout", 4), ("ffn2", 3 * STEPS),
          ("qkv", 12), ("out", 4), ("ffn3", 3 * STEPS)]
START, BANK, N_SLOTS, _u = {}, {}, 0, 0
for _name, _n in STAGES:
    START[_name], BANK[_name] = N_SLOTS, _u
    N_SLOTS += _n
    _u += {"ffn": 2 * STEPS, "ple": 4}.get(_name[:3], _n)

UNITS = ["ssm", "s5", "ffn0", "ple0", "kv", "q", "diff", "ffn1", "ple1", "even", "mixed", "ffn2",
         "odd", "stick", "ffn3"]
UNIT = {n: i for i, n in enumerate(UNITS)}
SET = dict(ssm=2, s5=1, ffn0=0, ple0=0, kv=1, q=0, diff=1, ffn1=0, ple1=0, even=1, mixed=1,
           ffn2=0, odd=0, stick=1, ffn3=0)
GAINS = ["ssm", "ffn0", "ple0", "kv", "q", "ffn1", "ple1", "even", "ffn2", "odd", "ffn3"]
GAIN = {n: i for i, n in enumerate(GAINS)}

COLS, _c = {}, 0
for _name, _n in [("gain", len(GAINS) * KT), ("conv", 2 * 22 * 8), ("dskip", KT), ("qk", 2),
                  ("subln", 1), ("evqk", 2), ("lam", 4), ("pscale", 4), ("ones", P), ("half", 2),
                  ("ident", P)]:
    COLS[_name] = (_c, _c + _n)
    _c += _n
N_COLS = _c
MIX = 15264


class Count:

    def __init__(self, sem):
        self.sem, self.n, self.i, self.per = sem, 0, None, 0

    def value(self):
        return self.n if self.i is None else self.i * self.per + self.n

    def enter(self, i, per):
        self.i, self.per, self.base = i, per, self.n

    def leave(self, turns):
        assert self.n - self.base == self.per, (self.n - self.base, self.per)
        self.n, self.i = self.base + self.per * turns, None


class Counts:

    def __init__(self, eng, sems):
        self.eng, self.sems, self.c = eng, sems, {}

    def of(self, name):
        if name not in self.c:
            self.c[name] = Count(self.sems(name))
        return self.c[name]

    def up(self, ins, name):
        c = self.of(name)
        c.n += 1
        ins.then_inc(c.sem, 1)

    def up_and_wait(self, ins, name):
        self.up(ins, name)
        self.eng.wait_ge(self.of(name).sem, self.of(name).value())

    def tell(self, name):
        c = self.of(name)
        c.n += 1
        self.eng.sem_inc(c.sem, 1)

    def wait(self, name, k=1):
        c = self.of(name)
        c.n += k
        self.eng.wait_ge(c.sem, c.value())

    def enter(self, i, **per):
        for name, k in per.items():
            self.of(name).enter(i, k)
        self.looped = list(per)

    def leave(self, turns):
        for name in self.looped:
            self.of(name).leave(turns)


def program(nc, a, out):
    f32, f32r = mybir.dt.float32, mybir.dt.float32r
    ALU, ACT, AX = mybir.AluOpType, mybir.ActivationFunctionType, mybir.AxisListType
    ctx = ExitStack()
    with ctx:
        def sb(name, shape, dt=f32):
            return ctx.enter_context(nc.sbuf_tensor(name, shape, dt))

        ring = sb("ring", [P, RING, 2048])
        w_hi = sb("w_hi", [P, SPLIT, 2048], f32r)
        w_lo = sb("w_lo", [P, SPLIT, 2048], f32r)
        x = sb("x", [P, KT, T])
        sq = sb("sq", [P, KT, T])
        par = sb("par", [P, N_COLS])
        rstd = sb("rstd", [P, T])
        tok = sb("tok", [P, 4])
        little = sb("little", [P, 8])
        mix = sb("mix", [P, MIX])
        with nc.sbuf_tensor("opnd_first", [P, 2, KT, T], f32r) as opnd_first:
            pass
        with nc.sbuf_tensor("s5_area", [P, 2, 2 * KT, T], f32) as s5_area:
            pass
        opnd = [sb(f"opnd{i}", [P, 2, KT, T], f32r) for i in range(2)] + [opnd_first]
        acc = ctx.enter_context(nc.psum_tensor("acc", [P, 4, 512], f32))
        up = [ctx.enter_context(nc.psum_tensor(f"up{i}", [P, 2, T], f32)) for i in range(2)]
        aux = [ctx.enter_context(nc.psum_tensor(f"aux{i}", [P, 512], f32)) for i in range(2)]

        eps, neg_lam, sub_g, lam_e = little[:, 0:1], little[:, 1:2], little[:, 2:3], little[:, 3:5]

        def pcol(name, lo=0, n=None):
            s, e = COLS[name]
            return par[:, s + lo:(s + lo + n) if n else e]

        ident, ones = pcol("ident"), pcol("ones")

        def gain(name, m):
            return pcol("gain", GAIN[name] * KT + m, 1)

        sems = {}

        def sem(name):
            if name not in sems:
                sems[name] = ctx.enter_context(nc.semaphore(name))
            return sems[name]

        ring_full = [sem(f"ring_full{i}") for i in range(RING)]
        DMAS = ["par", "x", "s5_par", "s5_mat", "s5_c", "s5_t", "pe0", "pe1", "bias_oh", "bias_w",
                "bias_r", "causal", "stickmask", "outd"]
        dma = {n: sem(f"dma_{n}") for n in DMAS}

        def carve(*sizes):
            at, views = 0, []
            for shape in sizes:
                n = int(np.prod(shape))
                v = mix[:, at:at + n]
                if len(shape) == 2:
                    v = v.rearrange("p (a b) -> p a b", a=shape[0])
                if len(shape) == 3:
                    v = v.rearrange("p (a b c) -> p a b c", a=shape[0], b=shape[1])
                views.append(v)
                at += n
            assert at <= MIX, at
            return views

        (s_cs, s_sn, s_p, s_c, s_b, s_y, s_tmat, s_prep, s_mag, s_phi, s_e, s_t, s_init) = carve(
            (PAIRS, P), (PAIRS, P), (2, 2, 2 * T), (2, PAIRS, 32), (2, KT, P), (2, T), (P,), (3, PAIRS), (PAIRS,),
            (PAIRS,), (3, PAIRS), (2, 2, 2), (2, 2))
        s_p = s_p.rearrange("p a e (k t) -> p a e k t", k=2)
        s_work = s_y.rearrange("p a (b c) -> p (a b) c", c=PAIRS)
        s_m = s5_area[:, 0].rearrange("p k t -> p (k t)").rearrange(
            "p (m e k t) -> p m e k t", m=4, e=2, k=2)
        s_raw = s5_area[:, 1].rearrange("p k t -> p (k t)").rearrange(
            "p (a b c) -> p a b c", a=4, b=PAIRS)
        (f_u, f_c, f_gg, f_h, f_pe) = carve((4, 258), (4, T), (2, T), (2, T), (4, T))
        (d_k, d_q, d_v, d_bias, d_tmp, d_sq, d_l, d_a, d_at, d_st) = carve(
            (KT, T), (KT, T), (TT, D), (HEADS, T), (3, 2 * T), (2, 2 * T), (2, 2 * T), (2, T),
            (2, 2 * T), (64,))
        d_oh = mix[0:33, 0:384 + HEADS]
        (e_v, e_k, e_q, e_pl, e_tmp, e_sq, e_l, e_a, e_at, e_mask, e_causal, e_w, e_rel, e_st, e_m8,
         e_out, e_pa, e_cnt, e_pw) = carve(
            (TT, P), (T,), (4, T), (7, T), (3, 2 * T), (2, 2 * T), (2, 2 * T), (2, 2 * T), (4, 2 * T),
            (2, T), (2, T), (TT, 4), (T,), (64,), (8,), (2, T), (4, 16 + T), (4, T), (4, P))
        e_pb = mix[:, 3328:3328 + 4 * (16 + T)].rearrange("p (a b) -> p a b", a=4)
        (k_k, k_q, k_v, k_mask, k_tri, k_z, k_t, k_b, k_a, k_out) = carve(
            (KT, T), (KT, T), (TT, D), (384,), (P,), (3, 384), (2, 384), (2, 384), (2, 384), (2, T))

        def by_chunk(v):
            return v.rearrange("p e k (c t) -> p e (k c) t", c=2)

        def chunks(v):
            return v.rearrange("p e (c t) -> p e c t", c=2)

        def local(table, n, k):
            return table[:, 2 * n:2 * n + 2].unsqueeze(2).broadcast_to([P, 2, k, P])

        def hi(name):
            return opnd[SET[name]][:, 0]

        def lo(name):
            return opnd[SET[name]][:, 1]

        block = ctx.enter_context(nc.Block())

        @block.sync
        def _(sp):
            def load(r, slot):
                sp.dma_start(ring[:, r], a["stream"][slot].rearrange("a p n -> (a p) n")).then_inc(ring_full[r], 16)

            sp.dma_start(par[:], a["par"]).then_inc(dma["par"], 16)
            sp.dma_start(x[:], a["x"]).then_inc(dma["x"], 16)
            for s in range(RING):
                load(s, slice(s, s + 1))
            turns = N_SLOTS // RING - 1
            with sp.Fori(0, turns) as i:
                for r in range(RING):
                    sp.wait_ge(sem("w_ready"), i * RING + (r + 1))
                    load(r, bass.ds(i * RING + (RING + r), 1))
            for s in range(RING * (turns + 1), N_SLOTS):
                sp.wait_ge(sem("w_ready"), s - RING + 1)
                load(s % RING, slice(s, s + 1))
            c = Counts(sp, sem)
            for m in range(KT):
                c.wait("x_ready", 8 * 9 + 1 if m == 0 else 1)
                sp.dma_start(out[m], x[:, m]).then_inc(dma["outd"], 16)
            sp.wait_ge(dma["outd"], 16 * KT)

        @block.gpsimd
        def _(pool):
            c = Counts(pool, sem)

            def low_part(s, k=0):
                c.wait("w_hi_ready")
                r, b = (s + k) % RING, (s + k) % SPLIT
                c.up(nc.gpsimd.tensor_tensor(w_lo[:, b], ring[:, r], w_hi[:, b].bitcast(f32), ALU.subtract),
                     "w_ready")

            for s in range(START["glu"]):
                low_part(s)

            def sums(n):
                m, r = s_m[:, n % 3], s_m[:, 3]
                c.wait("s5_prod", 2)
                c.up(nc.gpsimd.tensor_tensor(m[:, :, 1], r[:, :, 0], m[:, :, 1], ALU.subtract), "s5_sum")
                c.up(nc.gpsimd.tensor_tensor(m[:, :, 0], m[:, :, 0], r[:, :, 1], ALU.add), "s5_sum")

            def products(n):
                z = s_m[:, n % 3]
                c.wait("s5_scan")
                if n:
                    c.wait("s5_y")
                c.up(nc.gpsimd.tensor_tensor(by_chunk(s_p[:, 0]), local(s_cs, n, 4), by_chunk(z), ALU.mult),
                     "s5_out_pool")
                c.up(nc.gpsimd.tensor_tensor(chunks(s_p[:, 1, :, 1]), local(s_sn, n, 2), chunks(z[:, :, 1]), ALU.mult),
                     "s5_out_pool")

            for n in range(2 * KT + 1):
                if n < 2 * KT:
                    sums(n)
                if n in (5, 8, 11):
                    low_part(START["glu"] + n // 3 - 1)
                if n:
                    products(n - 1)

            first = START["glu"] + SPLIT
            turns = (N_SLOTS - first) // RING
            with pool.Fori(0, turns) as i:
                c.enter(i, w_hi_ready=RING, w_ready=RING)
                for k in range(RING):
                    low_part(first, k)
                c.leave(turns)
            for s in range(first + turns * RING, N_SLOTS):
                low_part(s)

        @block.scalar
        def _(act):
            c = Counts(act, sem)
            A = nc.scalar.activation
            ahead = [0]

            def high_part(s, i=None):
                dyn = 0 if i is None else i
                act.wait_ge(ring_full[s % RING], dyn * 16 + 16 * (s // RING + 1))
                if s >= SPLIT:
                    act.wait_ge(sem("mm_done"), dyn * RING + (s - SPLIT + 1))
                c.up(A(w_hi[:, s % SPLIT], ring[:, s % RING], ACT.Copy), "w_hi_ready")

            def high_parts_to(s):
                while ahead[0] <= min(s, N_SLOTS - 1):
                    high_part(ahead[0])
                    ahead[0] += 1

            def new_operand(name, squares=True):
                for m in range(KT):
                    if squares:
                        c.up(A(sq[:, m], x[:, m], ACT.Square), "sq_ready")
                    c.up(A(hi(name)[:, m], x[:, m], ACT.Copy, scale=gain(name, m)), "hi_ready")

            def from_psum(name, m, src, buf, scale=1.0):
                b = buf[:, m % 2]
                if m >= 2:
                    act.wait_ge(sem("lo_ready"), KT * UNIT[name] + m - 1)
                c.up_and_wait(A(b, src, ACT.Copy, scale=scale), "act_step")
                c.up(A(hi(name)[:, m], b, ACT.Copy), "hi_ready")

            def rms():
                c.wait("ssq")
                c.up(A(tok[:, 0:2], aux[0][:, 0:2], ACT.Sqrt, scale=1.0 / D, bias=eps), "rms")
                c.wait("rstd_bc")
                c.up(A(rstd[:], aux[1][:, 0:T], ACT.Copy), "rstd")

            act.dma_start(s_prep, a["s5_par"]).then_inc(dma["s5_par"], 16)
            act.dma_start(s_tmat, a["tmat"]).then_inc(dma["s5_t"], 16)
            act.wait_ge(dma["s5_par"], 16)
            w = s_work
            c.up(A(w[:, 0], s_prep[:, 2], ACT.Exp), "dt")
            c.wait("s5_mu")
            c.up(A(s_mag, w[:, 1], ACT.Exp), "mag")
            act.wait_ge(dma["par"], 16)
            act.wait_ge(dma["x"], 16)
            new_operand("ssm")
            high_parts_to(0)
            act.dma_start(s_raw[:, 0:2, :, :], a["s5_c"]).then_inc(dma["s5_c"], 16)
            act.dma_start(s_b, a["s5_b"]).then_inc(dma["s5_mat"], 16)
            high_parts_to(1)
            c.wait("lam_sum")
            c.up(A(lam_e, aux[1][:, 0:2], ACT.Exp), "lam_exp")
            c.wait("s5_turn")
            c.up(A(w[:, 4], s_phi, ACT.Sin, scale=TWO_PI), "s5_sc")
            c.up(A(w[:, 5], s_phi, ACT.Sin, scale=TWO_PI / 2), "s5_sc")
            c.up(A(s_e[:, 2], w[:, 12], ACT.Sin, scale=TWO_PI), "s5_sc")
            c.up(A(w[:, 13], w[:, 12], ACT.Sin, scale=TWO_PI / 2), "s5_sc")
            high_parts_to(2)

            def s5_tables(g):
                q = slice(8 * g, 8 * g + 8)
                c.wait("s5_frac")
                c.up_and_wait(A(s_cs[:, q], s_sn[:, q], ACT.Sin, scale=TWO_PI / 2), "s5_sin")
                c.up(A(s_sn[:, q], s_sn[:, q], ACT.Sin, scale=TWO_PI), "s5_sin")
                c.up(A(s_cs[:, q], s_cs[:, q], ACT.Square), "s5_half")

            s5_tables(0)
            s5_tables(1)
            c.wait("eps")
            rms()
            high_parts_to(3)
            s5_tables(2)
            s5_tables(3)

            high_parts_to(START["glu"] + SPLIT - 1)
            for m in range(KT):
                c.wait("s5_ysum")
                c.up_and_wait(A(s_y[:, 1], s_y[:, 0], ACT.Gelu_apprx_tanh), "act_step")
                c.up(A(hi("s5")[:, m], s_y[:, 1], ACT.Copy), "hi_ready")

            def operand_tile(name, m):
                c.wait("x_ready")
                c.up(A(sq[:, m], x[:, m], ACT.Square), "sq_ready")
                c.up(A(hi(name)[:, m], x[:, m], ACT.Copy, scale=gain(name, m)), "hi_ready")

            for m in range(KT):
                s = START["glu"] + m
                high_parts_to(s + 2)
                act.wait_ge(sem("mm_done"), s + 1)
                c.up(A(f_gg[:, 0], up[m % 2][:, 1], ACT.Sigmoid), "gated")
                operand_tile("ffn0", m)

            def ffn(l, end):
                S = START[f"ffn{l}"]

                def gate():
                    c.wait("g_ready")
                    if l < 2:
                        c.up(A(f_gg[:, 0], f_c[:, 0], ACT.Gelu_apprx_tanh), "gated")
                    else:
                        c.up(A(f_gg[:, 0], f_u[:, 0, 2:258], ACT.Silu), "gated")

                high_parts_to(S + 2)
                rms()
                for s in range(S, S + 8):
                    high_parts_to(s + 2)
                    if s - S not in (4, 7):
                        gate()
                assert ahead[0] == S + 10
                turns = 4 if end else 3
                with act.Fori(0, turns) as i:
                    c.enter(i, g_ready=4, gated=4, w_hi_ready=6)
                    for k in range(6):
                        high_part(S + 10 + k, i)
                        if k % 3 != 2:
                            gate()
                    c.leave(turns)
                ahead[0] = S + 10 + 6 * turns
                for k in range(6 * turns, 24):
                    high_parts_to(S + 10 + k)
                    if k % 3 != 2:
                        gate()
                if end:
                    for m in range(KT):
                        operand_tile(end, m)

            def pe_operand(l):
                act.wait_ge(dma[f"pe{l}"], 16)
                for k in range(2):
                    c.up(A(opnd[1][:, 0, 6 + k], f_pe[:, k], ACT.Copy), "pe_hi")

            def ple(l, ends):
                S = START[f"ple{l}"]
                high_parts_to(S + 2)
                rms()
                for g in range(4):
                    high_parts_to(S + g + 4)
                    c.wait("ple_u")
                    c.up(A(f_c[:, 2 * (g % 2):2 * (g % 2) + 2], f_u[:, 2 * (g % 2):2 * (g % 2) + 2, 2:258],
                           ACT.Sigmoid), "gated")
                    for m in (2 * g, 2 * g + 1):
                        operand_tile(ends[0], m)
                for name in ends[1:]:
                    new_operand(name, squares=False)

            def residual(name, S):
                for m in range(KT):
                    high_parts_to(S + m // 2 + 2)
                    operand_tile(name, m)

            def norm_stats(n, tmp, sqb, st, src, deps):
                if n < deps:
                    c.wait("hn_raw")
                    c.up(A(sqb[:, n % 2], tmp[:, n % 3], ACT.Square), "hn_sq")
                if 1 <= n <= deps:
                    c.wait("hn_ssq")
                    o = 16 * ((n - 1) % 2)
                    c.up(A(st[:, o:o + 8], aux[0][:, o:o + 8], ACT.Sqrt, scale=1.0 / HD, bias=eps), "hn_rms")

            def softmax_exp(n, lbuf, st):
                nk = P * (n % 2 + 1)
                c.wait("neg_max")
                b = n % 2
                for e in range(2):
                    L = lbuf[:, b].rearrange("p (c k) -> p c k", c=2)[:, e, 0:nk]
                    c.up(A(L, L, ACT.Exp, bias=st[:, 40 + 2 * b + e:41 + 2 * b + e],
                           accum_out=st[:, 44 + 2 * b + e:45 + 2 * b + e]), "exps")

            def attn_copy(n, at, per):
                nk = n % 2 + 1
                c.wait("at_ps")
                src = up[n % 2][:].rearrange("p a t -> p (a t)").rearrange("p (j k q) -> p j k q", j=per, k=4 // per)
                for j in range(per):
                    t = (n // 2) % 2
                    dst = at[:, per * t + j].rearrange("p (k q) -> p k q", k=2)[:, 0:nk, (n % 2) * P:(n % 2) * P + P]
                    c.up(A(dst, src[:, j, 0:nk], ACT.Copy), "at_sb")

            act.dma_start(f_pe[:, 0:2], a["p0"]).then_inc(dma["pe0"], 16)
            pe_operand(0)
            ffn(0, "ple0")
            ple(0, ["kv", "q"])

            S = START["kvq"]
            high_parts_to(S + 2)
            c.wait("mix_free")
            act.dma_start(d_oh, a["bias_oh"]).then_inc(dma["bias_oh"], 16)
            c.wait("bias_sb")
            act.dma_start(a["scratch"], d_sq[0:HEADS, 0, 0:384].unsqueeze(1).broadcast_to([HEADS, P, 384])).then_inc(dma["bias_w"], 16)
            rms()
            act.wait_ge(dma["bias_w"], 16)
            act.dma_start(d_bias, a["scratch_toeplitz"]).then_inc(dma["bias_r"], 16)
            for n in range(8 + 1):
                high_parts_to(S + 4 + n + 2)
                norm_stats(n, d_tmp, d_sq, d_st, None, 8)
            high_parts_to(S + 14)
            for n in range(2 * HEADS + 2):
                if n < 2 * HEADS:
                    softmax_exp(n, d_l, d_st)
                if n >= 2:
                    attn_copy(n - 2, d_at, 1)
                if n >= 4 and n % 2 == 0:
                    h = n // 2 - 2
                    c.wait("pv")
                    c.up(A(sq[:, h], aux[h % 2][:, 0:T], ACT.Copy), "act_step")
                    c.up(A(d_q[:, h], aux[h % 2][:, 0:T], ACT.Square), "o_sq")
            for h in (HEADS - 1,):
                c.wait("pv")
                c.up(A(sq[:, h], aux[h % 2][:, 0:T], ACT.Copy), "act_step")
                c.up(A(d_q[:, h], aux[h % 2][:, 0:T], ACT.Square), "o_sq")
            c.wait("o_ssq")
            c.up(A(d_st[:, 0:16], acc[:, 0, 0:16], ACT.Sqrt, scale=1.0 / P, bias=eps), "o_rms")
            for m in range(KT):
                c.wait("o_norm")
                c.up(A(hi("diff")[:, m], sq[:, m], ACT.Copy, scale=sub_g), "hi_ready")
            residual("ffn1", START["wo"])

            act.dma_start(f_pe[:, 0:2], a["p1"]).then_inc(dma["pe1"], 16)
            pe_operand(1)
            ffn(1, "ple1")
            ple(1, ["even"])

            S = START["evin"]
            high_parts_to(S + 2)
            c.wait("mix_free")
            act.dma_start(e_causal, a["causal"]).then_inc(dma["causal"], 16)
            act.dma_start(e_cnt, a["count"]).then_inc(dma["causal"], 16)
            act.dma_start(e_pw, a["pool_w"]).then_inc(dma["causal"], 16)
            rms()
            for n in range(3 + 1):
                high_parts_to(S + 1 + n + 2)
                norm_stats(n, e_tmp, e_sq, e_st, None, 3)
            high_parts_to(S + 9)
            for m in range(4):
                c.wait("pool_ps")
                from_psum("mixed", m, aux[m % 2][:, 0:T], e_out, pcol("pscale", m, 1))
            for n in range(8 + 2):
                if n < 8:
                    softmax_exp(n, e_l, e_st)
                if n >= 2:
                    attn_copy(n - 2, e_at, 2)
                if n >= 4 and n % 2 == 0:
                    c.wait("pv")
                    h = n // 2 - 2
                    from_psum("mixed", 4 + h, aux[h % 2][:, 0:T], e_out)
            c.wait("pv")
            from_psum("mixed", 7, aux[1][:, 0:T], e_out)
            residual("ffn2", START["evout"])

            ffn(2, "odd")

            S = START["qkv"]
            high_parts_to(S + 2)
            c.wait("mix_free")
            act.dma_start(k_mask, a["stickmask"]).then_inc(dma["stickmask"], 16)
            act.dma_start(k_tri, a["tri"]).then_inc(dma["stickmask"], 16)
            rms()
            for s in range(S, S + 12):
                high_parts_to(s + 2)
            high_parts_to(S + 14)
            for n in range(STICKS + 3):
                if n < STICKS:
                    c.wait("z_sb")
                    t = k_t[:, n % 2]
                    c.up_and_wait(A(t, k_z[:, n % 3], ACT.Abs), "act_step")
                    c.up_and_wait(A(t, t, ACT.Exp, scale=-1.0), "act_step")
                    c.up(A(t, t, ACT.Ln, bias=1.0), "log1p")
                if 2 <= n < STICKS + 2:
                    c.wait("log_a")
                    if n >= 4:
                        c.wait("stick_pv")
                    c.up(A(k_a[:, n % 2], k_z[:, (n - 2) % 3], ACT.Exp), "a_sb")
                if n >= 4 and n % 2 == 0:
                    m = n // 2 - 2
                    act.wait_ge(sem("stick_pv"), 2 * m + 2)
                    from_psum("stick", m, aux[m % 2][:, 0:T], k_out)
            residual("ffn3", START["out"])
            ffn(3, None)

        @block.vector
        def _(dve):
            c = Counts(dve, sem)
            V = nc.vector

            def step(ins):
                c.up_and_wait(ins, "dve_step")

            def low_tile(name, m):
                c.wait("hi_ready")
                c.up(V.scalar_tensor_tensor(lo(name)[:, m], x[:, m], gain(name, m), hi(name)[:, m].bitcast(f32),
                                            ALU.mult, ALU.subtract), "lo_ready")

            def low_of(name, m, buf):
                c.wait("hi_ready")
                c.up(V.tensor_tensor(lo(name)[:, m], buf[:, m % 2], hi(name)[:, m].bitcast(f32), ALU.subtract),
                     "lo_ready")

            def rms():
                c.wait("rms")
                c.up_and_wait(V.reciprocal(tok[:, 2:4], tok[:, 0:2]), "rstd_tok")

            def over_rms(dst, u):
                c.up_and_wait(V.tensor_tensor(dst, up[u][:], rstd[:].unsqueeze(1).broadcast_to([P, 2, T]), ALU.mult),
                              "up_free")

            c.up(V.memset(eps, EPS), "eps")
            w = s_work
            lr, li = s_prep[:, 0], s_prep[:, 1]

            def less_whole_turns(dst, src, tmp):
                step(V.tensor_scalar(tmp, src, ROUND, -ROUND, ALU.add, ALU.add))
                step(V.tensor_tensor(dst, src, tmp, ALU.subtract))

            dve.wait_ge(dma["s5_par"], 16)
            c.wait("dt")
            c.up_and_wait(V.tensor_tensor(w[:, 1], lr, w[:, 0], ALU.mult), "s5_mu")
            step(V.tensor_tensor(w[:, 2], li, w[:, 0], ALU.mult))
            step(V.tensor_scalar(w[:, 2], w[:, 2], 1.0 / (2.0 * math.pi), None, ALU.mult))
            less_whole_turns(s_phi, w[:, 2], w[:, 3])
            step(V.tensor_scalar(w[:, 12], s_phi, float(P), None, ALU.mult))
            less_whole_turns(w[:, 12], w[:, 12], w[:, 3])
            c.tell("s5_turn")
            dve.wait_ge(dma["par"], 16)
            step(V.tensor_tensor(tok[:, 0:2], pcol("lam")[:, 0:2], pcol("lam")[:, 2:4], ALU.mult))
            c.up(V.tensor_scalar(sub_g, pcol("subln"), 1.0 - LAM_INIT, None, ALU.mult), "lam_prod")

            def s5_turns(g):
                q = slice(8 * g, 8 * g + 8)
                step(V.tensor_tensor(s_cs[:, q], s_tmat.unsqueeze(1).broadcast_to([P, 8, P]),
                                     s_phi[:, q].unsqueeze(2).broadcast_to([P, 8, P]), ALU.mult))
                less_whole_turns(s_sn[:, q], s_cs[:, q], s_sn[:, q])
                c.tell("s5_frac")

            def s5_cosines(g):
                q = slice(8 * g, 8 * g + 8)
                c.wait("s5_half")
                step(V.tensor_scalar(s_cs[:, q], s_cs[:, q], -2.0, 1.0, ALU.mult, ALU.add))
                c.tell("s5_tables")

            dve.wait_ge(dma["s5_t"], 16)
            s5_turns(0)
            dve.wait_ge(dma["x"], 16)
            for m in range(KT):
                low_tile("ssm", m)
            s5_turns(1)
            c.wait("lam_exp")
            step(V.tensor_tensor(neg_lam, little[:, 4:5], little[:, 3:4], ALU.subtract))
            step(V.tensor_scalar(neg_lam, neg_lam, -LAM_INIT, None, ALU.add))
            s5_turns(2)
            rms()
            s5_turns(3)
            c.wait("rstd")
            for s in range(4):
                if s == 2:
                    c.wait("mag")
                    c.wait("s5_sc", 4)
                    step(V.tensor_tensor(w[:, 6], w[:, 5], w[:, 5], ALU.mult))
                    step(V.tensor_scalar(w[:, 6], w[:, 6], -2.0, 1.0, ALU.mult, ALU.add))
                    step(V.tensor_tensor(w[:, 6], w[:, 6], s_mag, ALU.mult))
                    step(V.tensor_scalar(w[:, 6], w[:, 6], -1.0, None, ALU.add))
                    step(V.tensor_tensor(w[:, 7], w[:, 4], s_mag, ALU.mult))
                    step(V.tensor_tensor(w[:, 8], lr, lr, ALU.mult))
                    step(V.tensor_tensor(w[:, 9], li, li, ALU.mult))
                    step(V.tensor_tensor(w[:, 8], w[:, 8], w[:, 9], ALU.add))
                    step(V.reciprocal(w[:, 8], w[:, 8]))
                    step(V.tensor_tensor(w[:, 9], w[:, 6], lr, ALU.mult))
                    step(V.tensor_tensor(w[:, 10], w[:, 7], li, ALU.mult))
                    step(V.tensor_tensor(w[:, 9], w[:, 9], w[:, 10], ALU.add))
                    step(V.tensor_tensor(w[:, 9], w[:, 9], w[:, 8], ALU.mult))
                    step(V.tensor_tensor(w[:, 10], w[:, 7], lr, ALU.mult))
                    step(V.tensor_tensor(w[:, 11], w[:, 6], li, ALU.mult))
                    step(V.tensor_tensor(w[:, 10], w[:, 10], w[:, 11], ALU.subtract))
                    step(V.tensor_tensor(w[:, 10], w[:, 10], w[:, 8], ALU.mult))
                    step(V.tensor_tensor(w[:, 13], w[:, 13], w[:, 13], ALU.mult))
                    step(V.tensor_scalar(s_e[:, 0], w[:, 13], -2.0, 1.0, ALU.mult, ALU.add))
                    step(V.tensor_scalar(s_e[:, 1], s_e[:, 2], -1.0, None, ALU.mult))
                    dve.wait_ge(dma["s5_c"], 16)
                    cr, ci, t0, t1 = (s_raw[:, k] for k in range(4))
                    fr = w[:, 9].unsqueeze(2).broadcast_to([P, PAIRS, 32])
                    fi = w[:, 10].unsqueeze(2).broadcast_to([P, PAIRS, 32])
                    step(V.tensor_tensor(t0, cr, fr, ALU.mult))
                    step(V.tensor_tensor(t1, ci, fi, ALU.mult))
                    step(V.tensor_tensor(s_c[:, 0], t0, t1, ALU.subtract))
                    step(V.tensor_tensor(t0, cr, fi, ALU.mult))
                    step(V.tensor_tensor(t1, ci, fr, ALU.mult))
                    c.up_and_wait(V.tensor_tensor(s_c[:, 1], t0, t1, ALU.add), "s5_c_ready")
                dve.wait_ge(sem("mm_done"), START["w_in"] + s + 1)
                over_rms(sq[:, 2 * s:2 * s + 2], s % 2)
            for g in range(4):
                s5_cosines(g)

            def s5_products(n):
                c.wait("s5_bu")
                if n:
                    c.wait("s5_sum", 2)
                if n >= 3:
                    c.wait("s5_out_pool", 2)
                bu = acc[:, 2 * (n % 2):2 * (n % 2) + 2].rearrange("p e (k t) -> p e k t", t=P)
                c.up(V.tensor_tensor(by_chunk(s_m[:, n % 3]), local(s_cs, n, 4), bu, ALU.mult), "s5_prod")
                c.up(V.tensor_tensor(by_chunk(s_m[:, 3]), local(s_sn, n, 4), bu, ALU.mult), "s5_prod")

            def s5_scans(n):
                z = s_m[:, n % 3]

                def scans(chunk):
                    q = slice(chunk * P, chunk * P + P)
                    for e in range(2):
                        r = s_mag[:, 2 * n + e:2 * n + e + 1].broadcast_to([P, P])
                        for k in range(2):
                            ins = V.tensor_tensor_scan(z[:, e, k, q], r, z[:, e, k, q],
                                                       s_init[:, e, k:k + 1] if chunk else 0.0, ALU.mult, ALU.add)
                            c.up(ins, "s5_scanned")
                    dve.wait_ge(sem("s5_scanned"), c.of("s5_scanned").value())

                scans(0)
                end = z[:, :, :, P - 1]
                turn = s_e[:, :, 2 * n:2 * n + 2]
                c.up(V.tensor_tensor(s_t[:, 0], end, turn[:, 0].unsqueeze(2).broadcast_to([P, 2, 2]), ALU.mult), "dve_step")
                step(V.tensor_tensor(s_t[:, 1], end, turn[:, 1:3].rearrange("p k e -> p e k"), ALU.mult))
                c.up(V.tensor_tensor(s_init[:, :, 0], s_t[:, 0, :, 0], s_t[:, 1, :, 1], ALU.add), "dve_step")
                step(V.tensor_tensor(s_init[:, :, 1], s_t[:, 0, :, 1], s_t[:, 1, :, 0], ALU.add))
                scans(1)
                c.tell("s5_scan")

            def s5_back(n):
                if n:
                    c.wait("s5_y")
                for e in range(2):
                    c.up(V.scalar_tensor_tensor(chunks(s_p[:, 1, e, 0].unsqueeze(1))[:, 0],
                                                chunks(s_m[:, n % 3, e, 0].unsqueeze(1))[:, 0], -1.0,
                                                local(s_sn, n, 2)[:, e], ALU.mult, ALU.mult), "s5_out_dve")

            def s5_output(m):
                dve.wait_ge(sem("s5_y"), 2 * m + 2)
                c.up_and_wait(V.scalar_tensor_tensor(s_y[:, 0], sq[:, m], pcol("dskip", m, 1), aux[m % 2][:, 0:T],
                                                     ALU.mult, ALU.add), "s5_ysum")

            def s5_low(m):
                c.wait("hi_ready")
                c.up(V.tensor_tensor(lo("s5")[:, m], s_y[:, 1], hi("s5")[:, m].bitcast(f32), ALU.subtract), "lo_ready")

            for n in range(2 * KT + 1):
                if n < 2 * KT:
                    s5_products(n)
                else:
                    c.wait("s5_sum", 2)
                if n:
                    s5_scans(n - 1)
                    s5_back(n - 1)
                if n >= 4 and n % 2 == 0:
                    s5_output(n // 2 - 2)
                if n >= 5 and n % 2:
                    s5_low(n // 2 - 2)
            s5_low(KT - 2)
            s5_output(KT - 1)
            s5_low(KT - 1)

            for m in range(KT):
                c.wait("gated")
                step(V.tensor_tensor(f_h[:, 0], up[m % 2][:, 0], f_gg[:, 0], ALU.mult))
                c.tell("up_free")
                c.up_and_wait(V.tensor_tensor(x[:, m], x[:, m], f_h[:, 0], ALU.add), "x_ready")
                if m:
                    low_tile("ffn0", m - 1)
            low_tile("ffn0", KT - 1)

            def ffn(l, end):
                S = START[f"ffn{l}"]
                conv = l < 2
                if conv:
                    for t in range(2):
                        step(V.memset(f_u[:, t, 0:2], 0.0))
                rms()
                c.wait("rstd")

                def tile(s, k, u, i, n, parity, part):
                    dve.wait_ge(sem("mm_done"), s + k + 1 if i is None else i * 6 + (s + k + 1))
                    us = f_u[:, 0:2, 2:258]
                    if conv:
                        over_rms(us, u)
                        for t in range(2):
                            base = COLS["conv"][0] + (l * 22 * 8)
                            pr = par[:, base:base + 176].rearrange("p (n w) -> p n w", w=8)
                            if i is None:
                                w4 = [pr[:, n, 4 * t + q:4 * t + q + 1] for q in range(4)]
                            else:
                                w4 = [pr[:, bass.ds(i * 4 + n, 1), 4 * t + q:4 * t + q + 1].rearrange("p a b -> p (a b)")
                                      for q in range(4)]
                            step(V.tensor_scalar(f_c[:, t], f_u[:, t, 2:258], w4[2], w4[3], ALU.mult, ALU.add))
                            step(V.scalar_tensor_tensor(f_c[:, t], f_u[:, t, 1:257], w4[1], f_c[:, t], ALU.mult, ALU.add))
                            ins = V.scalar_tensor_tensor(f_c[:, t], f_u[:, t, 0:256], w4[0], f_c[:, t], ALU.mult, ALU.add)
                            if t == 0:
                                c.up_and_wait(ins, "g_ready")
                            else:
                                step(ins)
                        val = f_c[:, 1]
                    else:
                        over_rms(us, u)
                        c.tell("g_ready")
                        val = f_u[:, 1, 2:258]
                    c.wait("gated")
                    step(V.tensor_tensor(f_h[:, 0], f_gg[:, 0], val, ALU.mult))
                    hh, hl = opnd[1][:, 0, 2 * parity + part], opnd[1][:, 1, 2 * parity + part]
                    step(V.tensor_copy(hh, f_h[:, 0]))
                    c.up_and_wait(V.tensor_tensor(hl, f_h[:, 0], hh.bitcast(f32), ALU.subtract), "h_ready")

                up0 = BANK[f"ffn{l}"]
                for j in range(3):
                    for part in range(2):
                        s = S + part if j == 0 else S + 3 * j - 1 + part
                        tile(s, 0, (up0 + part) % 2, None, 2 * j + part, j % 2, part)
                with dve.Fori(0, 4) as i:
                    c.enter(i, **(dict(dve_step=28, up_free=4, g_ready=4, gated=4, h_ready=4) if conv
                                  else dict(dve_step=8, up_free=4, g_ready=4, gated=4, h_ready=4)))
                    for j in (3, 4):
                        for part in range(2):
                            tile(S + 8, 3 * (j - 3) + part, (up0 + part) % 2, i, 2 * j + part, j % 2, part)
                    c.leave(4)
                for m in range(KT):
                    if m % 2 == 0:
                        c.wait("acc_bank") if m < KT - 2 else dve.wait_ge(sem("mm_done"), S + 33)
                    c.up_and_wait(V.tensor_tensor(x[:, m], x[:, m], acc[:, m // 2, (m % 2) * T:(m % 2) * T + T],
                                                  ALU.add), "x_ready")
                    if m and end:
                        low_tile(end, m - 1)
                if end:
                    low_tile(end, KT - 1)

            def pe_operand():
                for k in range(2):
                    c.wait("pe_hi")
                    c.up(V.tensor_tensor(opnd[1][:, 1, 6 + k], f_pe[:, k], opnd[1][:, 0, 6 + k].bitcast(f32),
                                         ALU.subtract), "pe_ready")

            def ple(l, ends):
                S = START[f"ple{l}"]
                u0 = BANK[f"ple{l}"]
                rms()
                c.wait("rstd")
                for g in range(4):
                    b = 2 * (g % 2)
                    dve.wait_ge(sem("mm_done"), S + (0 if g == 0 else g + 1) + 1)
                    over_rms(f_u[:, b:b + 2, 2:258], (u0 + g) % 2)
                    c.tell("ple_u")
                    if g == 0:
                        dve.wait_ge(sem("mm_done"), S + 2)
                    c.wait("gated")
                    step(V.tensor_tensor(f_c[:, b:b + 2], f_c[:, b:b + 2],
                                         acc[:, g].rearrange("p (a t) -> p a t", a=2), ALU.mult))
                    for e in range(2):
                        m = 2 * g + e
                        c.up_and_wait(V.tensor_tensor(x[:, m], x[:, m], f_c[:, b + e], ALU.add), "x_ready")
                        if m:
                            low_tile(ends[0], m - 1)
                low_tile(ends[0], KT - 1)
                c.tell("mix_free")
                for name in ends[1:]:
                    for m in range(KT):
                        low_tile(name, m)

            def residual(name, S, u0):
                for g in range(4):
                    dve.wait_ge(sem("mm_done"), S + g + 1)
                    for e in range(2):
                        m = 2 * g + e
                        c.up_and_wait(V.tensor_tensor(x[:, m], x[:, m], up[(u0 + g) % 2][:, e], ALU.add), "x_ready")
                        if m:
                            low_tile(name, m - 1)
                    c.tell("up_free")
                low_tile(name, KT - 1)

            def values(s, u, dst, n):
                dve.wait_ge(sem("mm_done"), s + 1)
                for t in range(TT):
                    step(V.tensor_scalar(dst[:, t], up[u][:, t, 0:n], tok[:, 2 + t:3 + t], None, ALU.mult))

            def head_norm(n, count, S, u0, tmp, st, last):
                if n < count:
                    dve.wait_ge(sem("mm_done"), S + n + 1)
                    over_rms(tmp[:, n % 3].rearrange("p (a t) -> p a t", a=2), (u0 + n) % 2)
                    c.tell("hn_raw")
                if 1 <= n <= count:
                    o = 16 * ((n - 1) % 2)
                    c.wait("hn_rms")
                    c.up(V.reciprocal(st[:, o + 8:o + 16], st[:, o:o + 8]), "hn_rstd")
                if n >= 2:
                    c.wait("hn_bc")
                    last(n - 2)

            def softmax_head(n, lbuf, st, bias):
                nk = P * (n % 2 + 1)
                b = n % 2
                L = lbuf[:, b].rearrange("p (c k) -> p c k", c=2)[:, :, 0:nk]
                c.wait("scores")
                S2 = acc[:, 2 * b:2 * b + 2, 0:nk]
                c.up_and_wait(V.scalar_tensor_tensor(L, S2, HD ** -0.5, bias.unsqueeze(1).broadcast_to([P, 2, nk]),
                                                     ALU.mult, ALU.add), "scores_read")
                c.up(V.tensor_reduce(st[:, 40 + 2 * b:42 + 2 * b], L, AX.X, ALU.max, negate=True), "neg_max")

            def softmax_tail(n, lbuf, abuf, st, diff):
                nk = P * (n % 2 + 1)
                b = n % 2
                L = lbuf[:, b].rearrange("p (c k) -> p c k", c=2)[:, :, 0:nk]
                c.wait("exps", 2)
                if n >= 2:
                    c.wait("at_ps")
                r = st[:, 48 + 2 * b:50 + 2 * b]
                step(V.reciprocal(r, st[:, 44 + 2 * b:46 + 2 * b]))
                if diff:
                    step(V.tensor_tensor(r[:, 1:2], r[:, 1:2], neg_lam, ALU.mult))
                    step(V.tensor_scalar(L[:, 1], L[:, 1], r[:, 1:2], None, ALU.mult))
                    c.up(V.scalar_tensor_tensor(abuf[:, b, 0:nk], L[:, 0], r[:, 0:1], L[:, 1], ALU.mult, ALU.add),
                         "probs")
                else:
                    ab = abuf[:, b].rearrange("p (c k) -> p c k", c=2)
                    step(V.tensor_scalar(ab[:, 0, 0:nk], L[:, 0], r[:, 0:1], None, ALU.mult))
                    c.up(V.tensor_scalar(ab[:, 1, 0:nk], L[:, 1], r[:, 1:2], None, ALU.mult), "probs")
                dve.wait_ge(sem("probs"), c.of("probs").value())

            pe_operand()
            ffn(0, "ple0")
            ple(0, ["kv", "q"])

            S, u0 = START["kvq"], BANK["kvq"]
            c.wait("bias_ps")
            c.up(V.tensor_copy(d_sq[0:HEADS, 0, 0:384], aux[0][0:HEADS, 0:384]), "bias_sb")
            rms()
            for g in range(4):
                values(S + g, (u0 + g) % 2, d_v[:, :, g * 256:(g + 1) * 256], 256)
                c.tell("up_free")
            c.wait("rstd")

            def diff_normed(n):
                dst = (d_k if n % 2 == 0 else d_q)[:, 2 * (n // 2):2 * (n // 2) + 2]
                c.up_and_wait(V.scalar_tensor_tensor(dst, d_tmp[:, n % 3].rearrange("p (a t) -> p a t", a=2),
                                                     pcol("qk", n % 2, 1),
                                                     acc[:, n % 2].rearrange("p (a t) -> p a t", a=2),
                                                     ALU.mult, ALU.mult), "qk_ready")

            for n in range(8 + 2):
                head_norm(n, 8, S + 4, u0 + 4, d_tmp, d_st, diff_normed)
            dve.wait_ge(dma["bias_r"], 16)
            for n in range(2 * HEADS + 1):
                if n < 2 * HEADS:
                    h = n // 2
                    bias = d_bias[:, h, 0:T] if n % 2 else d_bias[:, h, P:T]
                    softmax_head(n, d_l, d_st, bias)
                if n >= 1:
                    softmax_tail(n - 1, d_l, d_a, d_st, True)
            c.wait("at_ps", 2)
            c.wait("o_rms")
            c.up(V.reciprocal(d_st[:, 16:32], d_st[:, 0:16]), "o_rstd")
            for m in range(KT):
                if m % 2 == 0:
                    c.wait("o_bc")
                c.up_and_wait(V.tensor_tensor(sq[:, m], sq[:, m], acc[:, m // 2, (m % 2) * T:(m % 2) * T + T],
                                              ALU.mult), "o_norm")
                c.wait("hi_ready")
                c.up(V.scalar_tensor_tensor(lo("diff")[:, m], sq[:, m], sub_g, hi("diff")[:, m].bitcast(f32),
                                            ALU.mult, ALU.subtract), "lo_ready")
            residual("ffn1", START["wo"], BANK["wo"])

            pe_operand()
            ffn(1, "ple1")
            ple(1, ["even"])

            S, u0 = START["evin"], BANK["evin"]
            rms()
            dve.wait_ge(sem("mm_done"), S + 1)
            for t in range(TT):
                step(V.tensor_scalar(e_v[:, t], up[u0 % 2][:, t, 0:P], tok[:, 2 + t:3 + t], None, ALU.mult))
                step(V.tensor_scalar(e_w[:, t], up[u0 % 2][:, t, P:P + 4], tok[:, 2 + t:3 + t], 1.0 / 16,
                                     ALU.mult, ALU.mult))
            c.tell("up_free")
            c.wait("rstd")

            def even_normed(n):
                src = e_tmp[:, n % 3].rearrange("p (a t) -> p a t", a=2)
                bc = acc[:, n % 2].rearrange("p (a t) -> p a t", a=2)
                if n == 0:
                    step(V.tensor_copy(e_pl[:, 0], src[:, 1]))
                    c.up_and_wait(V.scalar_tensor_tensor(e_k, src[:, 0], pcol("evqk", 0, 1), bc[:, 0],
                                                         ALU.mult, ALU.mult), "qk_ready")
                else:
                    c.up_and_wait(V.scalar_tensor_tensor(e_q[:, 2 * n - 2:2 * n], src, pcol("evqk", 1, 1), bc,
                                                         ALU.mult, ALU.mult), "qk_ready")

            for n in range(3 + 2):
                head_norm(n, 3, S + 1, u0 + 1, e_tmp, e_st, even_normed)
            for n in range(3):
                dve.wait_ge(sem("mm_done"), S + 5 + n)
                over_rms(e_pl[:, 1 + 2 * n:3 + 2 * n], (u0 + 4 + n) % 2)
                if n == 0:
                    c.tell("idx_ready")
            step(V.memset(e_pa[:, :, 0:16], 0.0))
            step(V.memset(e_pb[:, :, 0:16], 0.0))
            step(V.tensor_copy(e_pa[:, :, 16:], e_pl[:, 3:7]))
            src, dst = e_pa, e_pb
            for g in range(4):
                wdt = 2 ** g
                step(V.tensor_tensor(dst[:, g:, 16:], src[:, g:, 16:], src[:, g:, 16 - wdt:16 + T - wdt], ALU.add))
                src, dst = dst, src
            dve.wait_ge(dma["causal"], 48)
            for g in range(4):
                step(V.tensor_tensor(e_cnt[:, g], e_cnt[:, g], (e_pa if g % 2 else e_pb)[:, g, 16:], ALU.mult))
            c.up_and_wait(V.tensor_tensor(e_cnt, e_cnt, e_pl[:, 3:7], ALU.subtract), "pooled")
            for m in range(4):
                low_of("mixed", m, e_out)
            for qb in range(2):
                nk = P * (qb + 1)
                sc = e_mask[:, qb, 0:nk]
                c.wait("idx_ps")
                step(V.tensor_copy(sc, e_causal[:, qb, 0:nk]))
                for h in range(4):
                    rel = acc[:, h, 0:nk]
                    step(V.tensor_scalar(e_rel[:, 0:nk], rel, 0.0, e_w[:, qb, h:h + 1], ALU.max, ALU.mult))
                    step(V.tensor_tensor(sc, sc, e_rel[:, 0:nk], ALU.add))
                c.tell("idx_read")
                for _ in range(SEL // 8):
                    step(V.max(e_m8, sc))
                    step(V.match_replace(sc, e_m8, sc, TAKEN))
                step(V.tensor_scalar(sc, sc, TAKEN / 2, NEG, ALU.is_gt, ALU.mult))
                step(V.tensor_tensor(sc, sc, e_causal[:, qb, 0:nk], ALU.add))
            for n in range(8 + 1):
                if n < 8:
                    softmax_head(n, e_l, e_st, e_mask[:, n % 2, 0:P * (n % 2 + 1)])
                if n >= 1:
                    softmax_tail(n - 1, e_l, e_a, e_st, False)
                if n >= 5 and n % 2:
                    low_of("mixed", 4 + (n - 5) // 2, e_out)
            low_of("mixed", 6, e_out)
            low_of("mixed", 7, e_out)
            residual("ffn2", START["evout"], BANK["evout"])

            ffn(2, "odd")
            c.tell("mix_free")

            S, u0 = START["qkv"], BANK["qkv"]
            rms()
            for g in range(4):
                values(S + g, (u0 + g) % 2, k_v[:, :, g * 256:(g + 1) * 256], 256)
                c.tell("up_free")
            c.wait("rstd")
            for n in range(8):
                dve.wait_ge(sem("mm_done"), S + 5 + n)
                dst = (k_k if n % 2 == 0 else k_q)[:, 2 * (n // 2):2 * (n // 2) + 2]
                over_rms(dst, (u0 + 4 + n) % 2)
                c.tell("stick_qk")
            dve.wait_ge(dma["stickmask"], 32)
            for n in range(STICKS + 2):
                if n < STICKS:
                    c.wait("z_ps")
                    if n >= 3:
                        c.wait("a_sb")
                    c.up(V.scalar_tensor_tensor(k_z[:, n % 3], acc[:, n % 2, 0:384], HD ** -0.5, k_mask,
                                                ALU.mult, ALU.add), "z_sb")
                    dve.wait_ge(sem("z_sb"), c.of("z_sb").value())
                if 1 <= n <= STICKS:
                    c.wait("log1p")
                    h = n - 1
                    c.up(V.scalar_tensor_tensor(k_b[:, h % 2], k_z[:, h % 3], 0.0, k_t[:, h % 2], ALU.max, ALU.add),
                         "brk")
                if n >= 2:
                    h = n - 2
                    c.wait("remain")
                    c.up(V.tensor_tensor(k_z[:, h % 3], k_z[:, h % 3], acc[:, 2 + h % 2, 0:384], ALU.subtract),
                         "log_a")
                    if h % 2 == 1 and h >= 3:
                        low_of("stick", (h - 3) // 2, k_out)
            low_of("stick", 7, k_out)
            residual("ffn3", START["out"], BANK["out"])
            ffn(3, None)

        @block.tensor
        def _(pe):
            c = Counts(pe, sem)
            MM = nc.tensor.matmul
            used = [0]

            def slot_ready(s, i=None):
                pe.wait_ge(sem("w_ready"), s + 1 if i is None else i * 6 + (s + 1))

            def bank(i=None, loop_uses=0):
                u = used[0]
                used[0] += 1
                if u >= 2:
                    pe.wait_ge(sem("up_free"), u - 1 if i is None else i * 4 + (u - 1))
                return up[u % 2]

            def three(o, l_hi, l_lo, r_hi, r_lo, start, stop):
                MM(o, l_hi, r_hi, start=start, stop=False, skip_group_check=True)
                MM(o, l_lo, r_hi, start=False, stop=False, skip_group_check=True)
                return MM(o, l_hi, r_lo, start=False, stop=stop, skip_group_check=True)

            def up_slot(name, s, i=None, fresh=False, tiles=2):
                slot_ready(s, i)
                o = bank(i)
                b = s % SPLIT
                for k in range(KT):
                    if fresh:
                        c.wait("hi_ready")
                        c.wait("lo_ready")
                    for m in range(tiles):
                        w = slice((2 * k + m) * P, (2 * k + m + 1) * P)
                        ins = three(o[:, m], w_hi[:, b, w], w_lo[:, b, w], hi(name)[:, k], lo(name)[:, k],
                                    k == 0 and m == 0, k == KT - 1)
                c.up(ins, "mm_done")

            def token_slot(name, s, fresh=False):
                slot_ready(s)
                o = bank()
                b = s % SPLIT
                for k in range(KT):
                    if fresh:
                        c.wait("hi_ready")
                        c.wait("lo_ready")
                    for t in range(TT):
                        w = slice(2 * k * P, (2 * k + 2) * P)
                        q = slice(t * P, (t + 1) * P)
                        ins = three(o[:, t], hi(name)[:, k, q], lo(name)[:, k, q], w_hi[:, b, w], w_lo[:, b, w],
                                    k == 0 and t == 0, k == KT - 1)
                c.up(ins, "mm_done")

            def down_slot(s, ops, first, last, i=None, each=False):
                slot_ready(s, i)
                b = s % SPLIT
                for m in range(KT):
                    for k in range(2):
                        w = slice((8 * k + m) * P, (8 * k + m + 1) * P)
                        ins = three(acc[:, m // 2, (m % 2) * T:(m % 2) * T + T], w_hi[:, b, w], w_lo[:, b, w],
                                    opnd[1][:, 0, ops + k], opnd[1][:, 1, ops + k],
                                    first and k == 0 and m % 2 == 0, last and k == 1)
                    if each and m % 2 and m < KT - 1:
                        c.up(ins, "acc_bank")
                return ins

            def rms():
                c.wait("sq_ready", 8)
                for t in range(TT):
                    for k in range(KT):
                        ins = MM(aux[0][:, t:t + 1], sq[:, k, t * P:(t + 1) * P], ones[:, 0:1],
                                 start=(k == 0), stop=(k == KT - 1))
                c.up(ins, "ssq")

            def rms_out():
                c.wait("rstd_tok")
                for t in range(TT):
                    ins = MM(aux[1][:, t * P:(t + 1) * P], tok[:, 2 + t:3 + t].broadcast_to([P, P]), ident,
                             start=True, stop=True)
                c.up(ins, "rstd_bc")

            pe.wait_ge(dma["par"], 16)
            c.wait("lam_prod")
            c.up(MM(aux[1][:, 0:2], ones, tok[:, 0:2], start=True, stop=True), "lam_sum")

            S = START["w_in"]
            up_slot("ssm", S, fresh=True)
            rms()
            up_slot("ssm", S + 1)
            rms_out()
            up_slot("ssm", S + 2)
            up_slot("ssm", S + 3)
            pe.wait_ge(dma["s5_mat"], 16)
            c.wait("s5_c_ready")

            def s5_in(n):
                m, b = n // 2, n % 2
                if n % 2 == 0:
                    pe.wait_ge(sem("up_free"), m // 2 + 1)
                if n >= 2:
                    c.wait("s5_prod", 2)
                for e in range(2):
                    r = slice(32 * (2 * b + e), 32 * (2 * b + e) + 32)
                    for k in range(2):
                        ins = MM(acc[:, 2 * b + e, k * T:(k + 1) * T], s_b[r, k, m], sq[r, m], start=True, stop=True)
                c.up(ins, "s5_bu")

            def s5_out(n):
                m, b = n // 2, n % 2
                c.wait("s5_out_pool", 2)
                c.wait("s5_out_dve", 2)
                if n % 2 == 0 and m >= 2:
                    c.wait("s5_ysum")
                for e in range(2):
                    q = 2 * b + e
                    o = aux[m % 2][32 * q:32 * q + 32, 0:T]
                    i = 2 * n + e
                    MM(o, s_c[:, 0, i], s_p[:, 0, e, 0], start=True, stop=False, tile_position=(0, 32 * q))
                    MM(o, s_c[:, 1, i], s_p[:, 0, e, 1], start=False, stop=False, tile_position=(0, 32 * q))
                    MM(o, s_c[:, 1, i], s_p[:, 1, e, 0], start=False, stop=False, tile_position=(0, 32 * q))
                    ins = MM(o, s_c[:, 0, i], s_p[:, 1, e, 1], start=False, stop=True, tile_position=(0, 32 * q))
                c.up(ins, "s5_y")

            s5_in(0)
            s5_in(1)
            for n in range(2 * KT + 1):
                if n + 2 < 2 * KT:
                    s5_in(n + 2)
                if n == 0:
                    c.wait("s5_tables", 4)
                if n:
                    s5_out(n - 1)
            S = START["glu"]
            for m in range(KT):
                up_slot("s5", S + m, fresh=(m == 0))

            def ffn(l, name):
                S = START[f"ffn{l}"]
                assert used[0] == BANK[f"ffn{l}"]
                up_slot(name, S, fresh=True)
                rms()
                up_slot(name, S + 1)
                rms_out()
                up_slot(name, S + 2)
                up_slot(name, S + 3)

                def down(s, parity, first=False, last=False, i=None, each=False):
                    c.wait("h_ready", 2)
                    ins = down_slot(s, 2 * parity, first, last, i, each)
                    c.up(ins, "mm_done")

                down(S + 4, 0, first=True)
                up_slot(name, S + 5)
                up_slot(name, S + 6)
                down(S + 7, 1)
                with pe.Fori(0, 4) as i:
                    c.enter(i, h_ready=4, mm_done=6)
                    for k in (0, 3):
                        up_slot(name, S + 8 + k, i)
                        up_slot(name, S + 9 + k, i)
                        down(S + 10 + k, k // 3, i=i)
                    c.leave(4)
                used[0] += 3 * 4
                down(S + 32, 0, last=True, each=True)

            def ple(l):
                S = START[f"ple{l}"]
                assert used[0] == BANK[f"ple{l}"]
                up_slot(f"ple{l}", S, fresh=True)
                rms()
                c.wait("pe_ready", 2)
                ins = down_slot(S + 1, 6, True, True)
                c.up(ins, "mm_done")
                rms_out()
                for g in range(1, 4):
                    up_slot(f"ple{l}", S + g + 1)

            def head_stats(n, sqb):
                c.wait("hn_sq")
                for e in range(2):
                    for t in range(TT):
                        col = 16 * (n % 2) + 4 * t + 2 * e
                        ins = MM(aux[0][:, col:col + 2], sqb[:, n % 2, e * T + t * P:e * T + (t + 1) * P],
                                 pcol("half"), start=True, stop=True)
                c.up(ins, "hn_ssq")

            def head_bc(n, st):
                c.wait("hn_rstd")
                for e in range(2):
                    for t in range(TT):
                        col = 16 * (n % 2) + 8 + 4 * t + 2 * e
                        for g in range(2):
                            ins = MM(acc[HD * g:HD * g + HD, n % 2, e * T + t * P:e * T + (t + 1) * P],
                                     st[:, col + g:col + g + 1].broadcast_to([P, HD]), ident, start=True, stop=True,
                                     tile_position=(0, HD * g))
                c.up(ins, "hn_bc")

            def transposes(n, abuf, per):
                nk = n % 2 + 1
                c.wait("probs")
                if n >= 2:
                    c.wait("at_sb", per)
                for j in range(per):
                    for k in range(nk):
                        o = 4 // per * j + k
                        ins = nc.tensor.transpose(up[n % 2][:, o // 2, (o % 2) * P:(o % 2 + 1) * P],
                                                  abuf[:, n % 2, j * T + k * P:j * T + (k + 1) * P], ident)
                c.up(ins, "at_ps")

            def head_values(h, o, v, at, rows):
                MM(o[:, 0:T], v[:, 0], at[:, 0:T], start=True, stop=False, skip_group_check=True)
                return MM(o[:, P:T], v[:, 1], at[:, T + P:2 * T], start=False, stop=True, skip_group_check=True)

            ffn(0, "ffn0")
            ple(0)

            S = START["kvq"]
            assert used[0] == BANK["kvq"]
            token_slot("kv", S, fresh=True)
            pe.wait_ge(dma["bias_oh"], 16)
            c.up(MM(aux[0][0:HEADS, 0:384], d_oh[:, 384:384 + HEADS], d_oh[:, 0:384], start=True, stop=True), "bias_ps")
            c.wait("bias_sb")
            rms()
            token_slot("kv", S + 1)
            rms_out()
            token_slot("kv", S + 2)
            token_slot("kv", S + 3)
            c.wait("hi_ready", 8)
            c.wait("lo_ready", 8)
            for n in range(8 + 2):
                if n < 8:
                    up_slot("kv" if n % 2 == 0 else "q", S + 4 + n)
                if n >= 2:
                    if n >= 4:
                        c.wait("qk_ready")
                    head_bc(n - 2, d_st)
                if 1 <= n <= 8:
                    head_stats(n - 1, d_sq)
            c.wait("qk_ready", 2)

            def diff_scores(n):
                h, qb = n // 2, n % 2
                if n >= 2:
                    c.wait("scores_read")
                for e in range(2):
                    r = slice(HD * e, HD * e + HD)
                    ins = MM(acc[:, 2 * (n % 2) + e, 0:P * (qb + 1)], d_q[r, h, qb * P:(qb + 1) * P],
                             d_k[r, h, 0:P * (qb + 1)], start=True, stop=True)
                c.up(ins, "scores")

            def diff_values(h):
                pe.wait_ge(sem("at_sb"), 2 * h + 2)
                if h >= 2:
                    pe.wait_ge(sem("o_sq"), h - 1)
                ins = head_values(h, aux[h % 2], d_v[:, :, h * P:(h + 1) * P], d_at[:, h % 2], P)
                c.up(ins, "pv")

            for n in range(2 * HEADS + 3):
                if n < 2 * HEADS:
                    diff_scores(n)
                if 1 <= n <= 2 * HEADS:
                    transposes(n - 1, d_a, 1)
                if n >= 3 and n % 2 == 1 and (n - 3) // 2 < HEADS:
                    diff_values((n - 3) // 2)
            c.wait("o_sq", HEADS)
            c.wait("scores_read", 2)
            for h in range(HEADS):
                for t in range(TT):
                    ins = MM(acc[:, 0, 2 * h + t:2 * h + t + 1], d_q[:, h, t * P:(t + 1) * P], ones[:, 0:1],
                             start=True, stop=True)
            c.up(ins, "o_ssq")
            c.wait("o_rstd")
            c.wait("at_sb", 2)
            for m in range(KT):
                for t in range(TT):
                    ins = MM(acc[:, m // 2, (m % 2) * T + t * P:(m % 2) * T + (t + 1) * P],
                             d_st[:, 16 + 2 * m + t:17 + 2 * m + t].broadcast_to([P, P]), ident,
                             start=True, stop=True)
                if m % 2:
                    c.up(ins, "o_bc")
            S = START["wo"]
            assert used[0] == BANK["wo"]
            for g in range(4):
                up_slot("diff", S + g, fresh=(g == 0))

            ffn(1, "ffn1")
            ple(1)

            S = START["evin"]
            assert used[0] == BANK["evin"]
            token_slot("even", S, fresh=True)
            rms()
            up_slot("even", S + 1)
            rms_out()
            for n in range(1, 6):
                up_slot("even", S + 1 + n)
                if 2 <= n <= 4:
                    if n == 4:
                        c.wait("qk_ready")
                    head_bc(n - 2, e_st)
                if n <= 3:
                    head_stats(n - 1, e_sq)
            c.wait("idx_ready")
            c.wait("qk_ready", 2)
            for qb in range(2):
                if qb:
                    c.wait("idx_read")
                for h in range(4):
                    r = slice(HD * (h % 2), HD * (h % 2) + HD)
                    ins = MM(acc[:, h, 0:P * (qb + 1)],
                             e_pl[r, 1 + h // 2, qb * P:(qb + 1) * P], e_pl[r, 0, 0:P * (qb + 1)],
                             start=True, stop=True)
                c.up(ins, "idx_ps")
                if qb == 0:
                    c.wait("pooled")
                    for g in range(4):
                        if g >= 2:
                            c.wait("hi_ready")
                        c.up(MM(aux[g % 2][:, 0:T], e_pw[:, g], e_cnt[:, g], start=True, stop=True), "pool_ps")
            c.wait("idx_read")

            def even_scores(n):
                h, qb = n // 2, n % 2
                if n >= 2:
                    c.wait("scores_read")
                for e in range(2):
                    r = slice(HD * e, HD * e + HD)
                    ins = MM(acc[:, 2 * (n % 2) + e, 0:P * (qb + 1)], e_q[r, h, qb * P:(qb + 1) * P],
                             e_k[r, 0:P * (qb + 1)], start=True, stop=True)
                c.up(ins, "scores")

            at0 = 2 * HEADS
            for n in range(8 + 3):
                if n < 8:
                    even_scores(n)
                if 1 <= n <= 8:
                    transposes(n - 1, e_a, 2)
                if n >= 3 and n % 2 == 1:
                    h = (n - 3) // 2
                    pe.wait_ge(sem("at_sb"), at0 + 4 * (h + 1))
                    c.wait("hi_ready")
                    for e in range(2):
                        o = aux[h % 2][HD * e:HD * e + HD]
                        at = e_at[:, 2 * (h % 2) + e]
                        MM(o[:, 0:T], e_v[:, 0, HD * e:HD * e + HD], at[:, 0:T], start=True, stop=False,
                           tile_position=(0, HD * e), skip_group_check=True)
                        ins = MM(o[:, P:T], e_v[:, 1, HD * e:HD * e + HD], at[:, T + P:2 * T], start=False, stop=True,
                                 tile_position=(0, HD * e), skip_group_check=True)
                    c.up(ins, "pv")
            S = START["evout"]
            assert used[0] == BANK["evout"]
            c.wait("hi_ready", 2)
            c.wait("lo_ready", 8)
            for g in range(4):
                up_slot("mixed", S + g)

            ffn(2, "ffn2")

            S = START["qkv"]
            assert used[0] == BANK["qkv"]
            token_slot("odd", S, fresh=True)
            rms()
            token_slot("odd", S + 1)
            rms_out()
            token_slot("odd", S + 2)
            token_slot("odd", S + 3)
            for n in range(8):
                up_slot("odd", S + 4 + n)
            pe.wait_ge(dma["stickmask"], 32)
            c.wait("stick_qk", 8)
            for n in range(STICKS + 3):
                if n < STICKS:
                    m, r = n // 2, slice(HD * (n % 2), HD * (n % 2) + HD)
                    if n >= 2:
                        c.wait("z_sb")
                    MM(acc[:, n % 2, 0:T], k_k[r, m, 0:P], k_q[r, m, 0:T], start=True, stop=True)
                    c.up(MM(acc[:, n % 2, T:T + P], k_k[r, m, P:T], k_q[r, m, P:T], start=True, stop=True), "z_ps")
                if 1 <= n <= STICKS:
                    h = n - 1
                    c.wait("brk")
                    if h >= 2:
                        c.wait("log_a")
                    o, b = acc[:, 2 + h % 2], k_b[:, h % 2]
                    MM(o[:, 0:T], k_tri, b[:, 0:T], start=True, stop=False, skip_group_check=True)
                    MM(o[:, P:T], ones, b[:, T:T + P], start=False, stop=False, skip_group_check=True)
                    c.up(MM(o[:, T:T + P], k_tri, b[:, T:T + P], start=False, stop=True, skip_group_check=True),
                         "remain")
                if n >= 3:
                    h = n - 3
                    m, r = h // 2, HD * (h % 2)
                    c.wait("a_sb")
                    if h % 2 == 0 and m >= 2:
                        c.wait("hi_ready")
                    o = aux[m % 2][r:r + HD]
                    MM(o[:, 0:T], k_v[:, 0, h * HD:(h + 1) * HD], k_a[:, h % 2, 0:T], start=True, stop=False,
                       tile_position=(0, r), skip_group_check=True)
                    ins = MM(o[:, P:T], k_v[:, 1, h * HD:(h + 1) * HD], k_a[:, h % 2, T:T + P], start=False,
                             stop=True, tile_position=(0, r), skip_group_check=True)
                    c.up(ins, "stick_pv")
            S = START["out"]
            assert used[0] == BANK["out"]
            c.wait("hi_ready", 2)
            c.wait("lo_ready", 8)
            for g in range(4):
                up_slot("stick", S + g)
            ffn(3, "ffn3")


def _up(*cols):
    w = np.concatenate(cols, axis=1)
    if w.shape[1] < 256:
        w = np.pad(w, ((0, 0), (0, 256 - w.shape[1])))
    return w.reshape(KT, P, 256).transpose(1, 0, 2).reshape(P, 2048)


def _down(rows):
    return rows.reshape(2, P, D).transpose(1, 0, 2).reshape(P, 2048)


def _pieces(w, n=256):
    return [w[:, i:i + n] for i in range(0, w.shape[1], n)]


def _ffn_slots(gate, val, down):
    ups = [_up(gate[:, n * P:(n + 1) * P], val[:, n * P:(n + 1) * P]) for n in range(2 * STEPS)]
    downs = [_down(down[j * 256:(j + 1) * 256]) for j in range(STEPS)]
    out = ups[0:2]
    for j in range(1, STEPS):
        out += [ups[2 * j], ups[2 * j + 1], downs[j - 1]]
    return out + [downs[STEPS - 1]]


def _stream(i):
    s = [_up(c) for c in _pieces(i["ssm_w_in"][0])]
    glu = i["ssm_w_glu"][0]
    s += [_up(glu[:, m * P:(m + 1) * P], glu[:, D + m * P:D + (m + 1) * P]) for m in range(KT)]

    def ffn(l):
        w = i["ffn_w_up"][l]
        return _ffn_slots(w[:, :FF], w[:, FF:], i["ffn_w_down"][l])

    def ple(l):
        g = [_up(c) for c in _pieces(i["ple_w_gate"][l])]
        return [g[0], _down(i["ple_w_proj"][l])] + g[1:]

    def qk(k, q):
        return [_up(c) for pair in zip(_pieces(k), _pieces(q)) for c in pair]

    kv, wq = i["kv_w"], i["attn_w_q"][0]
    s += ffn(0) + ple(0)
    s += [_up(c) for c in _pieces(kv[:, D:])] + qk(kv[:, :D], wq)
    s += [_up(c) for c in _pieces(i["attn_w_o"][0])] + ffn(1) + ple(1)
    w = i["ev_w_in_2"][0]
    q, k, v, qi, ki, wi, u = (w[:, a:b] for a, b in [(0, 512), (512, 640), (640, 768), (768, 1024), (1024, 1088),
                                                     (1088, 1092), (1092, 1604)])
    q = np.concatenate([q[:, c * 64:(c + 1) * 64] for t in range(4) for c in (t, t + 4)], axis=1)
    s += [_up(v, wi), _up(k, ki, ki), _up(q[:, :256]), _up(q[:, 256:]), _up(qi), _up(u[:, :256]), _up(u[:, 256:])]
    w = i["ev_w_out_2"][0]
    w = np.concatenate([w[512:]] + [w[c * 64:(c + 1) * 64] for t in range(4) for c in (t, t + 4)], axis=0)
    s += [_up(c) for c in _pieces(w)]
    s += _ffn_slots(i["ffn_w1_2"][0], i["ffn_w3_2"][0], i["ffn_w2_2"][0])
    w = i["od_w_qkv_2"][0]
    s += [_up(c) for c in _pieces(w[:, 2 * D:])] + qk(w[:, D:2 * D], w[:, :D])
    s += [_up(c) for c in _pieces(i["od_w_out_2"][0])]
    s += _ffn_slots(i["ffn_w1_2"][1], i["ffn_w3_2"][1], i["ffn_w2_2"][1])
    assert len(s) == N_SLOTS
    return np.stack(s)


def _features(v):
    return np.moveaxis(v.reshape(v.shape[:-1] + (KT, P)), -1, 0)


def _bucket():
    n = 255 - np.arange(384)
    nf = np.maximum(n, 16).astype(np.float32)
    large = 16 + (np.log(nf / np.float32(16)) / np.float32(math.log(8.0)) * np.float32(16)).astype(np.int32)
    b = np.where(n < 16, n, np.minimum(large, 31))
    oh = np.zeros((33, 384), np.float32)
    for m in range(384):
        oh[b[m] if n[m] >= 0 else 32, m] = 1.0
    return oh


def _layout(i):
    f = np.float32
    i = {k: np.asarray(v) for k, v in i.items()}
    a = {"stream": _stream(i)}
    a["x"] = i["x"][0].T.reshape(KT, P, T).transpose(1, 0, 2)
    for l in range(2):
        a[f"p{l}"] = i["p"][l, 0].T.reshape(2, P, T).transpose(1, 0, 2)
    gains = np.stack([i["ssm_norm"][0], i["ffn_norm"][0], i["ple_norm"][0], i["kv_norm"], i["attn_norm"][0],
                      i["ffn_norm"][1], i["ple_norm"][1], i["norm_mix_g_2"][0], i["norm_ffn_g_2"][0],
                      i["norm_mix_g_2"][1], i["norm_ffn_g_2"][1]])
    cw = np.concatenate([i["ffn_conv_w"], i["ffn_conv_b"][:, None]], axis=1).reshape(2, 4, 2, 22, P)
    cw = cw.transpose(4, 0, 3, 2, 1).reshape(P, -1)
    col = lambda v: np.concatenate([v, v])[:, None]
    half = np.zeros((P, 2), f)
    half[:64, 0] = half[64:, 1] = 1.0
    lam = np.zeros((P, 4), f)
    for j, n in enumerate(["lambda_q1", "lambda_q2", "lambda_k1", "lambda_k2"]):
        lam[:64, j] = i[n][0]
    a["par"] = np.concatenate([
        _features(gains).reshape(P, -1), cw, _features(i["ssm_d"][0]), col(i["k_norm"]), col(i["q_norm"][0]),
        i["subln"][0][:, None], col(i["ev_k_norm_g_2"][0]), col(i["ev_q_norm_g_2"][0]), lam,
        i["ev_pool_scale_2"][0].reshape(4, P).T, np.ones((P, P), f), half, np.eye(P, dtype=f)], axis=1)
    pairs = lambda v: v.reshape(PAIRS, P).T
    dt = np.repeat(i["ssm_log_dt"][0][:, None], STATE, axis=1)
    a["s5_par"] = np.stack([pairs(i["ssm_lambda_re"][0]), pairs(i["ssm_lambda_im"][0]), pairs(dt)], axis=1)
    b = np.zeros((4, 32, 2, KT, P), f)
    cc = np.zeros((P, 2, PAIRS, 32), f)
    for r, (nb, ncn) in enumerate([("ssm_b_re", "ssm_c_re"), ("ssm_b_im", "ssm_c_im")]):
        bb, c_ = i[nb][0], i[ncn][0]
        for g in range(GROUPS):
            pr, h = g // 2, g % 2
            b[pr % 4, h * 16:h * 16 + 16, r, pr // 4, h * 64:h * 64 + 64] = bb[g].T
            cc[h * 64:h * 64 + 64, r, pr, h * 16:h * 16 + 16] = c_[g].T
    a["s5_b"], a["s5_c"] = b.reshape(P, 2, KT, P), cc
    a["tmat"] = np.broadcast_to(np.arange(P, dtype=f), (P, P))
    wb = np.concatenate([i["rel_bias"], np.full((1, HEADS), NEG, f)])
    a["bias_oh"] = np.concatenate([_bucket(), wb], axis=1)
    q, k = np.arange(P)[:, None], np.arange(T)[None, :]
    a["causal"] = np.stack([np.where(k <= q + P * j, 0, NEG) for j in range(2)], axis=1).astype(f)
    cnt = np.stack([1.0 / np.minimum(np.arange(1, T + 1), w) for w in (2, 4, 8, 16)]).astype(f)
    a["count"] = np.broadcast_to(cnt, (P, 4, T))
    a["pool_w"] = i["ev_pool_w_2"][0].transpose(1, 0, 2)
    s_, q_ = np.arange(P)[:, None], np.arange(T)[None, :]
    a["stickmask"] = np.concatenate([np.where(s_ < q_, 0, NEG), np.where(s_ < q_[:, :P], 0, NEG)], axis=1).astype(f)
    a["tri"] = (np.arange(P)[:, None] >= np.arange(P)[None, :]).astype(f)
    return {k: np.ascontiguousarray(v) for k, v in a.items()}


def kernel(**inputs):
    import concourse.bacc as bacc
    from concourse.bass_utils import run_bass_kernel_spmd

    arrays = _layout(inputs)
    nc = bacc.Bacc("TRN2", target_bir_lowering=False, num_devices=1)
    f32 = mybir.dt.float32
    a = {k: nc.dram_tensor(f"in_{k}", v.shape, f32, kind="ExternalInput").ap() for k, v in arrays.items()}
    scratch = nc.dram_tensor("bias_rows", (HEADS * P * 384,), f32, kind="Internal").ap()
    a["scratch"] = scratch.rearrange("(h p m) -> h p m", h=HEADS, p=P)
    a["scratch_toeplitz"] = bass.AP(tensor=scratch.tensor, offset=P - 1, ap=[[383, P], [P * 384, HEADS], [1, T]])
    out = nc.dram_tensor("out_x", (KT, P, T), f32, kind="ExternalOutput").ap()
    program(nc, a, out)
    r = run_bass_kernel_spmd(nc, [{f"in_{k}": v for k, v in arrays.items()}], core_ids=[0])
    return r.results[0]["out_x"].reshape(D, T).T.reshape(1, T, D)
```

```python
import math
from contextlib import ExitStack

import numpy as np

import concourse.bass as bass
from concourse import mybir

P = 128
D = 1024
T = 256
KT = D // P
TT = T // P
FF = 2816
STEPS = FF // (2 * P)
GROUPS, GDIM, STATE = 64, 16, 64
PAIRS = GROUPS // 2
HEADS, HD = 8, 64
SEL = 64
STICKS = 16
EPS = 1e-6
NEG = -1e30
TAKEN = -3e38
ROUND = 1.5 * 2.0 ** 23
LAM_INIT = 0.8 - 0.6 * math.exp(-0.3)
TWO_PI = 6.2831850

RING = 6
SPLIT = 3
STAGES = [("w_in", 4), ("glu", 8), ("ffn0", 3 * STEPS), ("ple0", 5), ("kvq", 12), ("wo", 4),
          ("ffn1", 3 * STEPS), ("ple1", 5), ("evin", 7), ("evout", 4), ("ffn2", 3 * STEPS),
          ("qkv", 12), ("out", 4), ("ffn3", 3 * STEPS)]
START, BANK, N_SLOTS, _u = {}, {}, 0, 0
for _name, _n in STAGES:
    START[_name], BANK[_name] = N_SLOTS, _u
    N_SLOTS += _n
    _u += {"ffn": 2 * STEPS, "ple": 4}.get(_name[:3], _n)

UNITS = ["ssm", "s5", "ffn0", "ple0", "kv", "q", "diff", "ffn1", "ple1", "even", "mixed", "ffn2",
         "odd", "stick", "ffn3"]
UNIT = {n: i for i, n in enumerate(UNITS)}
SET = dict(ssm=2, s5=1, ffn0=0, ple0=0, kv=1, q=0, diff=1, ffn1=0, ple1=0, even=1, mixed=1,
           ffn2=0, odd=0, stick=1, ffn3=0)
GAINS = ["ssm", "ffn0", "ple0", "kv", "q", "ffn1", "ple1", "even", "ffn2", "odd", "ffn3"]
GAIN = {n: i for i, n in enumerate(GAINS)}

COLS, _c = {}, 0
for _name, _n in [("gain", len(GAINS) * KT), ("conv", 2 * 22 * 8), ("dskip", KT), ("qk", 2),
                  ("subln", 1), ("evqk", 2), ("lam", 4), ("pscale", 4), ("ones", P),
                  ("ident", P)]:
    COLS[_name] = (_c, _c + _n)
    _c += _n
N_COLS = _c
MIX = 15264


class Count:

    def __init__(self, sem):
        self.sem, self.n, self.i, self.per = sem, 0, None, 0

    def value(self):
        return self.n if self.i is None else self.i * self.per + self.n

    def enter(self, i, per):
        self.i, self.per, self.base = i, per, self.n

    def leave(self, turns):
        assert self.n - self.base == self.per, (self.n - self.base, self.per)
        self.n, self.i = self.base + self.per * turns, None


class Counts:

    def __init__(self, eng, sems):
        self.eng, self.sems, self.c = eng, sems, {}

    def of(self, name):
        if name not in self.c:
            self.c[name] = Count(self.sems(name))
        return self.c[name]

    def up(self, ins, name):
        c = self.of(name)
        c.n += 1
        ins.then_inc(c.sem, 1)

    def up_and_wait(self, ins, name):
        self.up(ins, name)
        self.eng.wait_ge(self.of(name).sem, self.of(name).value())

    def tell(self, name):
        c = self.of(name)
        c.n += 1
        self.eng.sem_inc(c.sem, 1)

    def wait(self, name, k=1):
        c = self.of(name)
        c.n += k
        self.eng.wait_ge(c.sem, c.value())

    def enter(self, i, **per):
        for name, k in per.items():
            self.of(name).enter(i, k)
        self.looped = list(per)

    def leave(self, turns):
        for name in self.looped:
            self.of(name).leave(turns)


def program(nc, a, out):
    f32, f32r = mybir.dt.float32, mybir.dt.float32r
    ALU, ACT, AX = mybir.AluOpType, mybir.ActivationFunctionType, mybir.AxisListType
    ctx = ExitStack()
    with ctx:
        def sb(name, shape, dt=f32):
            return ctx.enter_context(nc.sbuf_tensor(name, shape, dt))

        ring = sb("ring", [P, RING, 2048])
        w_hi = sb("w_hi", [P, SPLIT, 2048], f32r)
        w_lo = sb("w_lo", [P, SPLIT, 2048], f32r)
        x = sb("x", [P, KT, T])
        sq = sb("sq", [P, KT, T])
        par = sb("par", [P, N_COLS])
        rstd = sb("rstd", [P, T])
        tok = sb("tok", [P, 4])
        little = sb("little", [P, 8])
        mix = sb("mix", [P, MIX])
        with nc.sbuf_tensor("opnd_first", [P, 2, KT, T], f32r) as opnd_first:
            pass
        with nc.sbuf_tensor("s5_area", [P, 2, 2 * KT, T], f32) as s5_area:
            pass
        opnd = [sb(f"opnd{i}", [P, 2, KT, T], f32r) for i in range(2)] + [opnd_first]
        acc = ctx.enter_context(nc.psum_tensor("acc", [P, 4, 512], f32))
        up = [ctx.enter_context(nc.psum_tensor(f"up{i}", [P, 2, T], f32)) for i in range(2)]
        aux = [ctx.enter_context(nc.psum_tensor(f"aux{i}", [P, 512], f32)) for i in range(2)]

        eps, neg_lam, sub_g, lam_e = little[:, 0:1], little[:, 1:2], little[:, 2:3], little[:, 3:5]

        def pcol(name, lo=0, n=None):
            s, e = COLS[name]
            return par[:, s + lo:(s + lo + n) if n else e]

        ident, ones = pcol("ident"), pcol("ones")

        def gain(name, m):
            return pcol("gain", GAIN[name] * KT + m, 1)

        sems = {}

        def sem(name):
            if name not in sems:
                sems[name] = ctx.enter_context(nc.semaphore(name))
            return sems[name]

        ring_full = [sem(f"ring_full{i}") for i in range(RING)]
        DMAS = ["par", "x", "s5_par", "s5_mat", "s5_c", "s5_t", "pe0", "pe1", "bias_oh", "bias_w",
                "bias_r", "halves", "causal", "stickmask", "outd"]
        dma = {n: sem(f"dma_{n}") for n in DMAS}

        def carve(*sizes):
            at, views = 0, []
            for shape in sizes:
                n = int(np.prod(shape))
                v = mix[:, at:at + n]
                if len(shape) == 2:
                    v = v.rearrange("p (a b) -> p a b", a=shape[0])
                if len(shape) == 3:
                    v = v.rearrange("p (a b c) -> p a b c", a=shape[0], b=shape[1])
                views.append(v)
                at += n
            assert at <= MIX, at
            return views

        (s_cs, s_sn, s_p, s_c, s_b, s_y, s_tmat, s_prep, s_mag, s_phi, s_e, s_t, s_init) = carve(
            (PAIRS, P), (PAIRS, P), (2, 2, 2 * T), (2, PAIRS, 32), (2, KT, P), (2, T), (P,), (3, PAIRS), (PAIRS,),
            (PAIRS,), (3, PAIRS), (2, 2, 2), (2, 2))
        s_p = s_p.rearrange("p a e (k t) -> p a e k t", k=2)
        s_work = s_y.rearrange("p a (b c) -> p (a b) c", c=PAIRS)
        s_m = s5_area[:, 0].rearrange("p k t -> p (k t)").rearrange(
            "p (m e k t) -> p m e k t", m=4, e=2, k=2)
        s_raw = s5_area[:, 1].rearrange("p k t -> p (k t)").rearrange(
            "p (a b c) -> p a b c", a=4, b=PAIRS)
        (f_u, f_c, f_gg, f_h, f_pe) = carve((4, 258), (4, T), (2, T), (2, T), (4, T))
        (d_k, d_q, d_v, d_bias, d_tmp, d_sq, d_l, d_a, d_at, d_st, d_half) = carve(
            (KT, T), (KT, T), (TT, D), (HEADS, T), (3, 2 * T), (2, 2 * T), (2, 2 * T), (2, T),
            (2, 2 * T), (64,), (P,))
        d_oh = mix[0:33, 0:384 + HEADS]
        (e_v, e_k, e_q, e_pl, e_tmp, e_sq, e_l, e_a, e_at, e_mask, e_causal, e_w, e_rel, e_st, e_m8,
         e_out, e_cnt, e_pw, e_half, e_u, e_pa) = carve(
            (TT, P), (T,), (4, T), (3, T), (3, 2 * T), (2, 2 * T), (2, 2 * T), (2, 2 * T), (4, 2 * T),
            (2, T), (2, T), (TT, 4), (T,), (64,), (8,), (2, T), (4, T), (4, P), (P,),
            (4, 16 + T), (4, 16 + T))
        e_pb = e_tmp.rearrange("p a b -> p (a b)")[:, 0:4 * (16 + T)].rearrange("p (a b) -> p a b", a=4)
        (k_k, k_q, k_v, k_mask, k_tri, k_z, k_t, k_b, k_a, k_out) = carve(
            (KT, T), (KT, T), (TT, D), (384,), (P,), (4, 384), (2, 384), (2, 384), (2, 384), (2, T))

        b_hi, b_lo = (v[:, START["w_in"] + 2].rearrange("p (r m c) -> p r m c", r=2, m=KT) for v in (w_hi, w_lo))

        def by_chunk(v):
            return v.rearrange("p e k (c t) -> p e (k c) t", c=2)

        def chunks(v):
            return v.rearrange("p e (c t) -> p e c t", c=2)

        def local(table, n, k):
            return table[:, 2 * n:2 * n + 2].unsqueeze(2).broadcast_to([P, 2, k, P])

        def hi(name):
            return opnd[SET[name]][:, 0]

        def lo(name):
            return opnd[SET[name]][:, 1]

        block = ctx.enter_context(nc.Block())

        @block.sync
        def _(sp):
            def load(r, slot):
                sp.dma_start(ring[:, r], a["stream"][slot].rearrange("a p n -> (a p) n")).then_inc(ring_full[r], 16)

            sp.dma_start(par[:], a["par"]).then_inc(dma["par"], 16)
            sp.dma_start(x[:], a["x"]).then_inc(dma["x"], 16)
            for s in range(RING):
                load(s, slice(s, s + 1))
            turns = N_SLOTS // RING - 1
            with sp.Fori(0, turns) as i:
                for r in range(RING):
                    sp.wait_ge(sem("w_ready"), i * RING + (r + 1))
                    load(r, bass.ds(i * RING + (RING + r), 1))
            for s in range(RING * (turns + 1), N_SLOTS):
                sp.wait_ge(sem("w_ready"), s - RING + 1)
                load(s % RING, slice(s, s + 1))
            c = Counts(sp, sem)
            for m in range(KT):
                c.wait("x_ready", 8 * 9 + 1 if m == 0 else 1)
                sp.dma_start(out[m], x[:, m]).then_inc(dma["outd"], 16)
            sp.wait_ge(dma["outd"], 16 * KT)

        @block.gpsimd
        def _(pool):
            c = Counts(pool, sem)

            def low_part(s, k=0):
                c.wait("w_hi_ready")
                r, b = (s + k) % RING, (s + k) % SPLIT
                c.up(nc.gpsimd.tensor_tensor(w_lo[:, b], ring[:, r], w_hi[:, b].bitcast(f32), ALU.subtract),
                     "w_ready")

            c.wait("w_hi_ready")
            c.wait("w_ready")
            for s in range(1, START["glu"]):
                low_part(s)

            def sums(n):
                m, r = s_m[:, n % 3], s_m[:, 3]
                c.wait("s5_prod", 2)
                c.up(nc.gpsimd.tensor_tensor(m[:, :, 1], r[:, :, 0], m[:, :, 1], ALU.subtract), "s5_sum")
                c.up(nc.gpsimd.tensor_tensor(m[:, :, 0], m[:, :, 0], r[:, :, 1], ALU.add), "s5_sum")

            def products(n):
                z = s_m[:, n % 3]
                c.wait("s5_scan")
                if n:
                    c.wait("s5_y_cos")
                c.up(nc.gpsimd.tensor_tensor(by_chunk(s_p[:, 0]), local(s_cs, n, 4), by_chunk(z), ALU.mult),
                     "s5_out_pool")

            for n in range(2 * KT + 1):
                if n < 2 * KT:
                    sums(n)
                if n == KT:
                    low_part(START["glu"])
                if n:
                    products(n - 1)
            for s in range(START["glu"] + 1, START["glu"] + SPLIT):
                low_part(s)

            def low_parts(first, end):
                turns = (end - first) // RING
                with pool.Fori(0, turns) as i:
                    c.enter(i, w_hi_ready=RING, w_ready=RING)
                    for k in range(RING):
                        low_part(first, k)
                    c.leave(turns)
                for s in range(first + turns * RING, end):
                    low_part(s)

            low_parts(START["glu"] + SPLIT, START["evout"] + SPLIT)
            c.wait("pool_in", 2)
            src, dst = e_u, e_pb
            for g in range(4):
                wdt = 2 ** g
                c.up_and_wait(nc.gpsimd.tensor_tensor(dst[:, g:, 16:], src[:, g:, 16:], src[:, g:, 16 - wdt:16 + T - wdt],
                                                      ALU.add), "pool_step")
                src, dst = dst, e_pa if g % 2 == 0 else e_pb
            pool.wait_ge(dma["causal"], 48)
            for g in range(4):
                c.up(nc.gpsimd.tensor_tensor(e_cnt[:, g], e_cnt[:, g], (e_pa if g % 2 else e_pb)[:, g, 16:], ALU.mult),
                     "pool_step")
            pool.wait_ge(sem("pool_step"), c.of("pool_step").value())
            c.up(nc.gpsimd.tensor_tensor(e_cnt, e_cnt, e_u[:, :, 16:], ALU.subtract), "pooled")
            low_parts(START["evout"] + SPLIT, N_SLOTS)

        @block.scalar
        def _(act):
            c = Counts(act, sem)
            A = nc.scalar.activation
            ahead = [0]

            def high_part(s, i=None):
                dyn = 0 if i is None else i
                act.wait_ge(ring_full[s % RING], dyn * 16 + 16 * (s // RING + 1))
                if s >= SPLIT:
                    act.wait_ge(sem("mm_done"), dyn * RING + (s - SPLIT + 1))
                c.up(A(w_hi[:, s % SPLIT], ring[:, s % RING], ACT.Copy), "w_hi_ready")

            def high_parts_to(s):
                while ahead[0] <= min(s, N_SLOTS - 1):
                    high_part(ahead[0])
                    ahead[0] += 1

            def new_operand(name, squares=True):
                for m in range(KT):
                    if squares:
                        c.up(A(sq[:, m], x[:, m], ACT.Square), "sq_ready")
                    c.up(A(hi(name)[:, m], x[:, m], ACT.Copy, scale=gain(name, m)), "hi_ready")

            def from_psum(name, m, src, buf, scale=1.0):
                b = buf[:, m % 2]
                if m >= 2:
                    act.wait_ge(sem("lo_ready"), KT * UNIT[name] + m - 1)
                c.up_and_wait(A(b, src, ACT.Copy, scale=scale), "act_step")
                c.up(A(hi(name)[:, m], b, ACT.Copy), "hi_ready")

            def rms(tokens=False):
                nc.scalar.preload_act_table_set("natural_log_exp_and_others")
                c.wait("ssq")
                c.up_and_wait(A(rstd[:], aux[1][:, 0:T], ACT.Ln, scale=1.0 / D, bias=eps), "act_step")
                c.up(A(rstd[:], rstd[:], ACT.Exp, scale=-0.5), "rstd")
                if tokens:
                    c.up_and_wait(A(tok[:, 2:4], aux[0][:, 0:2], ACT.Ln, scale=1.0 / D, bias=eps), "act_step")
                    c.up(A(tok[:, 2:4], tok[:, 2:4], ACT.Exp, scale=-0.5), "rstd_tok")

            act.dma_start(s_prep, a["s5_par"]).then_inc(dma["s5_par"], 16)
            act.dma_start(s_tmat, a["tmat"]).then_inc(dma["s5_t"], 16)
            act.wait_ge(dma["s5_par"], 16)
            w = s_work
            c.up(A(w[:, 0], s_prep[:, 2], ACT.Exp), "dt")
            c.wait("s5_mu")
            c.up(A(s_mag, w[:, 1], ACT.Exp), "mag")
            act.wait_ge(dma["par"], 16)
            act.wait_ge(dma["x"], 16)
            for m in range(KT):
                c.up(A(hi("ssm")[:, m], x[:, m], ACT.Copy, scale=gain("ssm", m)), "hi_ready")
            high_parts_to(1)
            for m in range(KT):
                c.up(A(sq[:, m], x[:, m], ACT.Square), "sq_ready")
            act.dma_start(s_raw[:, 0:2, :, :], a["s5_c"]).then_inc(dma["s5_c"], 16)
            act.dma_start(s_b, a["s5_b"]).then_inc(dma["s5_mat"], 16)
            c.wait("lam_sum")
            c.up(A(lam_e, aux[1][:, 0:2], ACT.Exp), "lam_exp")
            high_parts_to(2)
            c.wait("s5_turn")
            c.up(A(w[:, 4], s_phi, ACT.Sin, scale=TWO_PI), "s5_sc")
            c.up(A(w[:, 5], s_phi, ACT.Sin, scale=TWO_PI / 2), "s5_sc")
            c.up(A(s_e[:, 2], w[:, 12], ACT.Sin, scale=TWO_PI), "s5_sc")
            c.up(A(w[:, 13], w[:, 12], ACT.Sin, scale=TWO_PI / 2), "s5_sc")

            def s5_tables(g):
                q = slice(8 * g, 8 * g + 8)
                c.wait("s5_frac")
                c.up_and_wait(A(s_cs[:, q], s_sn[:, q], ACT.Sin, scale=TWO_PI / 2), "s5_sin")
                c.up(A(s_sn[:, q], s_sn[:, q], ACT.Sin, scale=TWO_PI), "s5_sin")
                c.up(A(s_cs[:, q], s_cs[:, q], ACT.Square), "s5_half")

            s5_tables(0)
            c.wait("eps")
            rms()
            high_parts_to(3)
            for g in range(1, 4):
                s5_tables(g)

            act.wait_ge(dma["s5_mat"], 16)
            act.wait_ge(sem("mm_done"), 3)
            c.up(A(b_hi, s_b, ACT.Copy), "b_hi")
            c.wait("s5_c_ready")
            for m in range(KT):
                act.wait_ge(sem("up_free"), m // 2 + 1)
                c.up(A(hi("s5")[:, m], sq[:, m], ACT.Copy), "u_hi")

            high_parts_to(START["glu"])
            for m in range(KT):
                if m == KT - 1:
                    act.wait_ge(sem("s5_bu"), 2 * KT)
                    high_parts_to(START["glu"] + SPLIT - 1)
                c.wait("s5_ysum")
                c.up_and_wait(A(s_y[:, 1], s_y[:, 0], ACT.Gelu_apprx_tanh), "act_step")
                c.up(A(hi("s5")[:, m], s_y[:, 1], ACT.Copy), "hi_ready")

            def operand_tile(name, m):
                c.wait("x_ready")
                c.up(A(sq[:, m], x[:, m], ACT.Square), "sq_ready")
                c.up(A(hi(name)[:, m], x[:, m], ACT.Copy, scale=gain(name, m)), "hi_ready")

            for m in range(KT):
                s = START["glu"] + m
                high_parts_to(s + 2)
                act.wait_ge(sem("mm_done"), s + 1)
                c.up(A(f_gg[:, 0], up[m % 2][:, 1], ACT.Sigmoid), "gated")
                operand_tile("ffn0", m)

            def ffn(l, end):
                S = START[f"ffn{l}"]

                def gate():
                    c.wait("g_ready")
                    if l < 2:
                        c.up(A(f_gg[:, 0], f_c[:, 0], ACT.Gelu_apprx_tanh), "gated")
                    else:
                        c.up(A(f_gg[:, 0], f_u[:, 0, 2:258], ACT.Silu), "gated")

                high_parts_to(S + 2)
                rms()
                for s in range(S, S + 8):
                    high_parts_to(s + 2)
                    if s - S not in (4, 7):
                        gate()
                assert ahead[0] == S + 10
                turns = 4 if end else 3
                with act.Fori(0, turns) as i:
                    c.enter(i, g_ready=4, gated=4, w_hi_ready=6)
                    for k in range(6):
                        high_part(S + 10 + k, i)
                        if k % 3 != 2:
                            gate()
                    c.leave(turns)
                ahead[0] = S + 10 + 6 * turns
                for k in range(6 * turns, 24):
                    high_parts_to(S + 10 + k)
                    if k % 3 != 2:
                        gate()
                if end:
                    for m in range(KT):
                        operand_tile(end, m)

            def pe_operand(l):
                act.wait_ge(dma[f"pe{l}"], 16)
                for k in range(2):
                    c.up(A(opnd[1][:, 0, 6 + k], f_pe[:, k], ACT.Copy), "pe_hi")

            def ple(l, ends):
                S = START[f"ple{l}"]
                high_parts_to(S + 2)
                rms()
                for g in range(4):
                    high_parts_to(S + g + 4)
                    c.wait("ple_u")
                    c.up(A(f_c[:, 2 * (g % 2):2 * (g % 2) + 2], f_u[:, 2 * (g % 2):2 * (g % 2) + 2, 2:258],
                           ACT.Sigmoid), "gated")
                    for m in (2 * g, 2 * g + 1):
                        operand_tile(ends[0], m)
                for name in ends[1:]:
                    new_operand(name, squares=False)

            def residual(name, S):
                for m in range(KT):
                    high_parts_to(S + m // 2 + 2)
                    operand_tile(name, m)

            def head_norms(n, count, raw, sqb, first):
                if n < count:
                    if n >= 2:
                        act.wait_ge(sem("qk_ready"), first + n - 1)
                    c.wait("hn_raw")
                    c.up(A(sqb[:, n % 2], raw[:, n % 3], ACT.Square), "hn_sq")
                if 1 <= n <= count:
                    b = sqb[:, (n - 1) % 2]
                    c.wait("hn_ssq")
                    c.up_and_wait(A(b, acc[:, (n - 1) % 2], ACT.Ln, scale=1.0 / HD, bias=eps), "hn_ln")
                    c.up(A(b, b, ACT.Exp, scale=-0.5), "hn_rstd")

            def softmax_exp(n, lbuf, st):
                nk = P * (n % 2 + 1)
                c.wait("neg_max")
                b = n % 2
                for e in range(2):
                    L = lbuf[:, b].rearrange("p (c k) -> p c k", c=2)[:, e, 0:nk]
                    c.up(A(L, L, ACT.Exp, bias=st[:, 40 + 2 * b + e:41 + 2 * b + e],
                           accum_out=st[:, 44 + 2 * b + e:45 + 2 * b + e]), "exps")

            def attn_copy(n, at, per):
                nk = n % 2 + 1
                c.wait("at_ps")
                src = up[n % 2][:].rearrange("p a t -> p (a t)").rearrange("p (j k q) -> p j k q", j=per, k=4 // per)
                for j in range(per):
                    t = (n // 2) % 2
                    dst = at[:, per * t + j].rearrange("p (k q) -> p k q", k=2)[:, 0:nk, (n % 2) * P:(n % 2) * P + P]
                    c.up(A(dst, src[:, j, 0:nk], ACT.Copy), "at_sb")

            act.dma_start(f_pe[:, 0:2], a["p0"]).then_inc(dma["pe0"], 16)
            pe_operand(0)
            ffn(0, "ple0")
            ple(0, ["kv", "q"])

            S = START["kvq"]
            high_parts_to(S + 2)
            c.wait("mix_free")
            act.dma_start(d_oh, a["bias_oh"]).then_inc(dma["bias_oh"], 16)
            act.dma_start(d_half, a["halves"]).then_inc(dma["halves"], 16)
            c.wait("bias_sb")
            act.dma_start(a["scratch"], d_sq[0:HEADS, 0, 0:384].unsqueeze(1).broadcast_to([HEADS, P, 384])).then_inc(dma["bias_w"], 16)
            rms(True)
            act.wait_ge(dma["bias_w"], 16)
            act.dma_start(d_bias, a["scratch_toeplitz"]).then_inc(dma["bias_r"], 16)
            for n in range(8 + 1):
                high_parts_to(S + 4 + n + 2)
                head_norms(n, 8, d_tmp, d_sq, 0)
            high_parts_to(S + 14)
            for n in range(2 * HEADS + 7):
                if n < 2 * HEADS:
                    softmax_exp(n, d_l, d_st)
                if 3 <= n < 2 * HEADS + 3:
                    attn_copy(n - 3, d_at, 1)
                if n % 2 and 5 <= n < 2 * HEADS + 5:
                    h = (n - 5) // 2
                    c.wait("pv")
                    c.up(A(sq[:, h], aux[h % 2][:, 0:T], ACT.Copy), "o_raw")
                    c.up(A(d_q[:, h], aux[h % 2][:, 0:T], ACT.Square), "o_sq")
                if n % 2 and n >= 7:
                    h = (n - 7) // 2
                    c.wait("o_ssq")
                    c.up_and_wait(A(d_q[:, h], aux[h % 2][:, T:2 * T], ACT.Ln, scale=1.0 / P, bias=eps), "o_ln")
                    c.up(A(d_q[:, h], d_q[:, h], ACT.Exp, scale=-0.5), "o_rstd")
                if n % 2 == 0 and n >= 8:
                    c.wait("o_norm")
                    c.up(A(hi("diff")[:, n // 2 - 4], sq[:, n // 2 - 4], ACT.Copy, scale=sub_g), "hi_ready")
            residual("ffn1", START["wo"])

            act.dma_start(f_pe[:, 0:2], a["p1"]).then_inc(dma["pe1"], 16)
            pe_operand(1)
            ffn(1, "ple1")
            ple(1, ["even"])

            S = START["evin"]
            high_parts_to(S + 2)
            c.wait("mix_free")
            act.dma_start(e_causal, a["causal"]).then_inc(dma["causal"], 16)
            act.dma_start(e_cnt, a["count"]).then_inc(dma["causal"], 16)
            act.dma_start(e_pw, a["pool_w"]).then_inc(dma["causal"], 16)
            act.dma_start(e_half, a["halves"]).then_inc(dma["halves"], 16)
            rms(True)
            for n in range(3 + 1):
                high_parts_to(S + 1 + n + 2)
                head_norms(n, 3, e_tmp, e_sq, 8)
            high_parts_to(S + 9)
            for n in range(8 + 5):
                if n < 8:
                    softmax_exp(n, e_l, e_st)
                if 3 <= n < 11:
                    attn_copy(n - 3, e_at, 2)
                if n >= 6 and n % 2 == 0:
                    c.wait("pv")
                    h = n // 2 - 3
                    from_psum("mixed", h, aux[h % 2][:, 0:T], e_out)
            for m in range(4):
                c.wait("pool_ps")
                from_psum("mixed", 4 + m, acc[:, m, 0:T], e_out, pcol("pscale", m, 1))
            residual("ffn2", START["evout"])

            ffn(2, "odd")

            S = START["qkv"]
            high_parts_to(S + 2)
            c.wait("mix_free")
            act.dma_start(k_mask, a["stickmask"]).then_inc(dma["stickmask"], 16)
            act.dma_start(k_tri, a["tri"]).then_inc(dma["stickmask"], 16)
            rms(True)
            for s in range(S, S + 12):
                high_parts_to(s + 2)
            high_parts_to(S + 14)
            nc.scalar.preload_act_table_set("natural_log_exp_and_others")
            for n in range(STICKS + 5):
                if n < STICKS:
                    c.wait("z_sb")
                    t = k_t[:, n % 2]
                    c.up_and_wait(A(t, k_z[:, n % 4], ACT.Abs), "act_step")
                    c.up_and_wait(A(t, t, ACT.Exp, scale=-1.0), "act_step")
                    c.up(A(t, t, ACT.Ln, bias=1.0), "log1p")
                if 3 <= n < STICKS + 3:
                    h = n - 3
                    c.wait("log_a")
                    if h >= 2:
                        c.wait("stick_pv")
                    c.up(A(k_a[:, h % 2], k_z[:, h % 4], ACT.Exp), "a_sb")
                if n >= 6 and n % 2 == 0:
                    m = n // 2 - 3
                    act.wait_ge(sem("stick_pv"), 2 * m + 2)
                    from_psum("stick", m, aux[m % 2][:, 0:T], k_out)
            residual("ffn3", START["out"])
            ffn(3, None)

        @block.vector
        def _(dve):
            c = Counts(dve, sem)
            V = nc.vector

            def step(ins):
                c.up_and_wait(ins, "dve_step")

            def low_tile(name, m, squares=True):
                c.wait("hi_ready")
                c.up(V.scalar_tensor_tensor(lo(name)[:, m], x[:, m], gain(name, m), hi(name)[:, m].bitcast(f32),
                                            ALU.mult, ALU.subtract), "lo_ready")
                if squares:
                    add_square(m)

            def low_of(name, m, buf):
                c.wait("hi_ready")
                c.up(V.tensor_tensor(lo(name)[:, m], buf[:, m % 2], hi(name)[:, m].bitcast(f32), ALU.subtract),
                     "lo_ready")

            def add_square(m):
                c.wait("sq_ready")
                if m > 1:
                    dve.wait_ge(sem("sq_sum"), c.of("sq_sum").value())
                if m:
                    c.up(V.tensor_tensor(sq[:, 0], sq[:, 0], sq[:, m], ALU.add), "sq_sum")

            def over_rms(dst, u):
                c.up_and_wait(V.tensor_tensor(dst, up[u][:], rstd[:].unsqueeze(1).broadcast_to([P, 2, T]), ALU.mult),
                              "up_free")

            c.up(V.memset(eps, EPS), "eps")
            w = s_work
            lr, li = s_prep[:, 0], s_prep[:, 1]

            def less_whole_turns(dst, src, tmp):
                step(V.tensor_scalar(tmp, src, ROUND, -ROUND, ALU.add, ALU.add))
                step(V.tensor_tensor(dst, src, tmp, ALU.subtract))

            dve.wait_ge(dma["s5_par"], 16)
            c.wait("dt")
            c.up_and_wait(V.tensor_tensor(w[:, 1], lr, w[:, 0], ALU.mult), "s5_mu")
            step(V.tensor_tensor(w[:, 2], li, w[:, 0], ALU.mult))
            step(V.tensor_scalar(w[:, 2], w[:, 2], 1.0 / (2.0 * math.pi), None, ALU.mult))
            less_whole_turns(s_phi, w[:, 2], w[:, 3])
            step(V.tensor_scalar(w[:, 12], s_phi, float(P), None, ALU.mult))
            less_whole_turns(w[:, 12], w[:, 12], w[:, 3])
            c.tell("s5_turn")
            dve.wait_ge(dma["par"], 16)
            step(V.tensor_tensor(tok[:, 0:2], pcol("lam")[:, 0:2], pcol("lam")[:, 2:4], ALU.mult))
            c.up(V.tensor_scalar(sub_g, pcol("subln"), 1.0 - LAM_INIT, None, ALU.mult), "lam_prod")

            def s5_turns(g):
                q = slice(8 * g, 8 * g + 8)
                step(V.tensor_tensor(s_cs[:, q], s_tmat.unsqueeze(1).broadcast_to([P, 8, P]),
                                     s_phi[:, q].unsqueeze(2).broadcast_to([P, 8, P]), ALU.mult))
                less_whole_turns(s_sn[:, q], s_cs[:, q], s_sn[:, q])
                c.tell("s5_frac")

            def s5_cosines(g):
                q = slice(8 * g, 8 * g + 8)
                c.wait("s5_half")
                step(V.tensor_scalar(s_cs[:, q], s_cs[:, q], -2.0, 1.0, ALU.mult, ALU.add))
                c.tell("s5_tables")

            dve.wait_ge(dma["s5_t"], 16)
            s5_turns(0)
            dve.wait_ge(dma["x"], 16)
            for m in range(KT):
                low_tile("ssm", m, squares=False)
            c.wait("w_hi_ready")
            c.up(V.tensor_tensor(w_lo[:, 0], ring[:, 0], w_hi[:, 0].bitcast(f32), ALU.subtract), "w_ready")
            for m in range(KT):
                add_square(m)
            s5_turns(1)
            c.wait("lam_exp")
            step(V.tensor_tensor(neg_lam, little[:, 4:5], little[:, 3:4], ALU.subtract))
            step(V.tensor_scalar(neg_lam, neg_lam, -LAM_INIT, None, ALU.add))
            s5_turns(2)
            s5_turns(3)
            c.wait("rstd")
            for s in range(4):
                if s == 2:
                    c.wait("mag")
                    c.wait("s5_sc", 4)
                    step(V.tensor_tensor(w[:, 6], w[:, 5], w[:, 5], ALU.mult))
                    step(V.tensor_scalar(w[:, 6], w[:, 6], -2.0, 1.0, ALU.mult, ALU.add))
                    step(V.tensor_tensor(w[:, 6], w[:, 6], s_mag, ALU.mult))
                    step(V.tensor_scalar(w[:, 6], w[:, 6], -1.0, None, ALU.add))
                    step(V.tensor_tensor(w[:, 7], w[:, 4], s_mag, ALU.mult))
                    step(V.tensor_tensor(w[:, 8], lr, lr, ALU.mult))
                    step(V.tensor_tensor(w[:, 9], li, li, ALU.mult))
                    step(V.tensor_tensor(w[:, 8], w[:, 8], w[:, 9], ALU.add))
                    step(V.reciprocal(w[:, 8], w[:, 8]))
                    step(V.tensor_tensor(w[:, 9], w[:, 6], lr, ALU.mult))
                    step(V.tensor_tensor(w[:, 10], w[:, 7], li, ALU.mult))
                    step(V.tensor_tensor(w[:, 9], w[:, 9], w[:, 10], ALU.add))
                    step(V.tensor_tensor(w[:, 9], w[:, 9], w[:, 8], ALU.mult))
                    step(V.tensor_tensor(w[:, 10], w[:, 7], lr, ALU.mult))
                    step(V.tensor_tensor(w[:, 11], w[:, 6], li, ALU.mult))
                    step(V.tensor_tensor(w[:, 10], w[:, 10], w[:, 11], ALU.subtract))
                    step(V.tensor_tensor(w[:, 10], w[:, 10], w[:, 8], ALU.mult))
                    step(V.tensor_tensor(w[:, 13], w[:, 13], w[:, 13], ALU.mult))
                    step(V.tensor_scalar(s_e[:, 0], w[:, 13], -2.0, 1.0, ALU.mult, ALU.add))
                    step(V.tensor_scalar(s_e[:, 1], s_e[:, 2], -1.0, None, ALU.mult))
                    dve.wait_ge(dma["s5_c"], 16)
                    cr, ci, t0, t1 = (s_raw[:, k] for k in range(4))
                    fr = w[:, 9].unsqueeze(2).broadcast_to([P, PAIRS, 32])
                    fi = w[:, 10].unsqueeze(2).broadcast_to([P, PAIRS, 32])
                    step(V.tensor_tensor(t0, cr, fr, ALU.mult))
                    step(V.tensor_tensor(t1, ci, fi, ALU.mult))
                    step(V.tensor_tensor(s_c[:, 0], t0, t1, ALU.subtract))
                    step(V.tensor_tensor(t0, cr, fi, ALU.mult))
                    step(V.tensor_tensor(t1, ci, fr, ALU.mult))
                    c.up_and_wait(V.tensor_tensor(s_c[:, 1], t0, t1, ALU.add), "s5_c_ready")
                dve.wait_ge(sem("mm_done"), START["w_in"] + s + 1)
                over_rms(sq[:, 2 * s:2 * s + 2], s % 2)
            c.wait("b_hi")
            c.up(V.tensor_tensor(b_lo, s_b, b_hi.bitcast(f32), ALU.subtract), "b_lo")
            for g in range(4):
                c.wait("u_hi", 2)
                q = slice(2 * g, 2 * g + 2)
                c.up(V.tensor_tensor(lo("s5")[:, q], sq[:, q], hi("s5")[:, q].bitcast(f32), ALU.subtract), "u_lo")
                s5_cosines(g)

            def s5_products(n):
                c.wait("s5_bu")
                if n:
                    c.wait("s5_sum", 2)
                if n >= 3:
                    c.wait("s5_out_pool")
                bu = acc[:, 2 * (n % 2):2 * (n % 2) + 2].rearrange("p e (k t) -> p e k t", t=P)
                c.up(V.tensor_tensor(by_chunk(s_m[:, n % 3]), local(s_cs, n, 4), bu, ALU.mult), "s5_prod")
                c.up(V.tensor_tensor(by_chunk(s_m[:, 3]), local(s_sn, n, 4), bu, ALU.mult), "s5_prod")

            def s5_scans(n):
                z = s_m[:, n % 3]

                def scans(chunk):
                    q = slice(chunk * P, chunk * P + P)
                    for e in range(2):
                        r = s_mag[:, 2 * n + e:2 * n + e + 1].broadcast_to([P, P])
                        for k in range(2):
                            ins = V.tensor_tensor_scan(z[:, e, k, q], r, z[:, e, k, q],
                                                       s_init[:, e, k:k + 1] if chunk else 0.0, ALU.mult, ALU.add)
                            c.up(ins, "s5_scanned")
                    dve.wait_ge(sem("s5_scanned"), c.of("s5_scanned").value())

                scans(0)
                end = z[:, :, :, P - 1]
                turn = s_e[:, :, 2 * n:2 * n + 2]
                c.up(V.tensor_tensor(s_t[:, 0], end, turn[:, 0].unsqueeze(2).broadcast_to([P, 2, 2]), ALU.mult), "dve_step")
                step(V.tensor_tensor(s_t[:, 1], end, turn[:, 1:3].rearrange("p k e -> p e k"), ALU.mult))
                c.up(V.tensor_tensor(s_init[:, :, 0], s_t[:, 0, :, 0], s_t[:, 1, :, 1], ALU.add), "dve_step")
                step(V.tensor_tensor(s_init[:, :, 1], s_t[:, 0, :, 1], s_t[:, 1, :, 0], ALU.add))
                scans(1)
                c.tell("s5_scan")

            def s5_back(n):
                if n:
                    c.wait("s5_y")
                for e in range(2):
                    c.up(V.scalar_tensor_tensor(chunks(s_p[:, 1, e, 0].unsqueeze(1))[:, 0],
                                                chunks(s_m[:, n % 3, e, 0].unsqueeze(1))[:, 0], -1.0,
                                                local(s_sn, n, 2)[:, e], ALU.mult, ALU.mult), "s5_out_dve")
                c.up(V.tensor_tensor(chunks(s_p[:, 1, :, 1]), local(s_sn, n, 2), chunks(s_m[:, n % 3, :, 1]), ALU.mult),
                     "s5_out_dve")

            def s5_output(m):
                dve.wait_ge(sem("s5_y"), 2 * m + 2)
                c.up_and_wait(V.scalar_tensor_tensor(s_y[:, 0], sq[:, m], pcol("dskip", m, 1), aux[m % 2][:, 0:T],
                                                     ALU.mult, ALU.add), "s5_ysum")

            def s5_low(m):
                c.wait("hi_ready")
                c.up(V.tensor_tensor(lo("s5")[:, m], s_y[:, 1], hi("s5")[:, m].bitcast(f32), ALU.subtract), "lo_ready")

            for n in range(2 * KT + 1):
                if n < 2 * KT:
                    s5_products(n)
                else:
                    c.wait("s5_sum", 2)
                if n:
                    s5_scans(n - 1)
                    s5_back(n - 1)
                if n >= 4 and n % 2 == 0:
                    s5_output(n // 2 - 2)
                if n >= 5 and n % 2:
                    s5_low(n // 2 - 2)
            s5_low(KT - 2)
            s5_output(KT - 1)
            s5_low(KT - 1)

            for m in range(KT):
                c.wait("gated")
                step(V.tensor_tensor(f_h[:, 0], up[m % 2][:, 0], f_gg[:, 0], ALU.mult))
                c.tell("up_free")
                c.up_and_wait(V.tensor_tensor(x[:, m], x[:, m], f_h[:, 0], ALU.add), "x_ready")
                if m:
                    low_tile("ffn0", m - 1)
            low_tile("ffn0", KT - 1)

            def ffn(l, end):
                S = START[f"ffn{l}"]
                conv = l < 2
                if conv:
                    for t in range(2):
                        step(V.memset(f_u[:, t, 0:2], 0.0))
                c.wait("rstd")

                def tile(s, k, u, i, n, parity, part):
                    dve.wait_ge(sem("mm_done"), s + k + 1 if i is None else i * 6 + (s + k + 1))
                    us = f_u[:, 0:2, 2:258]
                    if conv:
                        over_rms(us, u)
                        for t in range(2):
                            base = COLS["conv"][0] + (l * 22 * 8)
                            pr = par[:, base:base + 176].rearrange("p (n w) -> p n w", w=8)
                            if i is None:
                                w4 = [pr[:, n, 4 * t + q:4 * t + q + 1] for q in range(4)]
                            else:
                                w4 = [pr[:, bass.ds(i * 4 + n, 1), 4 * t + q:4 * t + q + 1].rearrange("p a b -> p (a b)")
                                      for q in range(4)]
                            step(V.tensor_scalar(f_c[:, t], f_u[:, t, 2:258], w4[2], w4[3], ALU.mult, ALU.add))
                            step(V.scalar_tensor_tensor(f_c[:, t], f_u[:, t, 1:257], w4[1], f_c[:, t], ALU.mult, ALU.add))
                            ins = V.scalar_tensor_tensor(f_c[:, t], f_u[:, t, 0:256], w4[0], f_c[:, t], ALU.mult, ALU.add)
                            if t == 0:
                                c.up_and_wait(ins, "g_ready")
                            else:
                                step(ins)
                        val = f_c[:, 1]
                    else:
                        over_rms(us, u)
                        c.tell("g_ready")
                        val = f_u[:, 1, 2:258]
                    c.wait("gated")
                    step(V.tensor_tensor(f_h[:, 0], f_gg[:, 0], val, ALU.mult))
                    hh, hl = opnd[1][:, 0, 2 * parity + part], opnd[1][:, 1, 2 * parity + part]
                    step(V.tensor_copy(hh, f_h[:, 0]))
                    c.up_and_wait(V.tensor_tensor(hl, f_h[:, 0], hh.bitcast(f32), ALU.subtract), "h_ready")

                up0 = BANK[f"ffn{l}"]
                for j in range(3):
                    for part in range(2):
                        s = S + part if j == 0 else S + 3 * j - 1 + part
                        tile(s, 0, (up0 + part) % 2, None, 2 * j + part, j % 2, part)
                with dve.Fori(0, 4) as i:
                    c.enter(i, **(dict(dve_step=28, up_free=4, g_ready=4, gated=4, h_ready=4) if conv
                                  else dict(dve_step=8, up_free=4, g_ready=4, gated=4, h_ready=4)))
                    for j in (3, 4):
                        for part in range(2):
                            tile(S + 8, 3 * (j - 3) + part, (up0 + part) % 2, i, 2 * j + part, j % 2, part)
                    c.leave(4)
                for m in range(KT):
                    if m % 2 == 0:
                        c.wait("acc_bank") if m < KT - 2 else dve.wait_ge(sem("mm_done"), S + 33)
                    c.up_and_wait(V.tensor_tensor(x[:, m], x[:, m], acc[:, m // 2, (m % 2) * T:(m % 2) * T + T],
                                                  ALU.add), "x_ready")
                    if m and end:
                        low_tile(end, m - 1)
                if end:
                    low_tile(end, KT - 1)

            def pe_operand():
                for k in range(2):
                    c.wait("pe_hi")
                    c.up(V.tensor_tensor(opnd[1][:, 1, 6 + k], f_pe[:, k], opnd[1][:, 0, 6 + k].bitcast(f32),
                                         ALU.subtract), "pe_ready")

            def ple(l, ends):
                S = START[f"ple{l}"]
                u0 = BANK[f"ple{l}"]
                c.wait("rstd")
                for g in range(4):
                    b = 2 * (g % 2)
                    dve.wait_ge(sem("mm_done"), S + (0 if g == 0 else g + 1) + 1)
                    over_rms(f_u[:, b:b + 2, 2:258], (u0 + g) % 2)
                    c.tell("ple_u")
                    if g == 0:
                        dve.wait_ge(sem("mm_done"), S + 2)
                    c.wait("gated")
                    step(V.tensor_tensor(f_c[:, b:b + 2], f_c[:, b:b + 2],
                                         acc[:, g].rearrange("p (a t) -> p a t", a=2), ALU.mult))
                    for e in range(2):
                        m = 2 * g + e
                        c.up_and_wait(V.tensor_tensor(x[:, m], x[:, m], f_c[:, b + e], ALU.add), "x_ready")
                        if m:
                            low_tile(ends[0], m - 1)
                low_tile(ends[0], KT - 1)
                c.tell("mix_free")
                for name in ends[1:]:
                    for m in range(KT):
                        low_tile(name, m, squares=False)

            def residual(name, S, u0):
                for g in range(4):
                    dve.wait_ge(sem("mm_done"), S + g + 1)
                    for e in range(2):
                        m = 2 * g + e
                        c.up_and_wait(V.tensor_tensor(x[:, m], x[:, m], up[(u0 + g) % 2][:, e], ALU.add), "x_ready")
                        if m:
                            low_tile(name, m - 1)
                    c.tell("up_free")
                low_tile(name, KT - 1)

            def values(s, u, dst, n):
                dve.wait_ge(sem("mm_done"), s + 1)
                for t in range(TT):
                    step(V.tensor_scalar(dst[:, t], up[u][:, t, 0:n], tok[:, 2 + t:3 + t], None, ALU.mult))

            def head_norm(n, count, S, u0, tmp, last):
                if n < count:
                    dve.wait_ge(sem("mm_done"), S + n + 1)
                    over_rms(tmp[:, n % 3].rearrange("p (a t) -> p a t", a=2), (u0 + n) % 2)
                    c.tell("hn_raw")
                if n >= 2:
                    c.wait("hn_rstd")
                    last(n - 2)

            def softmax_head(n, lbuf, st, bias):
                nk = P * (n % 2 + 1)
                b = n % 2
                L = lbuf[:, b].rearrange("p (c k) -> p c k", c=2)[:, :, 0:nk]
                c.wait("scores")
                S2 = acc[:, 2 * b:2 * b + 2, 0:nk]
                c.up_and_wait(V.scalar_tensor_tensor(L, S2, HD ** -0.5, bias.unsqueeze(1).broadcast_to([P, 2, nk]),
                                                     ALU.mult, ALU.add), "scores_read")
                c.up(V.tensor_reduce(st[:, 40 + 2 * b:42 + 2 * b], L, AX.X, ALU.max, negate=True), "neg_max")

            def softmax_tail(n, lbuf, abuf, st, diff):
                nk = P * (n % 2 + 1)
                b = n % 2
                L = lbuf[:, b].rearrange("p (c k) -> p c k", c=2)[:, :, 0:nk]
                c.wait("exps", 2)
                if n >= 2:
                    c.wait("at_ps")
                r = st[:, 48 + 2 * b:50 + 2 * b]
                step(V.reciprocal(r, st[:, 44 + 2 * b:46 + 2 * b]))
                if diff:
                    step(V.tensor_tensor(r[:, 1:2], r[:, 1:2], neg_lam, ALU.mult))
                    step(V.tensor_scalar(L[:, 1], L[:, 1], r[:, 1:2], None, ALU.mult))
                    c.up(V.scalar_tensor_tensor(abuf[:, b, 0:nk], L[:, 0], r[:, 0:1], L[:, 1], ALU.mult, ALU.add),
                         "probs")
                else:
                    ab = abuf[:, b].rearrange("p (c k) -> p c k", c=2)
                    step(V.tensor_scalar(ab[:, 0, 0:nk], L[:, 0], r[:, 0:1], None, ALU.mult))
                    c.up(V.tensor_scalar(ab[:, 1, 0:nk], L[:, 1], r[:, 1:2], None, ALU.mult), "probs")
                dve.wait_ge(sem("probs"), c.of("probs").value())

            pe_operand()
            ffn(0, "ple0")
            ple(0, ["kv", "q"])

            S, u0 = START["kvq"], BANK["kvq"]
            c.wait("bias_ps")
            c.up(V.tensor_copy(d_sq[0:HEADS, 0, 0:384], aux[0][0:HEADS, 0:384]), "bias_sb")
            c.wait("rstd_tok")
            for g in range(4):
                values(S + g, (u0 + g) % 2, d_v[:, :, g * 256:(g + 1) * 256], 256)
                c.tell("up_free")
            c.wait("rstd")

            def diff_normed(n):
                dst = (d_k if n % 2 == 0 else d_q)[:, 2 * (n // 2):2 * (n // 2) + 2]
                c.up_and_wait(V.scalar_tensor_tensor(dst, d_tmp[:, n % 3].rearrange("p (a t) -> p a t", a=2),
                                                     pcol("qk", n % 2, 1),
                                                     d_sq[:, n % 2].rearrange("p (a t) -> p a t", a=2),
                                                     ALU.mult, ALU.mult), "qk_ready")

            for n in range(8 + 2):
                head_norm(n, 8, S + 4, u0 + 4, d_tmp, diff_normed)
            dve.wait_ge(dma["bias_r"], 16)
            for n in range(2 * HEADS + 7):
                if n < 2 * HEADS:
                    h = n // 2
                    bias = d_bias[:, h, 0:T] if n % 2 else d_bias[:, h, P:T]
                    softmax_head(n, d_l, d_st, bias)
                if 1 <= n <= 2 * HEADS:
                    softmax_tail(n - 1, d_l, d_a, d_st, True)
                if n % 2 and n >= 7:
                    h = (n - 7) // 2
                    c.wait("o_raw")
                    c.wait("o_rstd")
                    c.up(V.tensor_tensor(sq[:, h], sq[:, h], d_q[:, h], ALU.mult), "o_norm")
                if n % 2 == 0 and n >= 8:
                    h = n // 2 - 4
                    dve.wait_ge(sem("o_norm"), h + 1)
                    c.wait("hi_ready")
                    c.up(V.scalar_tensor_tensor(lo("diff")[:, h], sq[:, h], sub_g, hi("diff")[:, h].bitcast(f32),
                                                ALU.mult, ALU.subtract), "lo_ready")
            c.wait("at_ps", 2)
            residual("ffn1", START["wo"], BANK["wo"])

            pe_operand()
            ffn(1, "ple1")
            ple(1, ["even"])

            S, u0 = START["evin"], BANK["evin"]
            c.wait("rstd_tok")
            dve.wait_ge(sem("mm_done"), S + 1)
            for t in range(TT):
                step(V.tensor_scalar(e_v[:, t], up[u0 % 2][:, t, 0:P], tok[:, 2 + t:3 + t], None, ALU.mult))
                step(V.tensor_scalar(e_w[:, t], up[u0 % 2][:, t, P:P + 4], tok[:, 2 + t:3 + t], 1.0 / 16,
                                     ALU.mult, ALU.mult))
            c.tell("up_free")
            c.wait("rstd")

            def even_normed(n):
                src = e_tmp[:, n % 3].rearrange("p (a t) -> p a t", a=2)
                bc = e_sq[:, n % 2].rearrange("p (a t) -> p a t", a=2)
                if n == 0:
                    step(V.tensor_copy(e_pl[:, 0], src[:, 1]))
                    c.up_and_wait(V.scalar_tensor_tensor(e_k, src[:, 0], pcol("evqk", 0, 1), bc[:, 0],
                                                         ALU.mult, ALU.mult), "qk_ready")
                else:
                    c.up_and_wait(V.scalar_tensor_tensor(e_q[:, 2 * n - 2:2 * n], src, pcol("evqk", 1, 1), bc,
                                                         ALU.mult, ALU.mult), "qk_ready")

            for n in range(3 + 2):
                head_norm(n, 3, S + 1, u0 + 1, e_tmp, even_normed)
            for b in (e_u, e_pa, e_pb):
                step(V.memset(b[:, :, 0:16], 0.0))
            dve.wait_ge(sem("mm_done"), S + 5)
            over_rms(e_pl[:, 1:3], (u0 + 4) % 2)
            c.tell("idx_ready")
            dve.wait_ge(dma["causal"], 48)
            for qb in range(2):
                nk = P * (qb + 1)
                sc = e_mask[:, qb, 0:nk]
                c.wait("idx_ps")
                step(V.tensor_copy(sc, e_causal[:, qb, 0:nk]))
                for h in range(4):
                    rel = acc[:, h, 0:nk]
                    step(V.tensor_scalar(e_rel[:, 0:nk], rel, 0.0, e_w[:, qb, h:h + 1], ALU.max, ALU.mult))
                    step(V.tensor_tensor(sc, sc, e_rel[:, 0:nk], ALU.add))
                c.tell("idx_read")
                dve.wait_ge(sem("mm_done"), S + 6 + qb)
                over_rms(e_u[:, 2 * qb:2 * qb + 2, 16:], (u0 + 5 + qb) % 2)
                c.tell("pool_in")
                for _ in range(SEL // 8):
                    step(V.max(e_m8, sc))
                    step(V.match_replace(sc, e_m8, sc, TAKEN))
                step(V.tensor_scalar(sc, sc, TAKEN / 2, NEG, ALU.is_gt, ALU.mult))
                step(V.tensor_tensor(sc, sc, e_causal[:, qb, 0:nk], ALU.add))
            for n in range(8 + 4):
                if n < 8:
                    softmax_head(n, e_l, e_st, e_mask[:, n % 2, 0:P * (n % 2 + 1)])
                if 1 <= n <= 8:
                    softmax_tail(n - 1, e_l, e_a, e_st, False)
                if n >= 7 and n % 2:
                    low_of("mixed", (n - 7) // 2, e_out)
            for m in range(3, KT):
                low_of("mixed", m, e_out)
            residual("ffn2", START["evout"], BANK["evout"])

            ffn(2, "odd")
            c.tell("mix_free")

            S, u0 = START["qkv"], BANK["qkv"]
            c.wait("rstd_tok")
            for g in range(4):
                values(S + g, (u0 + g) % 2, k_v[:, :, g * 256:(g + 1) * 256], 256)
                c.tell("up_free")
            c.wait("rstd")
            for n in range(8):
                dve.wait_ge(sem("mm_done"), S + 5 + n)
                dst = (k_k if n % 2 == 0 else k_q)[:, 2 * (n // 2):2 * (n // 2) + 2]
                over_rms(dst, (u0 + 4 + n) % 2)
                c.tell("stick_qk")
            dve.wait_ge(dma["stickmask"], 32)
            for n in range(STICKS + 3):
                if n < STICKS:
                    c.wait("z_ps")
                    if n >= 4:
                        c.wait("a_sb")
                    c.up(V.scalar_tensor_tensor(k_z[:, n % 4], acc[:, n % 2, 0:384], HD ** -0.5, k_mask,
                                                ALU.mult, ALU.add), "z_sb")
                if n >= 3:
                    h = n - 3
                    c.wait("remain")
                    c.up(V.tensor_tensor(k_z[:, h % 4], k_z[:, h % 4], acc[:, 2 + h % 2, 0:384], ALU.subtract),
                         "log_a")
                if 1 <= n <= STICKS:
                    c.wait("log1p")
                    h = n - 1
                    dve.wait_ge(sem("z_sb"), n)
                    c.up(V.scalar_tensor_tensor(k_b[:, h % 2], k_z[:, h % 4], 0.0, k_t[:, h % 2], ALU.max, ALU.add),
                         "brk")
                if n >= 7 and n % 2:
                    low_of("stick", (n - 7) // 2, k_out)
            low_of("stick", 6, k_out)
            low_of("stick", 7, k_out)
            residual("ffn3", START["out"], BANK["out"])
            ffn(3, None)

        @block.tensor
        def _(pe):
            c = Counts(pe, sem)
            MM = nc.tensor.matmul
            used = [0]

            def slot_ready(s, i=None):
                pe.wait_ge(sem("w_ready"), s + 1 if i is None else i * 6 + (s + 1))

            def bank(i=None, loop_uses=0):
                u = used[0]
                used[0] += 1
                if u >= 2:
                    pe.wait_ge(sem("up_free"), u - 1 if i is None else i * 4 + (u - 1))
                return up[u % 2]

            def three(o, l_hi, l_lo, r_hi, r_lo, start, stop):
                MM(o, l_hi, r_hi, start=start, stop=False, skip_group_check=True)
                MM(o, l_lo, r_hi, start=False, stop=False, skip_group_check=True)
                return MM(o, l_hi, r_lo, start=False, stop=stop, skip_group_check=True)

            def up_slot(name, s, i=None, fresh=False, tiles=2):
                slot_ready(s, i)
                o = bank(i)
                b = s % SPLIT
                for k in range(KT):
                    if fresh:
                        c.wait("hi_ready")
                        c.wait("lo_ready")
                    for m in range(tiles):
                        w = slice((2 * k + m) * P, (2 * k + m + 1) * P)
                        ins = three(o[:, m], w_hi[:, b, w], w_lo[:, b, w], hi(name)[:, k], lo(name)[:, k],
                                    k == 0 and m == 0, k == KT - 1)
                c.up(ins, "mm_done")

            def token_slot(name, s, fresh=False):
                slot_ready(s)
                o = bank()
                b = s % SPLIT
                for k in range(KT):
                    if fresh:
                        c.wait("hi_ready")
                        c.wait("lo_ready")
                    for t in range(TT):
                        w = slice(2 * k * P, (2 * k + 2) * P)
                        q = slice(t * P, (t + 1) * P)
                        ins = three(o[:, t], hi(name)[:, k, q], lo(name)[:, k, q], w_hi[:, b, w], w_lo[:, b, w],
                                    k == 0 and t == 0, k == KT - 1)
                c.up(ins, "mm_done")

            def down_slot(s, ops, first, last, i=None, each=False):
                slot_ready(s, i)
                b = s % SPLIT
                for m in range(KT):
                    for k in range(2):
                        w = slice((8 * k + m) * P, (8 * k + m + 1) * P)
                        ins = three(acc[:, m // 2, (m % 2) * T:(m % 2) * T + T], w_hi[:, b, w], w_lo[:, b, w],
                                    opnd[1][:, 0, ops + k], opnd[1][:, 1, ops + k],
                                    first and k == 0 and m % 2 == 0, last and k == 1)
                    if each and m % 2 and m < KT - 1:
                        c.up(ins, "acc_bank")
                return ins

            def rms(tokens=False):
                c.wait("sq_sum", KT - 1)
                ins = MM(aux[1][:, 0:T], ones, sq[:, 0], start=True, stop=True)
                if tokens:
                    for t in range(TT):
                        ins = MM(aux[0][:, t:t + 1], sq[:, 0, t * P:(t + 1) * P], ones[:, 0:1], start=True, stop=True)
                c.up(ins, "ssq")

            pe.wait_ge(dma["par"], 16)
            c.wait("lam_prod")
            c.up(MM(aux[1][:, 0:2], ones, tok[:, 0:2], start=True, stop=True), "lam_sum")

            S = START["w_in"]
            up_slot("ssm", S, fresh=True)
            c.wait("lam_exp")
            rms()
            up_slot("ssm", S + 1)
            up_slot("ssm", S + 2)
            up_slot("ssm", S + 3)
            c.wait("b_lo")

            def s5_in(n):
                m, b = n // 2, n % 2
                if n % 4 == 0:
                    c.wait("u_lo")
                if n >= 2:
                    c.wait("s5_prod", 2)
                for e in range(2):
                    r = slice(32 * (2 * b + e), 32 * (2 * b + e) + 32)
                    for k in range(2):
                        ins = three(acc[:, 2 * b + e, k * T:(k + 1) * T], b_hi[r, k, m], b_lo[r, k, m],
                                    hi("s5")[r, m], lo("s5")[r, m], True, True)
                c.up(ins, "s5_bu")

            def s5_out(n):
                m, b = n // 2, n % 2
                c.wait("s5_out_pool")
                if n % 2 == 0 and m >= 2:
                    c.wait("s5_ysum")
                for part, order in ((0, (0, 1)), (1, (1, 0))):
                    for e in range(2):
                        q = 2 * b + e
                        for k in range(2):
                            ins = MM(aux[m % 2][32 * q:32 * q + 32, 0:T], s_c[:, order[k], 2 * n + e],
                                     s_p[:, part, e, k], start=(part == 0 and k == 0), stop=(part == 1 and k == 1),
                                     tile_position=(0, 32 * q), skip_group_check=True)
                    if part == 0:
                        c.up(ins, "s5_y_cos")
                        c.wait("s5_out_dve", 3)
                c.up(ins, "s5_y")

            s5_in(0)
            s5_in(1)
            for n in range(2 * KT + 1):
                if n + 2 < 2 * KT:
                    s5_in(n + 2)
                if n == 0:
                    c.wait("s5_tables", 4)
                if n:
                    s5_out(n - 1)
            S = START["glu"]
            for m in range(KT):
                up_slot("s5", S + m, fresh=(m == 0))

            def ffn(l, name):
                S = START[f"ffn{l}"]
                assert used[0] == BANK[f"ffn{l}"]
                up_slot(name, S, fresh=True)
                rms()
                up_slot(name, S + 1)
                up_slot(name, S + 2)
                up_slot(name, S + 3)

                def down(s, parity, first=False, last=False, i=None, each=False):
                    c.wait("h_ready", 2)
                    ins = down_slot(s, 2 * parity, first, last, i, each)
                    c.up(ins, "mm_done")

                down(S + 4, 0, first=True)
                up_slot(name, S + 5)
                up_slot(name, S + 6)
                down(S + 7, 1)
                with pe.Fori(0, 4) as i:
                    c.enter(i, h_ready=4, mm_done=6)
                    for k in (0, 3):
                        up_slot(name, S + 8 + k, i)
                        up_slot(name, S + 9 + k, i)
                        down(S + 10 + k, k // 3, i=i)
                    c.leave(4)
                used[0] += 3 * 4
                down(S + 32, 0, last=True, each=True)

            def ple(l):
                S = START[f"ple{l}"]
                assert used[0] == BANK[f"ple{l}"]
                up_slot(f"ple{l}", S, fresh=True)
                rms()
                c.wait("pe_ready", 2)
                ins = down_slot(S + 1, 6, True, True)
                c.up(ins, "mm_done")
                for g in range(1, 4):
                    up_slot(f"ple{l}", S + g + 1)

            def head_stats(n, sqb, half):
                c.wait("hn_sq")
                if n >= 2:
                    c.wait("hn_ln")
                c.up(MM(acc[:, n % 2], half, sqb[:, n % 2], start=True, stop=True), "hn_ssq")

            def transposes(n, abuf, per):
                nk = n % 2 + 1
                c.wait("probs")
                if n >= 2:
                    c.wait("at_sb", per)
                for j in range(per):
                    for k in range(nk):
                        o = 4 // per * j + k
                        ins = nc.tensor.transpose(up[n % 2][:, o // 2, (o % 2) * P:(o % 2 + 1) * P],
                                                  abuf[:, n % 2, j * T + k * P:j * T + (k + 1) * P], ident)
                c.up(ins, "at_ps")

            def head_values(h, o, v, at, rows):
                MM(o[:, 0:T], v[:, 0], at[:, 0:T], start=True, stop=False, skip_group_check=True)
                return MM(o[:, P:T], v[:, 1], at[:, T + P:2 * T], start=False, stop=True, skip_group_check=True)

            ffn(0, "ffn0")
            ple(0)

            S = START["kvq"]
            assert used[0] == BANK["kvq"]
            token_slot("kv", S, fresh=True)
            pe.wait_ge(dma["bias_oh"], 16)
            c.up(MM(aux[0][0:HEADS, 0:384], d_oh[:, 384:384 + HEADS], d_oh[:, 0:384], start=True, stop=True), "bias_ps")
            c.wait("bias_sb")
            rms(True)
            token_slot("kv", S + 1)
            token_slot("kv", S + 2)
            token_slot("kv", S + 3)
            c.wait("hi_ready", 8)
            c.wait("lo_ready", 8)
            pe.wait_ge(dma["halves"], 16)
            for n in range(8 + 1):
                if n < 8:
                    up_slot("kv" if n % 2 == 0 else "q", S + 4 + n)
                if n >= 1:
                    head_stats(n - 1, d_sq, d_half)
            c.wait("hn_ln", 2)
            c.wait("qk_ready", 8)

            def diff_scores(n):
                h, qb = n // 2, n % 2
                if n >= 2:
                    c.wait("scores_read")
                for e in range(2):
                    r = slice(HD * e, HD * e + HD)
                    ins = MM(acc[:, 2 * (n % 2) + e, 0:P * (qb + 1)], d_q[r, h, qb * P:(qb + 1) * P],
                             d_k[r, h, 0:P * (qb + 1)], start=True, stop=True)
                c.up(ins, "scores")

            def diff_values(h):
                pe.wait_ge(sem("at_sb"), 2 * h + 2)
                if h >= 2:
                    pe.wait_ge(sem("o_ln"), h - 1)
                ins = head_values(h, aux[h % 2], d_v[:, :, h * P:(h + 1) * P], d_at[:, h % 2], P)
                c.up(ins, "pv")

            for n in range(2 * HEADS + 5):
                if n < 2 * HEADS:
                    diff_scores(n)
                if 3 <= n < 2 * HEADS + 3:
                    transposes(n - 3, d_a, 1)
                if n % 2 and n >= 5:
                    diff_values((n - 5) // 2)
                if n % 2 == 0 and n >= 6:
                    h = n // 2 - 3
                    c.wait("o_sq")
                    c.up(MM(aux[h % 2][:, T:2 * T], ones, d_q[:, h], start=True, stop=True), "o_ssq")
            c.wait("scores_read", 2)
            c.wait("at_sb", 2)
            S = START["wo"]
            assert used[0] == BANK["wo"]
            for g in range(4):
                up_slot("diff", S + g, fresh=(g == 0))

            ffn(1, "ffn1")
            ple(1)

            S = START["evin"]
            assert used[0] == BANK["evin"]
            token_slot("even", S, fresh=True)
            rms(True)
            pe.wait_ge(dma["halves"], 32)
            for n in range(4):
                up_slot("even", S + 1 + n)
                if n:
                    head_stats(n - 1, e_sq, e_half)
            c.wait("hn_ln", 2)
            c.wait("idx_ready")
            c.wait("qk_ready")
            for qb in range(2):
                if qb:
                    c.wait("idx_read")
                for h in range(4):
                    r = slice(HD * (h % 2), HD * (h % 2) + HD)
                    ins = MM(acc[:, h, 0:P * (qb + 1)],
                             e_pl[r, 1 + h // 2, qb * P:(qb + 1) * P], e_pl[r, 0, 0:P * (qb + 1)],
                             start=True, stop=True)
                c.up(ins, "idx_ps")
                up_slot("even", S + 5 + qb)
            c.wait("qk_ready", 2)
            c.wait("idx_read")
            pe.wait_ge(sem("up_free"), BANK["evout"])

            def even_scores(n):
                h, qb = n // 2, n % 2
                if n >= 2:
                    c.wait("scores_read")
                for e in range(2):
                    r = slice(HD * e, HD * e + HD)
                    ins = MM(acc[:, 2 * (n % 2) + e, 0:P * (qb + 1)], e_q[r, h, qb * P:(qb + 1) * P],
                             e_k[r, 0:P * (qb + 1)], start=True, stop=True)
                c.up(ins, "scores")

            at0 = 2 * HEADS
            for n in range(8 + 4):
                if n < 8:
                    even_scores(n)
                if 3 <= n < 11:
                    transposes(n - 3, e_a, 2)
                if n >= 5 and n % 2:
                    h = (n - 5) // 2
                    pe.wait_ge(sem("at_sb"), at0 + 4 * (h + 1))
                    if h >= 2:
                        pe.wait_ge(sem("hi_ready"), KT * UNIT["mixed"] + h - 1)
                    for e in range(2):
                        o = aux[h % 2][HD * e:HD * e + HD]
                        at = e_at[:, 2 * (h % 2) + e]
                        MM(o[:, 0:T], e_v[:, 0, HD * e:HD * e + HD], at[:, 0:T], start=True, stop=False,
                           tile_position=(0, HD * e), skip_group_check=True)
                        ins = MM(o[:, P:T], e_v[:, 1, HD * e:HD * e + HD], at[:, T + P:2 * T], start=False, stop=True,
                                 tile_position=(0, HD * e), skip_group_check=True)
                    c.up(ins, "pv")
                if n == 9:
                    c.wait("scores_read", 2)
                    c.wait("pooled")
                    for m in range(4):
                        c.up(MM(acc[:, m, 0:T], e_pw[:, m], e_cnt[:, m], start=True, stop=True), "pool_ps")
            S = START["evout"]
            assert used[0] == BANK["evout"]
            c.wait("at_sb", 4)
            for g in range(4):
                up_slot("mixed", S + g, fresh=(g == 0))

            ffn(2, "ffn2")

            S = START["qkv"]
            assert used[0] == BANK["qkv"]
            token_slot("odd", S, fresh=True)
            rms(True)
            token_slot("odd", S + 1)
            token_slot("odd", S + 2)
            token_slot("odd", S + 3)
            for n in range(8):
                up_slot("odd", S + 4 + n)
            pe.wait_ge(dma["stickmask"], 32)
            c.wait("stick_qk", 8)
            for n in range(STICKS + 4):
                if n < STICKS:
                    m, r = n // 2, slice(HD * (n % 2), HD * (n % 2) + HD)
                    if n >= 2:
                        c.wait("z_sb")
                    MM(acc[:, n % 2, 0:T], k_k[r, m, 0:P], k_q[r, m, 0:T], start=True, stop=True)
                    c.up(MM(acc[:, n % 2, T:T + P], k_k[r, m, P:T], k_q[r, m, P:T], start=True, stop=True), "z_ps")
                if 2 <= n < STICKS + 2:
                    h = n - 2
                    c.wait("brk")
                    if h >= 2:
                        c.wait("log_a")
                    o, b = acc[:, 2 + h % 2], k_b[:, h % 2]
                    MM(o[:, 0:T], k_tri, b[:, 0:T], start=True, stop=False, skip_group_check=True)
                    MM(o[:, P:T], ones, b[:, T:T + P], start=False, stop=False, skip_group_check=True)
                    c.up(MM(o[:, T:T + P], k_tri, b[:, T:T + P], start=False, stop=True, skip_group_check=True),
                         "remain")
                if n >= 4:
                    h = n - 4
                    m, r = h // 2, HD * (h % 2)
                    c.wait("a_sb")
                    if h % 2 == 0 and m >= 2:
                        pe.wait_ge(sem("hi_ready"), KT * UNIT["stick"] + m - 1)
                    o = aux[m % 2][r:r + HD]
                    MM(o[:, 0:T], k_v[:, 0, h * HD:(h + 1) * HD], k_a[:, h % 2, 0:T], start=True, stop=False,
                       tile_position=(0, r), skip_group_check=True)
                    ins = MM(o[:, P:T], k_v[:, 1, h * HD:(h + 1) * HD], k_a[:, h % 2, T:T + P], start=False,
                             stop=True, tile_position=(0, r), skip_group_check=True)
                    c.up(ins, "stick_pv")
            S = START["out"]
            assert used[0] == BANK["out"]
            for g in range(4):
                up_slot("stick", S + g, fresh=(g == 0))
            ffn(3, "ffn3")


def _up(*cols):
    w = np.concatenate(cols, axis=1)
    if w.shape[1] < 256:
        w = np.pad(w, ((0, 0), (0, 256 - w.shape[1])))
    return w.reshape(KT, P, 256).transpose(1, 0, 2).reshape(P, 2048)


def _down(rows):
    return rows.reshape(2, P, D).transpose(1, 0, 2).reshape(P, 2048)


def _pieces(w, n=256):
    return [w[:, i:i + n] for i in range(0, w.shape[1], n)]


def _ffn_slots(gate, val, down):
    ups = [_up(gate[:, n * P:(n + 1) * P], val[:, n * P:(n + 1) * P]) for n in range(2 * STEPS)]
    downs = [_down(down[j * 256:(j + 1) * 256]) for j in range(STEPS)]
    out = ups[0:2]
    for j in range(1, STEPS):
        out += [ups[2 * j], ups[2 * j + 1], downs[j - 1]]
    return out + [downs[STEPS - 1]]


def _stream(i):
    s = [_up(c) for c in _pieces(i["ssm_w_in"][0])]
    glu = i["ssm_w_glu"][0]
    s += [_up(glu[:, m * P:(m + 1) * P], glu[:, D + m * P:D + (m + 1) * P]) for m in range(KT)]

    def ffn(l):
        w = i["ffn_w_up"][l]
        return _ffn_slots(w[:, :FF], w[:, FF:], i["ffn_w_down"][l])

    def ple(l):
        g = [_up(c) for c in _pieces(i["ple_w_gate"][l])]
        return [g[0], _down(i["ple_w_proj"][l])] + g[1:]

    def qk(k, q):
        return [_up(c) for pair in zip(_pieces(k), _pieces(q)) for c in pair]

    kv, wq = i["kv_w"], i["attn_w_q"][0]
    s += ffn(0) + ple(0)
    s += [_up(c) for c in _pieces(kv[:, D:])] + qk(kv[:, :D], wq)
    s += [_up(c) for c in _pieces(i["attn_w_o"][0])] + ffn(1) + ple(1)
    w = i["ev_w_in_2"][0]
    q, k, v, qi, ki, wi, u = (w[:, a:b] for a, b in [(0, 512), (512, 640), (640, 768), (768, 1024), (1024, 1088),
                                                     (1088, 1092), (1092, 1604)])
    q = np.concatenate([q[:, c * 64:(c + 1) * 64] for t in range(4) for c in (t, t + 4)], axis=1)
    s += [_up(v, wi), _up(k, ki, ki), _up(q[:, :256]), _up(q[:, 256:]), _up(qi), _up(u[:, :256]), _up(u[:, 256:])]
    w = i["ev_w_out_2"][0]
    w = np.concatenate([w[c * 64:(c + 1) * 64] for t in range(4) for c in (t, t + 4)] + [w[512:]], axis=0)
    s += [_up(c) for c in _pieces(w)]
    s += _ffn_slots(i["ffn_w1_2"][0], i["ffn_w3_2"][0], i["ffn_w2_2"][0])
    w = i["od_w_qkv_2"][0]
    s += [_up(c) for c in _pieces(w[:, 2 * D:])] + qk(w[:, D:2 * D], w[:, :D])
    s += [_up(c) for c in _pieces(i["od_w_out_2"][0])]
    s += _ffn_slots(i["ffn_w1_2"][1], i["ffn_w3_2"][1], i["ffn_w2_2"][1])
    assert len(s) == N_SLOTS
    return np.stack(s)


def _features(v):
    return np.moveaxis(v.reshape(v.shape[:-1] + (KT, P)), -1, 0)


def _bucket():
    n = 255 - np.arange(384)
    nf = np.maximum(n, 16).astype(np.float32)
    large = 16 + (np.log(nf / np.float32(16)) / np.float32(math.log(8.0)) * np.float32(16)).astype(np.int32)
    b = np.where(n < 16, n, np.minimum(large, 31))
    oh = np.zeros((33, 384), np.float32)
    for m in range(384):
        oh[b[m] if n[m] >= 0 else 32, m] = 1.0
    return oh


def _layout(i):
    f = np.float32
    i = {k: np.asarray(v) for k, v in i.items()}
    a = {"stream": _stream(i)}
    a["x"] = i["x"][0].T.reshape(KT, P, T).transpose(1, 0, 2)
    for l in range(2):
        a[f"p{l}"] = i["p"][l, 0].T.reshape(2, P, T).transpose(1, 0, 2)
    gains = np.stack([i["ssm_norm"][0], i["ffn_norm"][0], i["ple_norm"][0], i["kv_norm"], i["attn_norm"][0],
                      i["ffn_norm"][1], i["ple_norm"][1], i["norm_mix_g_2"][0], i["norm_ffn_g_2"][0],
                      i["norm_mix_g_2"][1], i["norm_ffn_g_2"][1]])
    cw = np.concatenate([i["ffn_conv_w"], i["ffn_conv_b"][:, None]], axis=1).reshape(2, 4, 2, 22, P)
    cw = cw.transpose(4, 0, 3, 2, 1).reshape(P, -1)
    col = lambda v: np.concatenate([v, v])[:, None]
    lam = np.zeros((P, 4), f)
    for j, n in enumerate(["lambda_q1", "lambda_q2", "lambda_k1", "lambda_k2"]):
        lam[:64, j] = i[n][0]
    a["par"] = np.concatenate([
        _features(gains).reshape(P, -1), cw, _features(i["ssm_d"][0]), col(i["k_norm"]), col(i["q_norm"][0]),
        i["subln"][0][:, None], col(i["ev_k_norm_g_2"][0]), col(i["ev_q_norm_g_2"][0]), lam,
        i["ev_pool_scale_2"][0].reshape(4, P).T, np.ones((P, P), f), np.eye(P, dtype=f)], axis=1)
    pairs = lambda v: v.reshape(PAIRS, P).T
    dt = np.repeat(i["ssm_log_dt"][0][:, None], STATE, axis=1)
    a["s5_par"] = np.stack([pairs(i["ssm_lambda_re"][0]), pairs(i["ssm_lambda_im"][0]), pairs(dt)], axis=1)
    b = np.zeros((4, 32, 2, KT, P), f)
    cc = np.zeros((P, 2, PAIRS, 32), f)
    for r, (nb, ncn) in enumerate([("ssm_b_re", "ssm_c_re"), ("ssm_b_im", "ssm_c_im")]):
        bb, c_ = i[nb][0], i[ncn][0]
        for g in range(GROUPS):
            pr, h = g // 2, g % 2
            b[pr % 4, h * 16:h * 16 + 16, r, pr // 4, h * 64:h * 64 + 64] = bb[g].T
            cc[h * 64:h * 64 + 64, r, pr, h * 16:h * 16 + 16] = c_[g].T
    a["s5_b"], a["s5_c"] = b.reshape(P, 2, KT, P), cc
    a["tmat"] = np.broadcast_to(np.arange(P, dtype=f), (P, P))
    wb = np.concatenate([i["rel_bias"], np.full((1, HEADS), NEG, f)])
    a["bias_oh"] = np.concatenate([_bucket(), wb], axis=1)
    q, k = np.arange(P)[:, None], np.arange(T)[None, :]
    a["causal"] = np.stack([np.where(k <= q + P * j, 0, NEG) for j in range(2)], axis=1).astype(f)
    cnt = np.stack([1.0 / np.minimum(np.arange(1, T + 1), w) for w in (2, 4, 8, 16)]).astype(f)
    a["count"] = np.broadcast_to(cnt, (P, 4, T))
    a["halves"] = np.kron(np.eye(2), np.ones((HD, HD))).astype(f)
    a["pool_w"] = i["ev_pool_w_2"][0].transpose(1, 0, 2)
    s_, q_ = np.arange(P)[:, None], np.arange(T)[None, :]
    a["stickmask"] = np.concatenate([np.where(s_ < q_, 0, NEG), np.where(s_ < q_[:, :P], 0, NEG)], axis=1).astype(f)
    a["tri"] = (np.arange(P)[:, None] >= np.arange(P)[None, :]).astype(f)
    return {k: np.ascontiguousarray(v) for k, v in a.items()}


def kernel(**inputs):
    import concourse.bacc as bacc
    from concourse.bass_utils import run_bass_kernel_spmd

    arrays = _layout(inputs)
    nc = bacc.Bacc("TRN2", target_bir_lowering=False, num_devices=1)
    f32 = mybir.dt.float32
    a = {k: nc.dram_tensor(f"in_{k}", v.shape, f32, kind="ExternalInput").ap() for k, v in arrays.items()}
    scratch = nc.dram_tensor("bias_rows", (HEADS * P * 384,), f32, kind="Internal").ap()
    a["scratch"] = scratch.rearrange("(h p m) -> h p m", h=HEADS, p=P)
    a["scratch_toeplitz"] = bass.AP(tensor=scratch.tensor, offset=P - 1, ap=[[383, P], [P * 384, HEADS], [1, T]])
    out = nc.dram_tensor("out_x", (KT, P, T), f32, kind="ExternalOutput").ap()
    program(nc, a, out)
    r = run_bass_kernel_spmd(nc, [{f"in_{k}": v for k, v in arrays.items()}], core_ids=[0])
    return r.results[0]["out_x"].reshape(D, T).T.reshape(1, T, D)
```

```python
import math
from contextlib import ExitStack

import numpy as np

import concourse.bass as bass
from concourse import mybir

P = 128
D = 1024
T = 256
KT = D // P
TT = T // P
FF = 2816
STEPS = FF // (2 * P)
GROUPS, GDIM, STATE = 64, 16, 64
PAIRS = GROUPS // 2
HEADS, HD = 8, 64
SEL = 64
STICKS = 16
EPS = 1e-6
NEG = -1e30
TAKEN = -3e38
ROUND = 1.5 * 2.0 ** 23
LAM_INIT = 0.8 - 0.6 * math.exp(-0.3)
TWO_PI = 6.2831850

RING = 6
SPLIT = 3
STAGES = [("w_in", 4), ("glu", 8), ("ffn0", 3 * STEPS), ("ple0", 5), ("kvq", 12), ("wo", 4),
          ("ffn1", 3 * STEPS), ("ple1", 5), ("evin", 7), ("evout", 4), ("ffn2", 3 * STEPS),
          ("qkv", 12), ("out", 4), ("ffn3", 3 * STEPS)]
START, BANK, N_SLOTS, _u = {}, {}, 0, 0
for _name, _n in STAGES:
    START[_name], BANK[_name] = N_SLOTS, _u
    N_SLOTS += _n
    _u += {"ffn": 2 * STEPS, "ple": 4}.get(_name[:3], _n)

UNITS = ["ssm", "s5", "ffn0", "ple0", "kv", "q", "diff", "ffn1", "ple1", "even", "mixed", "ffn2",
         "odd", "stick", "ffn3"]
UNIT = {n: i for i, n in enumerate(UNITS)}
SET = dict(ssm=2, s5=1, ffn0=0, ple0=0, kv=1, q=0, diff=1, ffn1=0, ple1=0, even=1, mixed=1,
           ffn2=0, odd=0, stick=1, ffn3=0)
GAINS = ["ssm", "ffn0", "ple0", "kv", "q", "ffn1", "ple1", "even", "ffn2", "odd", "ffn3"]
GAIN = {n: i for i, n in enumerate(GAINS)}

COLS, _c = {}, 0
for _name, _n in [("gain", len(GAINS) * KT), ("conv", 2 * 22 * 8), ("dskip", KT), ("qk", 2),
                  ("subln", 1), ("evqk", 2), ("lam", 4), ("pscale", 4), ("ones", P),
                  ("ident", P)]:
    COLS[_name] = (_c, _c + _n)
    _c += _n
N_COLS = _c
MIX = 15264


class Count:

    def __init__(self, sem):
        self.sem, self.n, self.i, self.per = sem, 0, None, 0

    def value(self):
        return self.n if self.i is None else self.i * self.per + self.n

    def enter(self, i, per):
        self.i, self.per, self.base = i, per, self.n

    def leave(self, turns):
        assert self.n - self.base == self.per, (self.n - self.base, self.per)
        self.n, self.i = self.base + self.per * turns, None


class Counts:

    def __init__(self, eng, sems):
        self.eng, self.sems, self.c = eng, sems, {}

    def of(self, name):
        if name not in self.c:
            self.c[name] = Count(self.sems(name))
        return self.c[name]

    def up(self, ins, name):
        c = self.of(name)
        c.n += 1
        ins.then_inc(c.sem, 1)

    def up_and_wait(self, ins, name):
        self.up(ins, name)
        self.eng.wait_ge(self.of(name).sem, self.of(name).value())

    def tell(self, name):
        c = self.of(name)
        c.n += 1
        self.eng.sem_inc(c.sem, 1)

    def wait(self, name, k=1):
        c = self.of(name)
        c.n += k
        self.eng.wait_ge(c.sem, c.value())

    def enter(self, i, **per):
        for name, k in per.items():
            self.of(name).enter(i, k)
        self.looped = list(per)

    def leave(self, turns):
        for name in self.looped:
            self.of(name).leave(turns)


def program(nc, a, out):
    f32, f32r = mybir.dt.float32, mybir.dt.float32r
    ALU, ACT, AX = mybir.AluOpType, mybir.ActivationFunctionType, mybir.AxisListType
    ctx = ExitStack()
    with ctx:
        def sb(name, shape, dt=f32):
            return ctx.enter_context(nc.sbuf_tensor(name, shape, dt))

        ring = sb("ring", [P, RING, 2048])
        w_hi = sb("w_hi", [P, SPLIT, 2048], f32r)
        w_lo = sb("w_lo", [P, SPLIT, 2048], f32r)
        x = sb("x", [P, KT, T])
        sq = sb("sq", [P, KT, T])
        par = sb("par", [P, N_COLS])
        rstd = sb("rstd", [P, T])
        tok = sb("tok", [P, 4])
        little = sb("little", [P, 8])
        with nc.sbuf_tensor("mix_r", [P, MIX], f32r) as mix_r:
            pass
        mix = sb("mix", [P, MIX])
        with nc.sbuf_tensor("opnd_first", [P, 2, KT, T], f32r) as opnd_first:
            pass
        with nc.sbuf_tensor("s5_area", [P, 2, 2 * KT, T], f32) as s5_area:
            pass
        opnd = [sb(f"opnd{i}", [P, 2, KT, T], f32r) for i in range(2)] + [opnd_first]
        acc = ctx.enter_context(nc.psum_tensor("acc", [P, 4, 512], f32))
        up = [ctx.enter_context(nc.psum_tensor(f"up{i}", [P, 2, T], f32)) for i in range(2)]
        aux = [ctx.enter_context(nc.psum_tensor(f"aux{i}", [P, 512], f32)) for i in range(2)]

        eps, neg_lam, sub_g, lam_e = little[:, 0:1], little[:, 1:2], little[:, 2:3], little[:, 3:5]

        def pcol(name, lo=0, n=None):
            s, e = COLS[name]
            return par[:, s + lo:(s + lo + n) if n else e]

        ident, ones = pcol("ident"), pcol("ones")

        def gain(name, m):
            return pcol("gain", GAIN[name] * KT + m, 1)

        sems = {}

        def sem(name):
            if name not in sems:
                sems[name] = ctx.enter_context(nc.semaphore(name))
            return sems[name]

        ring_full = [sem(f"ring_full{i}") for i in range(RING)]
        DMAS = ["par", "x", "s5_par", "s5_mat", "s5_c", "s5_t", "pe0", "pe1", "bias_oh", "bias_w",
                "bias_r", "halves", "causal", "stickmask", "outd"]
        dma = {n: sem(f"dma_{n}") for n in DMAS}

        def carve(*sizes):
            at, views = 0, []
            for shape in sizes:
                n = int(np.prod(shape))
                v = mix[:, at:at + n]
                if len(shape) == 2:
                    v = v.rearrange("p (a b) -> p a b", a=shape[0])
                if len(shape) == 3:
                    v = v.rearrange("p (a b c) -> p a b c", a=shape[0], b=shape[1])
                views.append(v)
                at += n
            assert at <= MIX, at
            return views

        (s_cs, s_sn, s_p, s_c, s_b, s_y, s_tmat, s_prep, s_mag, s_phi, s_e, s_t, s_init) = carve(
            (PAIRS, P), (PAIRS, P), (2, 2, 2 * T), (2, PAIRS, 32), (2, KT, P), (2, T), (P,), (3, PAIRS), (PAIRS,),
            (PAIRS,), (3, PAIRS), (2, 2, 2), (2, 2))
        s_p = s_p.rearrange("p a e (k t) -> p a e k t", k=2)
        s_work = s_y.rearrange("p a (b c) -> p (a b) c", c=PAIRS)
        s_m = s5_area[:, 0].rearrange("p k t -> p (k t)").rearrange(
            "p (m e k t) -> p m e k t", m=4, e=2, k=2)
        s_raw = s5_area[:, 1].rearrange("p (a h k) t -> p a h (k t)", a=2, h=2)[:, :, 1].rearrange(
            "p a (b c) -> p a b c", b=PAIRS)
        s_cf = s_p[:, 0].rearrange("p e k t -> p (e k t)").rearrange("p (b c) -> p b c", b=PAIRS)
        (f_u, f_c, f_gg, f_h, f_pe) = carve((4, 258), (4, T), (2, T), (2, T), (4, T))
        (d_k, d_q, d_v, d_bias, d_tmp, d_sq, d_l, d_a, d_at, d_st, d_half) = carve(
            (KT, T), (KT, T), (TT, D), (HEADS, T), (3, 2 * T), (2, 2 * T), (2, 2 * T), (2, T),
            (2, 2 * T), (64,), (P,))
        at = KT * T * 2 + TT * D + HEADS * T + 12 * T + 8 * T + 64 + P
        d_sq_r = mix_r[:, at:at + 4 * T].rearrange("p (a b) -> p a b", a=2)
        d_half_r = mix_r[:, at + 4 * T:at + 4 * T + P]
        assert at + 4 * T + P <= MIX
        d_row = d_a.rearrange("p a b -> p (a b)")[0:HEADS, 0:384]
        d_oh = mix[0:33, 0:384 + HEADS]
        (e_v, e_k, e_q, e_pl, e_tmp, e_sq, e_l, e_a, e_at, e_mask, e_causal, e_w, e_rel, e_st, e_m8,
         e_out, e_cnt, e_pw, e_half, e_u, e_pa) = carve(
            (TT, P), (T,), (4, T), (3, T), (3, 2 * T), (2, 2 * T), (2, 2 * T), (2, 2 * T), (4, 2 * T),
            (2, T), (2, T), (TT, 4), (T,), (64,), (8,), (2, T), (4, T), (4, P), (P,),
            (4, 16 + T), (4, 16 + T))
        at = 256 + 256 + 4 * T + 3 * T + 5 * 2 * T
        e_sq_r = mix_r[:, at:at + 4 * T].rearrange("p (a b) -> p a b", a=2)
        at += 2 * 2 * T
        e_half_r = mix_r[:, at:at + P]
        e_pb = e_tmp.rearrange("p a b -> p (a b)")[:, 0:4 * (16 + T)].rearrange("p (a b) -> p a b", a=4)
        (k_k, k_q, k_v, k_mask, k_tri, k_z, k_t, k_b, k_a, k_out) = carve(
            (KT, T), (KT, T), (TT, D), (384,), (P,), (6, 384), (2, 384), (2, 384), (2, 384), (2, T))

        b_hi, b_lo = (v[:, START["w_in"] + 2].rearrange("p (r m c) -> p r m c", r=2, m=KT) for v in (w_hi, w_lo))

        def by_chunk(v):
            return v.rearrange("p e k (c t) -> p e (k c) t", c=2)

        def chunks(v):
            return v.rearrange("p e (c t) -> p e c t", c=2)

        def local(table, n, k):
            return table[:, 2 * n:2 * n + 2].unsqueeze(2).broadcast_to([P, 2, k, P])

        def hi(name):
            return opnd[SET[name]][:, 0]

        def lo(name):
            return opnd[SET[name]][:, 1]

        block = ctx.enter_context(nc.Block())

        @block.sync
        def _(sp):
            def load(r, slot):
                sp.dma_start(ring[:, r], a["stream"][slot].rearrange("a p n -> (a p) n")).then_inc(ring_full[r], 16)

            sp.dma_start(par[:], a["par"]).then_inc(dma["par"], 16)
            sp.dma_start(x[:], a["x"]).then_inc(dma["x"], 16)
            for s in range(RING):
                load(s, slice(s, s + 1))
            turns = N_SLOTS // RING - 1
            with sp.Fori(0, turns) as i:
                for r in range(RING):
                    sp.wait_ge(sem("w_ready"), i * RING + (r + 1))
                    load(r, bass.ds(i * RING + (RING + r), 1))
            for s in range(RING * (turns + 1), N_SLOTS):
                sp.wait_ge(sem("w_ready"), s - RING + 1)
                load(s % RING, slice(s, s + 1))
            c = Counts(sp, sem)
            for m in range(KT):
                c.wait("x_ready", 8 * 9 + 1 if m == 0 else 1)
                sp.dma_start(out[m], x[:, m]).then_inc(dma["outd"], 16)
            sp.wait_ge(dma["outd"], 16 * KT)

        @block.gpsimd
        def _(pool):
            c = Counts(pool, sem)

            def low_part(s, k=0):
                c.wait("w_hi_ready")
                r, b = (s + k) % RING, (s + k) % SPLIT
                c.up(nc.gpsimd.tensor_tensor(w_lo[:, b], ring[:, r], w_hi[:, b].bitcast(f32), ALU.subtract),
                     "w_ready")

            c.wait("w_hi_ready")
            c.wait("w_ready")
            for s in range(1, START["glu"]):
                low_part(s)

            pool.wait_ge(dma["s5_c"], 16)
            c.wait("s5_f")
            w = s_work
            cr, ci = s_raw[:, 0], s_raw[:, 1]
            fr = w[:, 9].unsqueeze(2).broadcast_to([P, PAIRS, 32])
            fi = w[:, 10].unsqueeze(2).broadcast_to([P, PAIRS, 32])
            for k, (f0, f1, op) in enumerate([(fr, fi, ALU.subtract), (fi, fr, ALU.add)]):
                c.up(nc.gpsimd.tensor_tensor(s_c[:, k], cr, f0, ALU.mult), "pool_step")
                c.up_and_wait(nc.gpsimd.tensor_tensor(s_cf, ci, f1, ALU.mult), "pool_step")
                c.up_and_wait(nc.gpsimd.tensor_tensor(s_c[:, k], s_c[:, k], s_cf, op), "s5_c_ready")

            def sums(n):
                m, r = s_m[:, n % 3], s_m[:, 3]
                c.wait("s5_prod", 2)
                c.up(nc.gpsimd.tensor_tensor(m[:, :, 1], r[:, :, 0], m[:, :, 1], ALU.subtract), "s5_sum")
                c.up(nc.gpsimd.tensor_tensor(m[:, :, 0], m[:, :, 0], r[:, :, 1], ALU.add), "s5_sum")

            def products(n):
                z = s_m[:, n % 3]
                c.wait("s5_scan")
                if n:
                    c.wait("s5_y_cos")
                c.up(nc.gpsimd.tensor_tensor(by_chunk(s_p[:, 0]), local(s_cs, n, 4), by_chunk(z), ALU.mult),
                     "s5_out_pool")
                if n:
                    c.wait("s5_y")
                c.up(nc.gpsimd.tensor_tensor(chunks(s_p[:, 1, :, 1]), local(s_sn, n, 2), chunks(z[:, :, 1]), ALU.mult),
                     "s5_out_pool")

            c.wait("s5_tables", 4)
            for n in range(2 * KT + 1):
                if n < 2 * KT:
                    sums(n)
                if n:
                    products(n - 1)
            c.wait("w_hi_ready")
            c.wait("w_ready")
            for s in range(START["glu"] + 1, START["glu"] + SPLIT):
                low_part(s)

            def low_parts(first, end):
                turns = (end - first) // RING
                with pool.Fori(0, turns) as i:
                    c.enter(i, w_hi_ready=RING, w_ready=RING)
                    for k in range(RING):
                        low_part(first, k)
                    c.leave(turns)
                for s in range(first + turns * RING, end):
                    low_part(s)

            low_parts(START["glu"] + SPLIT, START["evout"] + SPLIT)
            c.wait("pool_in", 2)
            src, dst = e_u, e_pb
            for g in range(4):
                wdt = 2 ** g
                c.up_and_wait(nc.gpsimd.tensor_tensor(dst[:, g:, 16:], src[:, g:, 16:], src[:, g:, 16 - wdt:16 + T - wdt],
                                                      ALU.add), "pool_step")
                src, dst = dst, e_pa if g % 2 == 0 else e_pb
            pool.wait_ge(dma["causal"], 48)
            for g in range(4):
                c.up(nc.gpsimd.tensor_tensor(e_cnt[:, g], e_cnt[:, g], (e_pa if g % 2 else e_pb)[:, g, 16:], ALU.mult),
                     "pool_step")
            pool.wait_ge(sem("pool_step"), c.of("pool_step").value())
            c.up(nc.gpsimd.tensor_tensor(e_cnt, e_cnt, e_u[:, :, 16:], ALU.subtract), "pooled")
            low_parts(START["evout"] + SPLIT, N_SLOTS)

        @block.scalar
        def _(act):
            c = Counts(act, sem)
            A = nc.scalar.activation
            ahead = [0]

            def high_part(s, i=None):
                dyn = 0 if i is None else i
                act.wait_ge(ring_full[s % RING], dyn * 16 + 16 * (s // RING + 1))
                if s >= SPLIT:
                    act.wait_ge(sem("mm_done"), dyn * RING + (s - SPLIT + 1))
                c.up(A(w_hi[:, s % SPLIT], ring[:, s % RING], ACT.Copy), "w_hi_ready")

            def high_parts_to(s):
                while ahead[0] <= min(s, N_SLOTS - 1):
                    high_part(ahead[0])
                    ahead[0] += 1

            def new_operand(name, squares=True):
                for m in range(KT):
                    if squares:
                        c.up(A(sq[:, m], x[:, m], ACT.Square), "sq_ready")
                    c.up(A(hi(name)[:, m], x[:, m], ACT.Copy, scale=gain(name, m)), "hi_ready")

            def from_psum(name, m, src, buf, scale=1.0):
                b = buf[:, m % 2]
                if m >= 2:
                    act.wait_ge(sem("lo_ready"), KT * UNIT[name] + m - 1)
                c.up_and_wait(A(b, src, ACT.Copy, scale=scale), "act_step")
                c.up(A(hi(name)[:, m], b, ACT.Copy), "hi_ready")

            def rms(tokens=False):
                nc.scalar.preload_act_table_set("natural_log_exp_and_others")
                c.wait("ssq")
                c.up_and_wait(A(rstd[:], aux[1][:, 0:T], ACT.Ln, scale=1.0 / D, bias=eps), "act_step")
                c.up(A(rstd[:], rstd[:], ACT.Exp, scale=-0.5), "rstd")
                if tokens:
                    c.up_and_wait(A(tok[:, 2:4], aux[0][:, 0:2], ACT.Ln, scale=1.0 / D, bias=eps), "act_step")
                    c.up(A(tok[:, 2:4], tok[:, 2:4], ACT.Exp, scale=-0.5), "rstd_tok")

            act.dma_start(s_prep, a["s5_par"]).then_inc(dma["s5_par"], 16)
            act.dma_start(s_tmat, a["tmat"]).then_inc(dma["s5_t"], 16)
            act.wait_ge(dma["s5_par"], 16)
            w = s_work
            c.up(A(w[:, 0], s_prep[:, 2], ACT.Exp), "dt")
            c.wait("s5_mu")
            c.up(A(s_mag, w[:, 1], ACT.Exp), "mag")
            act.wait_ge(dma["par"], 16)
            act.wait_ge(dma["x"], 16)
            for m in range(KT):
                c.up(A(hi("ssm")[:, m], x[:, m], ACT.Copy, scale=gain("ssm", m)), "hi_ready")
            high_parts_to(1)
            for m in range(KT):
                c.up(A(sq[:, m], x[:, m], ACT.Square), "sq_ready")
            act.dma_start(s_raw, a["s5_c"]).then_inc(dma["s5_c"], 16)
            act.dma_start(s_b, a["s5_b"]).then_inc(dma["s5_mat"], 16)
            c.wait("lam_sum")
            c.up(A(lam_e, aux[1][:, 0:2], ACT.Exp), "lam_exp")
            high_parts_to(2)
            c.wait("s5_turn")
            c.up(A(w[:, 4], s_phi, ACT.Sin, scale=TWO_PI), "s5_sc")
            c.up(A(w[:, 5], s_phi, ACT.Sin, scale=TWO_PI / 2), "s5_sc")
            c.up(A(s_e[:, 2], w[:, 12], ACT.Sin, scale=TWO_PI), "s5_sc")
            c.up(A(w[:, 13], w[:, 12], ACT.Sin, scale=TWO_PI / 2), "s5_sc")

            def s5_tables(g):
                q = slice(8 * g, 8 * g + 8)
                c.wait("s5_frac")
                c.up_and_wait(A(s_cs[:, q], s_sn[:, q], ACT.Sin, scale=TWO_PI / 2), "s5_sin")
                c.up(A(s_sn[:, q], s_sn[:, q], ACT.Sin, scale=TWO_PI), "s5_sin")
                c.up(A(s_cs[:, q], s_cs[:, q], ACT.Square), "s5_half")

            s5_tables(0)
            c.wait("eps")
            rms()
            high_parts_to(3)
            s5_tables(1)

            def u_high(m):
                act.wait_ge(sem("up_free"), m // 2 + 1)
                c.up(A(hi("s5")[:, m], sq[:, m], ACT.Copy), "u_hi")

            for m in range(4):
                u_high(m)
            s5_tables(2)
            s5_tables(3)
            act.wait_ge(dma["s5_mat"], 16)
            act.wait_ge(sem("mm_done"), 3)
            c.up(A(b_hi, s_b, ACT.Copy), "b_hi")
            high_parts_to(START["glu"])
            c.wait("s5_c_ready", 2)
            for m in range(4, KT):
                u_high(m)

            for m in range(KT):
                if m == KT - 2:
                    act.wait_ge(sem("s5_bu"), 2 * KT)
                    high_parts_to(START["glu"] + SPLIT - 1)
                c.wait("s5_ysum")
                c.up_and_wait(A(s_y[:, 1], s_y[:, 0], ACT.Gelu_apprx_tanh), "act_step")
                c.up(A(hi("s5")[:, m], s_y[:, 1], ACT.Copy), "hi_ready")

            def operand_tile(name, m):
                c.wait("x_ready")
                c.up(A(sq[:, m], x[:, m], ACT.Square), "sq_ready")
                c.up(A(hi(name)[:, m], x[:, m], ACT.Copy, scale=gain(name, m)), "hi_ready")

            for m in range(KT):
                s = START["glu"] + m
                high_parts_to(s + 2)
                act.wait_ge(sem("mm_done"), s + 1)
                c.up(A(f_gg[:, 0], up[m % 2][:, 1], ACT.Sigmoid), "gated")
                if m == KT - 1:
                    high_parts_to(s + 3)
                operand_tile("ffn0", m)

            def ffn(l, end):
                S = START[f"ffn{l}"]

                def gate():
                    c.wait("g_ready")
                    if l < 2:
                        c.up(A(f_gg[:, 0], f_c[:, 0], ACT.Gelu_apprx_tanh), "gated")
                    else:
                        c.up(A(f_gg[:, 0], f_u[:, 0, 2:258], ACT.Silu), "gated")

                high_parts_to(S + 2)
                rms()
                for s in range(S, S + 8):
                    high_parts_to(s + 2)
                    if s - S not in (4, 7):
                        gate()
                assert ahead[0] == S + 10
                turns = 4 if end else 3
                with act.Fori(0, turns) as i:
                    c.enter(i, g_ready=4, gated=4, w_hi_ready=6)
                    for k in range(6):
                        high_part(S + 10 + k, i)
                        if k % 3 != 2:
                            gate()
                    c.leave(turns)
                ahead[0] = S + 10 + 6 * turns
                for k in range(6 * turns, 24):
                    high_parts_to(S + 10 + k)
                    if k % 3 != 2:
                        gate()
                if end:
                    high_parts_to(S + 34)
                    for m in range(KT):
                        operand_tile(end, m)

            def pe_operand(l):
                act.wait_ge(dma[f"pe{l}"], 16)
                for k in range(2):
                    c.up(A(opnd[1][:, 0, 6 + k], f_pe[:, k], ACT.Copy), "pe_hi")

            def ple(l, ends):
                S = START[f"ple{l}"]
                high_parts_to(S + 3)
                rms()
                for g in range(4):
                    c.wait("ple_u")
                    c.up(A(f_c[:, 2 * (g % 2):2 * (g % 2) + 2], f_u[:, 2 * (g % 2):2 * (g % 2) + 2, 2:258],
                           ACT.Sigmoid), "gated")
                    high_parts_to(S + g + 4)
                    for m in (2 * g, 2 * g + 1):
                        operand_tile(ends[0], m)
                for name in ends[1:]:
                    new_operand(name, squares=False)

            def residual(name, S):
                for m in range(KT):
                    high_parts_to(S + m // 2 + (3 if m >= 6 else 2))
                    operand_tile(name, m)

            def head_norms(n, count, raw, sqb, sq_r, first, banks):
                if n < count:
                    if n >= 2:
                        act.wait_ge(sem("qk_ready"), first + n - 1)
                    c.wait("hn_raw")
                    c.up_and_wait(A(sqb[:, n % 2], raw[:, n % 3], ACT.Square), "act_step")
                    if n:
                        act.wait_ge(sem("hn_ssq"), first + n)
                    c.up(A(sq_r[:, 0], sqb[:, n % 2], ACT.Copy), "hn_sq")
                if 1 <= n <= count:
                    b = sqb[:, (n - 1) % 2]
                    c.wait("hn_ssq")
                    dve_read = sem("hn_lo")
                    act.wait_ge(dve_read, first + n)
                    c.up_and_wait(A(b, banks[(n - 1) % 2], ACT.Ln, scale=1.0 / HD, bias=eps), "hn_ln")
                    c.up(A(b, b, ACT.Exp, scale=-0.5), "hn_rstd")

            def softmax_exp(n, lbuf, st):
                nk = P * (n % 2 + 1)
                c.wait("neg_max")
                b = n % 2
                for e in range(2):
                    L = lbuf[:, b].rearrange("p (c k) -> p c k", c=2)[:, e, 0:nk]
                    c.up(A(L, L, ACT.Exp, bias=st[:, 40 + 2 * b + e:41 + 2 * b + e],
                           accum_out=st[:, 44 + 2 * b + e:45 + 2 * b + e]), "exps")

            def attn_copy(n, at, per):
                nk = n % 2 + 1
                c.wait("at_ps")
                src = up[n % 2][:].rearrange("p a t -> p (a t)").rearrange("p (j k q) -> p j k q", j=per, k=4 // per)
                for j in range(per):
                    t = (n // 2) % 2
                    dst = at[:, per * t + j].rearrange("p (k q) -> p k q", k=2)[:, 0:nk, (n % 2) * P:(n % 2) * P + P]
                    c.up(A(dst, src[:, j, 0:nk], ACT.Copy), "at_sb")

            act.dma_start(f_pe[:, 0:2], a["p0"]).then_inc(dma["pe0"], 16)
            pe_operand(0)
            ffn(0, "ple0")
            ple(0, ["kv", "q"])

            S = START["kvq"]
            high_parts_to(S + 2)
            c.wait("mix_free")
            act.dma_start(d_oh, a["bias_oh"]).then_inc(dma["bias_oh"], 16)
            act.dma_start(d_half, a["halves"]).then_inc(dma["halves"], 16)
            rms(True)
            high_parts_to(S + 3)
            c.wait("bias_sb")
            act.dma_start(a["scratch"], d_row.unsqueeze(1).broadcast_to([HEADS, P, 384])).then_inc(dma["bias_w"], 16)
            act.wait_ge(dma["halves"], 16)
            c.up(A(d_half_r, d_half, ACT.Copy), "half_r")
            for n in range(8):
                high_parts_to(S + 4 + n + 2)
                if n == 4:
                    act.wait_ge(dma["bias_w"], 16)
                    act.dma_start(d_bias, a["scratch_toeplitz"]).then_inc(dma["bias_r"], 16)
                head_norms(n, 8, d_tmp, d_sq, d_sq_r, 0, [aux[0][:], aux[1][:]])
            high_parts_to(S + 14)
            for n in range(2 * HEADS + 10):
                if n % 2 and 7 <= n < 2 * HEADS + 7:
                    h = (n - 7) // 2
                    c.wait("pv")
                    c.up(A(sq[:, h], aux[h % 2][:, 0:T], ACT.Copy), "o_raw")
                    c.up(A(d_q[:, h], aux[h % 2][:, 0:T], ACT.Square), "o_sq")
                if n % 2 and 9 <= n < 2 * HEADS + 9:
                    h = (n - 9) // 2
                    c.wait("o_ssq")
                    c.up_and_wait(A(d_q[:, h], aux[h % 2][:, T:2 * T], ACT.Ln, scale=1.0 / P, bias=eps), "o_ln")
                    c.up(A(d_q[:, h], d_q[:, h], ACT.Exp, scale=-0.5), "o_rstd")
                if n % 2 and n >= 11:
                    c.wait("o_norm")
                    c.up(A(hi("diff")[:, (n - 11) // 2], sq[:, (n - 11) // 2], ACT.Copy, scale=sub_g), "hi_ready")
                if 3 <= n < 2 * HEADS + 3:
                    attn_copy(n - 3, d_at, 1)
                if n < 2 * HEADS:
                    softmax_exp(n, d_l, d_st)
                if n == 0:
                    head_norms(8, 8, d_tmp, d_sq, d_sq_r, 0, [aux[0][:], aux[1][:]])
            residual("ffn1", START["wo"])

            act.dma_start(f_pe[:, 0:2], a["p1"]).then_inc(dma["pe1"], 16)
            pe_operand(1)
            ffn(1, "ple1")
            ple(1, ["even"])

            S = START["evin"]
            high_parts_to(S + 2)
            c.wait("mix_free")
            act.dma_start(e_half, a["halves"]).then_inc(dma["halves"], 16)
            act.dma_start(e_causal, a["causal"]).then_inc(dma["causal"], 16)
            act.dma_start(e_cnt, a["count"]).then_inc(dma["causal"], 16)
            act.dma_start(e_pw, a["pool_w"]).then_inc(dma["causal"], 16)
            rms(True)
            e_relu = e_at.rearrange("p a b -> p (a b)").rearrange("p (q h k) -> p q h k", q=2, h=4)
            for n in range(3 + 1):
                high_parts_to(S + (3, 5, 6, 8)[n])
                if n in (1, 2):
                    nk = P * n
                    c.wait("idx_ps")
                    c.up(A(e_relu[:, n - 1, :, 0:nk], acc[:, 0:4, 0:nk], ACT.Relu), "idx_relu")
                if n == 0:
                    act.wait_ge(dma["halves"], 32)
                    c.up(A(e_half_r, e_half, ACT.Copy), "half_r")
                head_norms(n, 3, e_tmp, e_sq, e_sq_r, 8, [aux[0][:], aux[1][:]])
            high_parts_to(S + 9)
            for n in range(8 + 5):
                if 3 <= n < 11:
                    attn_copy(n - 3, e_at, 2)
                if n < 8:
                    softmax_exp(n, e_l, e_st)
                if n >= 6 and n % 2 == 0:
                    c.wait("pv")
                    h = n // 2 - 3
                    from_psum("mixed", h, aux[h % 2][:, 0:T], e_out)
            for m in range(4):
                c.wait("pool_ps")
                from_psum("mixed", 4 + m, acc[:, m, 0:T], e_out, pcol("pscale", m, 1))
            residual("ffn2", START["evout"])

            ffn(2, "odd")

            S = START["qkv"]
            high_parts_to(S + 2)
            c.wait("mix_free")
            act.dma_start(k_mask, a["stickmask"]).then_inc(dma["stickmask"], 16)
            act.dma_start(k_tri, a["tri"]).then_inc(dma["stickmask"], 16)
            rms(True)
            for s in range(S, S + 12):
                high_parts_to(s + 2)
            high_parts_to(S + 14)
            for n in range(STICKS + 5):
                if n < STICKS:
                    c.wait("z_abs")
                    t = k_t[:, n % 2]
                    c.up_and_wait(A(t, t, ACT.Exp, scale=-1.0), "act_step")
                    c.up(A(t, t, ACT.Ln, bias=1.0), "log1p")
                if 3 <= n < STICKS + 3:
                    h = n - 3
                    c.wait("log_a")
                    if h >= 2:
                        c.wait("stick_pv")
                    c.up(A(k_a[:, h % 2], k_z[:, h % 6], ACT.Exp), "a_sb")
                if n >= 6 and n % 2 == 0:
                    m = n // 2 - 3
                    act.wait_ge(sem("stick_pv"), 2 * m + 2)
                    from_psum("stick", m, aux[m % 2][:, 0:T], k_out)
            residual("ffn3", START["out"])
            ffn(3, None)

        @block.vector
        def _(dve):
            c = Counts(dve, sem)
            V = nc.vector

            def step(ins):
                c.up_and_wait(ins, "dve_step")

            def low_tile(name, m, squares=True):
                c.wait("hi_ready")
                c.up(V.scalar_tensor_tensor(lo(name)[:, m], x[:, m], gain(name, m), hi(name)[:, m].bitcast(f32),
                                            ALU.mult, ALU.subtract), "lo_ready")
                if squares:
                    add_square(m)

            def low_of(name, m, buf):
                c.wait("hi_ready")
                c.up(V.tensor_tensor(lo(name)[:, m], buf[:, m % 2], hi(name)[:, m].bitcast(f32), ALU.subtract),
                     "lo_ready")

            def add_square(m):
                c.wait("sq_ready")
                if m > 1:
                    dve.wait_ge(sem("sq_sum"), c.of("sq_sum").value())
                if m:
                    c.up(V.tensor_tensor(sq[:, 0], sq[:, 0], sq[:, m], ALU.add), "sq_sum")

            def over_rms(dst, u):
                c.up_and_wait(V.tensor_tensor(dst, up[u][:], rstd[:].unsqueeze(1).broadcast_to([P, 2, T]), ALU.mult),
                              "up_free")

            c.up(V.memset(eps, EPS), "eps")
            w = s_work
            lr, li = s_prep[:, 0], s_prep[:, 1]

            def less_whole_turns(dst, src, tmp):
                step(V.tensor_scalar(tmp, src, ROUND, -ROUND, ALU.add, ALU.add))
                step(V.tensor_tensor(dst, src, tmp, ALU.subtract))

            dve.wait_ge(dma["s5_par"], 16)
            c.wait("dt")
            c.up_and_wait(V.tensor_tensor(w[:, 1], lr, w[:, 0], ALU.mult), "s5_mu")
            step(V.tensor_tensor(w[:, 2], li, w[:, 0], ALU.mult))
            step(V.tensor_scalar(w[:, 2], w[:, 2], 1.0 / (2.0 * math.pi), None, ALU.mult))
            less_whole_turns(s_phi, w[:, 2], w[:, 3])
            step(V.tensor_scalar(w[:, 12], s_phi, float(P), None, ALU.mult))
            less_whole_turns(w[:, 12], w[:, 12], w[:, 3])
            c.tell("s5_turn")
            dve.wait_ge(dma["par"], 16)
            step(V.tensor_tensor(tok[:, 0:2], pcol("lam")[:, 0:2], pcol("lam")[:, 2:4], ALU.mult))
            c.up(V.tensor_scalar(sub_g, pcol("subln"), 1.0 - LAM_INIT, None, ALU.mult), "lam_prod")

            def s5_turns(g):
                q = slice(8 * g, 8 * g + 8)
                step(V.tensor_tensor(s_cs[:, q], s_tmat.unsqueeze(1).broadcast_to([P, 8, P]),
                                     s_phi[:, q].unsqueeze(2).broadcast_to([P, 8, P]), ALU.mult))
                less_whole_turns(s_sn[:, q], s_cs[:, q], s_sn[:, q])
                c.tell("s5_frac")

            def s5_cosines(g):
                q = slice(8 * g, 8 * g + 8)
                c.wait("s5_half")
                step(V.tensor_scalar(s_cs[:, q], s_cs[:, q], -2.0, 1.0, ALU.mult, ALU.add))
                c.tell("s5_tables")

            def s5_u_low(g):
                c.wait("u_hi", 2)
                q = slice(2 * g, 2 * g + 2)
                c.up(V.tensor_tensor(lo("s5")[:, q], sq[:, q], hi("s5")[:, q].bitcast(f32), ALU.subtract), "u_lo")

            dve.wait_ge(dma["x"], 16)
            for m in range(KT):
                low_tile("ssm", m, squares=False)
            c.wait("w_hi_ready")
            c.up(V.tensor_tensor(w_lo[:, 0], ring[:, 0], w_hi[:, 0].bitcast(f32), ALU.subtract), "w_ready")
            dve.wait_ge(dma["s5_t"], 16)
            s5_turns(0)
            c.wait("sq_ready", KT)
            for h in (4, 2, 1):
                c.up_and_wait(V.tensor_tensor(sq[:, 0:h], sq[:, 0:h], sq[:, h:2 * h], ALU.add), "sq_sum")
            s5_turns(1)
            c.wait("lam_exp")
            step(V.tensor_tensor(neg_lam, little[:, 4:5], little[:, 3:4], ALU.subtract))
            step(V.tensor_scalar(neg_lam, neg_lam, -LAM_INIT, None, ALU.add))
            for s in range(4):
                if s == 0:
                    c.wait("mag")
                    c.wait("s5_sc", 4)
                    step(V.tensor_tensor(w[:, 6], w[:, 5], w[:, 5], ALU.mult))
                    step(V.tensor_scalar(w[:, 6], w[:, 6], -2.0, 1.0, ALU.mult, ALU.add))
                    step(V.tensor_tensor(w[:, 6], w[:, 6], s_mag, ALU.mult))
                    step(V.tensor_scalar(w[:, 6], w[:, 6], -1.0, None, ALU.add))
                    step(V.tensor_tensor(w[:, 7], w[:, 4], s_mag, ALU.mult))
                    step(V.tensor_tensor(w[:, 8], lr, lr, ALU.mult))
                    step(V.tensor_tensor(w[:, 9], li, li, ALU.mult))
                    step(V.tensor_tensor(w[:, 8], w[:, 8], w[:, 9], ALU.add))
                    step(V.reciprocal(w[:, 8], w[:, 8]))
                    step(V.tensor_tensor(w[:, 9], w[:, 6], lr, ALU.mult))
                    step(V.tensor_tensor(w[:, 10], w[:, 7], li, ALU.mult))
                    step(V.tensor_tensor(w[:, 9], w[:, 9], w[:, 10], ALU.add))
                    step(V.tensor_tensor(w[:, 9], w[:, 9], w[:, 8], ALU.mult))
                    step(V.tensor_tensor(w[:, 10], w[:, 7], lr, ALU.mult))
                    step(V.tensor_tensor(w[:, 11], w[:, 6], li, ALU.mult))
                    step(V.tensor_tensor(w[:, 10], w[:, 10], w[:, 11], ALU.subtract))
                    step(V.tensor_tensor(w[:, 10], w[:, 10], w[:, 8], ALU.mult))
                    step(V.tensor_tensor(w[:, 13], w[:, 13], w[:, 13], ALU.mult))
                    step(V.tensor_scalar(s_e[:, 0], w[:, 13], -2.0, 1.0, ALU.mult, ALU.add))
                    step(V.tensor_scalar(s_e[:, 1], s_e[:, 2], -1.0, None, ALU.mult))
                    c.tell("s5_f")
                    c.wait("rstd")
                if s == 2:
                    s5_turns(2)
                    s5_turns(3)
                dve.wait_ge(sem("mm_done"), START["w_in"] + s + 1)
                over_rms(sq[:, 2 * s:2 * s + 2], s % 2)
                if s == 2:
                    s5_cosines(0)
                    s5_cosines(1)
                    s5_u_low(0)
                    s5_u_low(1)
                    s5_cosines(2)
                    c.wait("b_hi")
                    c.up(V.tensor_tensor(b_lo, s_b, b_hi.bitcast(f32), ALU.subtract), "b_lo")
            s5_cosines(3)

            def s5_products(n):
                c.wait("s5_bu")
                if n:
                    c.wait("s5_sum", 2)
                if n >= 3:
                    c.wait("s5_out_pool", 2)
                bu = acc[:, 2 * (n % 2):2 * (n % 2) + 2].rearrange("p e (k t) -> p e k t", t=P)
                c.up(V.tensor_tensor(by_chunk(s_m[:, n % 3]), local(s_cs, n, 4), bu, ALU.mult), "s5_prod")
                c.up(V.tensor_tensor(by_chunk(s_m[:, 3]), local(s_sn, n, 4), bu, ALU.mult), "s5_prod")

            def s5_scans(n):
                z = s_m[:, n % 3]

                def scans(chunk):
                    q = slice(chunk * P, chunk * P + P)
                    for e in range(2):
                        r = s_mag[:, 2 * n + e:2 * n + e + 1].broadcast_to([P, P])
                        for k in range(2):
                            ins = V.tensor_tensor_scan(z[:, e, k, q], r, z[:, e, k, q],
                                                       s_init[:, e, k:k + 1] if chunk else 0.0, ALU.mult, ALU.add)
                            c.up(ins, "s5_scanned")
                    dve.wait_ge(sem("s5_scanned"), c.of("s5_scanned").value())

                scans(0)
                end = z[:, :, :, P - 1]
                turn = s_e[:, :, 2 * n:2 * n + 2]
                c.up(V.tensor_tensor(s_t[:, 0], end, turn[:, 0].unsqueeze(2).broadcast_to([P, 2, 2]), ALU.mult), "dve_step")
                step(V.tensor_tensor(s_t[:, 1], end, turn[:, 1:3].rearrange("p k e -> p e k"), ALU.mult))
                c.up(V.tensor_tensor(s_init[:, :, 0], s_t[:, 0, :, 0], s_t[:, 1, :, 1], ALU.add), "dve_step")
                step(V.tensor_tensor(s_init[:, :, 1], s_t[:, 0, :, 1], s_t[:, 1, :, 0], ALU.add))
                scans(1)
                c.tell("s5_scan")

            def s5_back(n):
                if n:
                    c.wait("s5_y")
                for e in range(2):
                    c.up(V.scalar_tensor_tensor(chunks(s_p[:, 1, e, 0].unsqueeze(1))[:, 0],
                                                chunks(s_m[:, n % 3, e, 0].unsqueeze(1))[:, 0], -1.0,
                                                local(s_sn, n, 2)[:, e], ALU.mult, ALU.mult), "s5_out_dve")

            def s5_output(m):
                dve.wait_ge(sem("s5_y"), 2 * m + 2)
                c.up_and_wait(V.scalar_tensor_tensor(s_y[:, 0], sq[:, m], pcol("dskip", m, 1), aux[m % 2][:, 0:T],
                                                     ALU.mult, ALU.add), "s5_ysum")

            def s5_low(m):
                c.wait("hi_ready")
                c.up(V.tensor_tensor(lo("s5")[:, m], s_y[:, 1], hi("s5")[:, m].bitcast(f32), ALU.subtract), "lo_ready")

            for n in range(2 * KT + 1):
                if n < 2 * KT:
                    s5_products(n)
                else:
                    c.wait("s5_sum", 2)
                if n:
                    s5_scans(n - 1)
                    if n == 1:
                        c.wait("s5_c_ready", 2)
                    s5_back(n - 1)
                if n in (3, 5):
                    s5_u_low(n // 2 + 1)
                if n >= 4 and n % 2 == 0:
                    s5_output(n // 2 - 2)
                if n >= 5 and n % 2:
                    s5_low(n // 2 - 2)
            s = START["glu"]
            c.wait("w_hi_ready", 4)
            c.up(V.tensor_tensor(w_lo[:, s % SPLIT], ring[:, s % RING], w_hi[:, s % SPLIT].bitcast(f32), ALU.subtract),
                 "w_ready")
            s5_low(KT - 2)
            s5_output(KT - 1)
            s5_low(KT - 1)

            for m in range(KT):
                c.wait("gated")
                step(V.tensor_tensor(f_h[:, 0], up[m % 2][:, 0], f_gg[:, 0], ALU.mult))
                c.tell("up_free")
                c.up_and_wait(V.tensor_tensor(x[:, m], x[:, m], f_h[:, 0], ALU.add), "x_ready")
                if m:
                    low_tile("ffn0", m - 1)
            low_tile("ffn0", KT - 1)

            def ffn(l, end):
                S = START[f"ffn{l}"]
                conv = l < 2
                if conv:
                    for t in range(2):
                        step(V.memset(f_u[:, t, 0:2], 0.0))
                c.wait("rstd")

                def tile(s, k, u, i, n, parity, part):
                    dve.wait_ge(sem("mm_done"), s + k + 1 if i is None else i * 6 + (s + k + 1))
                    us = f_u[:, 0:2, 2:258]
                    if conv:
                        over_rms(us, u)
                        for t in range(2):
                            base = COLS["conv"][0] + (l * 22 * 8)
                            pr = par[:, base:base + 176].rearrange("p (n w) -> p n w", w=8)
                            if i is None:
                                w4 = [pr[:, n, 4 * t + q:4 * t + q + 1] for q in range(4)]
                            else:
                                w4 = [pr[:, bass.ds(i * 4 + n, 1), 4 * t + q:4 * t + q + 1].rearrange("p a b -> p (a b)")
                                      for q in range(4)]
                            step(V.tensor_scalar(f_c[:, t], f_u[:, t, 2:258], w4[2], w4[3], ALU.mult, ALU.add))
                            step(V.scalar_tensor_tensor(f_c[:, t], f_u[:, t, 1:257], w4[1], f_c[:, t], ALU.mult, ALU.add))
                            ins = V.scalar_tensor_tensor(f_c[:, t], f_u[:, t, 0:256], w4[0], f_c[:, t], ALU.mult, ALU.add)
                            if t == 0:
                                c.up_and_wait(ins, "g_ready")
                            else:
                                step(ins)
                        val = f_c[:, 1]
                    else:
                        over_rms(us, u)
                        c.tell("g_ready")
                        val = f_u[:, 1, 2:258]
                    c.wait("gated")
                    step(V.tensor_tensor(f_h[:, 0], f_gg[:, 0], val, ALU.mult))
                    hh, hl = opnd[1][:, 0, 2 * parity + part], opnd[1][:, 1, 2 * parity + part]
                    step(V.tensor_copy(hh, f_h[:, 0]))
                    c.up_and_wait(V.tensor_tensor(hl, f_h[:, 0], hh.bitcast(f32), ALU.subtract), "h_ready")

                up0 = BANK[f"ffn{l}"]
                for j in range(3):
                    for part in range(2):
                        s = S + part if j == 0 else S + 3 * j - 1 + part
                        tile(s, 0, (up0 + part) % 2, None, 2 * j + part, j % 2, part)
                with dve.Fori(0, 4) as i:
                    c.enter(i, **(dict(dve_step=28, up_free=4, g_ready=4, gated=4, h_ready=4) if conv
                                  else dict(dve_step=8, up_free=4, g_ready=4, gated=4, h_ready=4)))
                    for j in (3, 4):
                        for part in range(2):
                            tile(S + 8, 3 * (j - 3) + part, (up0 + part) % 2, i, 2 * j + part, j % 2, part)
                    c.leave(4)
                for m in range(KT):
                    if m % 2 == 0:
                        c.wait("acc_bank") if m < KT - 2 else dve.wait_ge(sem("mm_done"), S + 33)
                    c.up_and_wait(V.tensor_tensor(x[:, m], x[:, m], acc[:, m // 2, (m % 2) * T:(m % 2) * T + T],
                                                  ALU.add), "x_ready")
                    if m and end:
                        low_tile(end, m - 1)
                if end:
                    low_tile(end, KT - 1)

            def pe_operand():
                for k in range(2):
                    c.wait("pe_hi")
                    c.up(V.tensor_tensor(opnd[1][:, 1, 6 + k], f_pe[:, k], opnd[1][:, 0, 6 + k].bitcast(f32),
                                         ALU.subtract), "pe_ready")

            def ple(l, ends):
                S = START[f"ple{l}"]
                u0 = BANK[f"ple{l}"]
                c.wait("rstd")
                for g in range(4):
                    b = 2 * (g % 2)
                    dve.wait_ge(sem("mm_done"), S + g + 2)
                    over_rms(f_u[:, b:b + 2, 2:258], (u0 + g) % 2)
                    c.tell("ple_u")
                    c.wait("gated")
                    step(V.tensor_tensor(f_c[:, b:b + 2], f_c[:, b:b + 2],
                                         acc[:, g].rearrange("p (a t) -> p a t", a=2), ALU.mult))
                    for e in range(2):
                        m = 2 * g + e
                        c.up_and_wait(V.tensor_tensor(x[:, m], x[:, m], f_c[:, b + e], ALU.add), "x_ready")
                        if m:
                            low_tile(ends[0], m - 1)
                low_tile(ends[0], KT - 1)
                c.tell("mix_free")
                for name in ends[1:]:
                    for m in range(KT):
                        low_tile(name, m, squares=False)

            def residual(name, S, u0):
                for g in range(4):
                    dve.wait_ge(sem("mm_done"), S + g + 1)
                    for e in range(2):
                        m = 2 * g + e
                        c.up_and_wait(V.tensor_tensor(x[:, m], x[:, m], up[(u0 + g) % 2][:, e], ALU.add), "x_ready")
                        if m:
                            low_tile(name, m - 1)
                    c.tell("up_free")
                low_tile(name, KT - 1)

            def values(s, u, dst, n):
                dve.wait_ge(sem("mm_done"), s + 1)
                for t in range(TT):
                    step(V.tensor_scalar(dst[:, t], up[u][:, t, 0:n], tok[:, 2 + t:3 + t], None, ALU.mult))

            def head_raw(n, s, u, tmp):
                dve.wait_ge(sem("mm_done"), s + 1)
                over_rms(tmp[:, n % 3].rearrange("p (a t) -> p a t", a=2), u)
                c.tell("hn_raw")

            def head_low(n, sqb, sq_r):
                c.wait("hn_sq")
                c.up(V.tensor_tensor(sq_r[:, 1], sqb[:, n % 2], sq_r[:, 0].bitcast(f32), ALU.subtract), "hn_lo")

            def softmax_head(n, lbuf, st, bias):
                nk = P * (n % 2 + 1)
                b = n % 2
                L = lbuf[:, b].rearrange("p (c k) -> p c k", c=2)[:, :, 0:nk]
                c.wait("scores")
                S2 = acc[:, 2 * b:2 * b + 2, 0:nk]
                c.up_and_wait(V.scalar_tensor_tensor(L, S2, HD ** -0.5, bias.unsqueeze(1).broadcast_to([P, 2, nk]),
                                                     ALU.mult, ALU.add), "scores_read")
                c.up(V.tensor_reduce(st[:, 40 + 2 * b:42 + 2 * b], L, AX.X, ALU.max, negate=True), "neg_max")

            def softmax_tail(n, lbuf, abuf, st, diff):
                nk = P * (n % 2 + 1)
                b = n % 2
                L = lbuf[:, b].rearrange("p (c k) -> p c k", c=2)[:, :, 0:nk]
                c.wait("exps", 2)
                if n >= 2:
                    c.wait("at_ps")
                r = st[:, 48 + 2 * b:50 + 2 * b]
                step(V.reciprocal(r, st[:, 44 + 2 * b:46 + 2 * b]))
                if diff:
                    step(V.tensor_scalar(L[:, 1], L[:, 1], r[:, 1:2], neg_lam, ALU.mult, ALU.mult))
                    c.up(V.scalar_tensor_tensor(abuf[:, b, 0:nk], L[:, 0], r[:, 0:1], L[:, 1], ALU.mult, ALU.add),
                         "probs")
                else:
                    ab = abuf[:, b].rearrange("p (c k) -> p c k", c=2)
                    step(V.tensor_scalar(ab[:, 0, 0:nk], L[:, 0], r[:, 0:1], None, ALU.mult))
                    c.up(V.tensor_scalar(ab[:, 1, 0:nk], L[:, 1], r[:, 1:2], None, ALU.mult), "probs")
                dve.wait_ge(sem("probs"), c.of("probs").value())

            pe_operand()
            ffn(0, "ple0")
            ple(0, ["kv", "q"])

            S, u0 = START["kvq"], BANK["kvq"]
            c.wait("rstd_tok")
            for g in range(4):
                values(S + g, (u0 + g) % 2, d_v[:, :, g * 256:(g + 1) * 256], 256)
                c.tell("up_free")
                if g == 1:
                    c.wait("bias_ps")
                    c.up(V.tensor_copy(d_row, aux[0][0:HEADS, 0:384]), "bias_sb")
            c.wait("rstd")

            def diff_normed(n):
                c.wait("hn_rstd")
                dst = (d_k if n % 2 == 0 else d_q)[:, 2 * (n // 2):2 * (n // 2) + 2]
                c.up_and_wait(V.scalar_tensor_tensor(dst, d_tmp[:, n % 3].rearrange("p (a t) -> p a t", a=2),
                                                     pcol("qk", n % 2, 1),
                                                     d_sq[:, n % 2].rearrange("p (a t) -> p a t", a=2),
                                                     ALU.mult, ALU.mult), "qk_ready")

            for n in range(8):
                if n < 8:
                    head_raw(n, S + 4 + n, (u0 + 4 + n) % 2, d_tmp)
                if n >= 2:
                    diff_normed(n - 2)
                if n < 8:
                    head_low(n, d_sq, d_sq_r)
            dve.wait_ge(dma["bias_r"], 16)
            for n in range(2 * HEADS + 10):
                if n < 2 * HEADS:
                    h = n // 2
                    bias = d_bias[:, h, 0:T] if n % 2 else d_bias[:, h, P:T]
                    softmax_head(n, d_l, d_st, bias)
                if 1 <= n <= 2 * HEADS:
                    softmax_tail(n - 1, d_l, d_a, d_st, True)
                if n in (4, 6):
                    diff_normed(4 + n // 2)
                if n % 2 == 0 and 10 <= n < 2 * HEADS + 10:
                    h = (n - 10) // 2
                    c.wait("o_raw")
                    c.wait("o_rstd")
                    c.up(V.tensor_tensor(sq[:, h], sq[:, h], d_q[:, h], ALU.mult), "o_norm")
                if n % 2 and n >= 11:
                    h = (n - 11) // 2
                    dve.wait_ge(sem("o_norm"), h + 1)
                    c.wait("hi_ready")
                    c.up(V.scalar_tensor_tensor(lo("diff")[:, h], sq[:, h], sub_g, hi("diff")[:, h].bitcast(f32),
                                                ALU.mult, ALU.subtract), "lo_ready")
            c.wait("at_ps", 2)
            residual("ffn1", START["wo"], BANK["wo"])

            pe_operand()
            ffn(1, "ple1")
            ple(1, ["even"])

            S, u0 = START["evin"], BANK["evin"]
            c.wait("rstd_tok")
            dve.wait_ge(sem("mm_done"), S + 1)
            for t in range(TT):
                step(V.tensor_scalar(e_v[:, t], up[u0 % 2][:, t, 0:P], tok[:, 2 + t:3 + t], None, ALU.mult))
                step(V.tensor_scalar(e_w[:, t], up[u0 % 2][:, t, P:P + 4], tok[:, 2 + t:3 + t], 1.0 / 16,
                                     ALU.mult, ALU.mult))
            c.tell("up_free")
            c.wait("rstd")

            def even_normed(n):
                c.wait("hn_rstd")
                src = e_tmp[:, n % 3].rearrange("p (a t) -> p a t", a=2)
                bc = e_sq[:, n % 2].rearrange("p (a t) -> p a t", a=2)
                if n == 0:
                    c.up_and_wait(V.scalar_tensor_tensor(e_k, src[:, 0], pcol("evqk", 0, 1), bc[:, 0],
                                                         ALU.mult, ALU.mult), "qk_ready")
                else:
                    c.up_and_wait(V.scalar_tensor_tensor(e_q[:, 2 * n - 2:2 * n], src, pcol("evqk", 1, 1), bc,
                                                         ALU.mult, ALU.mult), "qk_ready")

            def pooled_slot(g):
                dve.wait_ge(sem("mm_done"), S + 6 + g)
                over_rms(e_u[:, 2 * g:2 * g + 2, 16:], (u0 + 5 + g) % 2)
                c.tell("pool_in")

            e_relu = e_at.rearrange("p a b -> p (a b)").rearrange("p (q h k) -> p q h k", q=2, h=4)

            def index(qb, between):
                nk = P * (qb + 1)
                sc = e_mask[:, qb, 0:nk]
                c.wait("idx_relu")
                for h in range(4):
                    step(V.scalar_tensor_tensor(sc, e_relu[:, qb, h, 0:nk], e_w[:, qb, h:h + 1],
                                                sc if h else e_causal[:, qb, 0:nk], ALU.mult, ALU.add))
                if -1 in between:
                    between[-1]()
                for r in range(SEL // 8):
                    step(V.max(e_m8, sc))
                    step(V.match_replace(sc, e_m8, sc, TAKEN))
                    if r in between:
                        between[r]()
                step(V.tensor_scalar(sc, sc, TAKEN / 2, NEG, ALU.is_gt, ALU.mult))
                step(V.tensor_tensor(sc, sc, e_causal[:, qb, 0:nk], ALU.add))

            def raw(n, s):
                head_raw(n, S + s, (u0 + s) % 2, e_tmp)

            def low(n):
                head_low(n, e_sq, e_sq_r)

            raw(0, 1)
            step(V.tensor_copy(e_pl[:, 0], e_tmp[:, 0, T:2 * T]))
            low(0)
            for b in (e_u, e_pa):
                step(V.memset(b[:, :, 0:16], 0.0))
            dve.wait_ge(sem("mm_done"), S + 3)
            over_rms(e_pl[:, 1:3], (u0 + 2) % 2)
            c.tell("idx_ready")
            dve.wait_ge(dma["causal"], 48)
            index(0, {4: lambda: raw(1, 3), 7: lambda: low(1)})
            even_normed(0)
            index(1, {-1: lambda: raw(2, 4), 1: lambda: low(2), 3: lambda: even_normed(1), 5: lambda: pooled_slot(0)})
            even_normed(2)
            step(V.memset(e_pb[:, :, 0:16], 0.0))
            pooled_slot(1)
            for n in range(8 + 4):
                if n < 8:
                    softmax_head(n, e_l, e_st, e_mask[:, n % 2, 0:P * (n % 2 + 1)])
                if 1 <= n <= 8:
                    softmax_tail(n - 1, e_l, e_a, e_st, False)
                if n >= 7 and n % 2:
                    low_of("mixed", (n - 7) // 2, e_out)
            for m in range(3, KT):
                low_of("mixed", m, e_out)
            residual("ffn2", START["evout"], BANK["evout"])

            ffn(2, "odd")
            c.tell("mix_free")

            S, u0 = START["qkv"], BANK["qkv"]
            c.wait("rstd_tok")
            for g in range(4):
                values(S + g, (u0 + g) % 2, k_v[:, :, g * 256:(g + 1) * 256], 256)
                c.tell("up_free")
            c.wait("rstd")
            for n in range(8):
                dve.wait_ge(sem("mm_done"), S + 5 + n)
                dst = (k_k if n % 2 == 0 else k_q)[:, 2 * (n // 2):2 * (n // 2) + 2]
                over_rms(dst, (u0 + 4 + n) % 2)
                c.tell("stick_qk")
            dve.wait_ge(dma["stickmask"], 32)
            for n in range(STICKS + 3):
                if n < STICKS:
                    c.wait("z_ps")
                    if n >= 6:
                        c.wait("a_sb")
                    c.up(V.scalar_tensor_tensor(k_z[:, n % 6], acc[:, n % 2, 0:384], HD ** -0.5, k_mask,
                                                ALU.mult, ALU.add), "z_sb")
                if n >= 3:
                    h = n - 3
                    c.wait("remain")
                    c.up(V.tensor_tensor(k_z[:, h % 6], k_z[:, h % 6], acc[:, 2 + h % 2, 0:384], ALU.subtract),
                         "log_a")
                if n < STICKS:
                    dve.wait_ge(sem("z_sb"), n + 1)
                    c.up(V.scalar_tensor_tensor(k_t[:, n % 2], k_z[:, n % 6], -1.0, k_z[:, n % 6], ALU.mult, ALU.max),
                         "z_abs")
                if 1 <= n <= STICKS:
                    c.wait("log1p")
                    h = n - 1
                    c.up(V.scalar_tensor_tensor(k_b[:, h % 2], k_z[:, h % 6], 0.0, k_t[:, h % 2], ALU.max, ALU.add),
                         "brk")
                if n >= 7 and n % 2:
                    low_of("stick", (n - 7) // 2, k_out)
            low_of("stick", 6, k_out)
            low_of("stick", 7, k_out)
            residual("ffn3", START["out"], BANK["out"])
            ffn(3, None)

        @block.tensor
        def _(pe):
            c = Counts(pe, sem)
            MM = nc.tensor.matmul
            used = [0]

            def slot_ready(s, i=None):
                pe.wait_ge(sem("w_ready"), s + 1 if i is None else i * 6 + (s + 1))

            def bank(i=None, loop_uses=0):
                u = used[0]
                used[0] += 1
                if u >= 2:
                    pe.wait_ge(sem("up_free"), u - 1 if i is None else i * 4 + (u - 1))
                return up[u % 2]

            def three(o, l_hi, l_lo, r_hi, r_lo, start, stop):
                MM(o, l_hi, r_hi, start=start, stop=False, skip_group_check=True)
                MM(o, l_lo, r_hi, start=False, stop=False, skip_group_check=True)
                return MM(o, l_hi, r_lo, start=False, stop=stop, skip_group_check=True)

            def up_slot(name, s, i=None, fresh=False, tiles=2):
                slot_ready(s, i)
                o = bank(i)
                b = s % SPLIT
                for k in range(KT):
                    if fresh:
                        c.wait("hi_ready")
                        c.wait("lo_ready")
                    for m in range(tiles):
                        w = slice((2 * k + m) * P, (2 * k + m + 1) * P)
                        ins = three(o[:, m], w_hi[:, b, w], w_lo[:, b, w], hi(name)[:, k], lo(name)[:, k],
                                    k == 0 and m == 0, k == KT - 1)
                c.up(ins, "mm_done")

            def begin_slot(s):
                slot_ready(s)
                return bank()

            def slot_part(name, s, o, ks):
                b = s % SPLIT
                for k in ks:
                    c.wait("hi_ready")
                    c.wait("lo_ready")
                    for m in range(2):
                        w = slice((2 * k + m) * P, (2 * k + m + 1) * P)
                        ins = three(o[:, m], w_hi[:, b, w], w_lo[:, b, w], hi(name)[:, k], lo(name)[:, k],
                                    k == 0 and m == 0, k == KT - 1)
                if ks[-1] == KT - 1:
                    c.up(ins, "mm_done")

            def token_slot(name, s, fresh=False):
                slot_ready(s)
                o = bank()
                b = s % SPLIT
                for k in range(KT):
                    if fresh:
                        c.wait("hi_ready")
                        c.wait("lo_ready")
                    for t in range(TT):
                        w = slice(2 * k * P, (2 * k + 2) * P)
                        q = slice(t * P, (t + 1) * P)
                        ins = three(o[:, t], hi(name)[:, k, q], lo(name)[:, k, q], w_hi[:, b, w], w_lo[:, b, w],
                                    k == 0 and t == 0, k == KT - 1)
                c.up(ins, "mm_done")

            def down_slot(s, ops, first, last, i=None, each=False, added=None):
                slot_ready(s, i)
                b = s % SPLIT
                for m in range(KT):
                    if added is not None and m % 2 == 0:
                        pe.wait_ge(sem("x_ready"), added + m + 2)
                    for k in range(2):
                        w = slice((8 * k + m) * P, (8 * k + m + 1) * P)
                        ins = three(acc[:, m // 2, (m % 2) * T:(m % 2) * T + T], w_hi[:, b, w], w_lo[:, b, w],
                                    opnd[1][:, 0, ops + k], opnd[1][:, 1, ops + k],
                                    first and k == 0 and m % 2 == 0, last and k == 1)
                    if each and m % 2 and m < KT - 1:
                        c.up(ins, "acc_bank")
                return ins

            def rms(tokens=False, adds=KT - 1):
                c.wait("sq_sum", adds)
                ins = MM(aux[1][:, 0:T], ones, sq[:, 0], start=True, stop=True)
                if tokens:
                    for t in range(TT):
                        ins = MM(aux[0][:, t:t + 1], sq[:, 0, t * P:(t + 1) * P], ones[:, 0:1], start=True, stop=True)
                c.up(ins, "ssq")

            pe.wait_ge(dma["par"], 16)
            c.wait("lam_prod")
            c.up(MM(aux[1][:, 0:2], ones, tok[:, 0:2], start=True, stop=True), "lam_sum")

            S = START["w_in"]
            up_slot("ssm", S, fresh=True)
            c.wait("lam_exp")
            rms(adds=3)
            up_slot("ssm", S + 1)
            up_slot("ssm", S + 2)
            up_slot("ssm", S + 3)
            c.wait("b_lo")

            def s5_in(n):
                m, b = n // 2, n % 2
                if n % 4 == 0:
                    c.wait("u_lo")
                if n >= 2:
                    c.wait("s5_prod", 2)
                for e in range(2):
                    r = slice(32 * (2 * b + e), 32 * (2 * b + e) + 32)
                    for k in range(2):
                        ins = three(acc[:, 2 * b + e, k * T:(k + 1) * T], b_hi[r, k, m], b_lo[r, k, m],
                                    hi("s5")[r, m], lo("s5")[r, m], True, True)
                c.up(ins, "s5_bu")

            def s5_out(n):
                m, b = n // 2, n % 2
                c.wait("s5_out_pool")
                if n % 2 == 0 and m >= 2:
                    c.wait("s5_ysum")
                for part, order in ((0, (0, 1)), (1, (1, 0))):
                    for e in range(2):
                        q = 2 * b + e
                        for k in range(2):
                            ins = MM(aux[m % 2][32 * q:32 * q + 32, 0:T], s_c[:, order[k], 2 * n + e],
                                     s_p[:, part, e, k], start=(part == 0 and k == 0), stop=(part == 1 and k == 1),
                                     tile_position=(0, 32 * q), skip_group_check=True)
                    if part == 0:
                        c.up(ins, "s5_y_cos")
                        c.wait("s5_out_dve", 2)
                        c.wait("s5_out_pool")
                c.up(ins, "s5_y")

            s5_in(0)
            s5_in(1)
            for n in range(2 * KT + 1):
                if n + 2 < 2 * KT:
                    s5_in(n + 2)
                if n == 1:
                    c.wait("s5_c_ready", 2)
                if n == 2 * KT:
                    o = begin_slot(START["glu"])
                    slot_part("s5", START["glu"], o, range(4))
                if n:
                    s5_out(n - 1)
            S = START["glu"]
            slot_part("s5", S, o, range(4, KT))
            for m in range(1, KT):
                up_slot("s5", S + m)

            def ffn(l, name):
                S = START[f"ffn{l}"]
                assert used[0] == BANK[f"ffn{l}"]
                up_slot(name, S, fresh=True)
                rms()
                up_slot(name, S + 1)
                up_slot(name, S + 2)
                up_slot(name, S + 3)

                def down(s, parity, first=False, last=False, i=None, each=False):
                    c.wait("h_ready", 2)
                    ins = down_slot(s, 2 * parity, first, last, i, each)
                    c.up(ins, "mm_done")

                down(S + 4, 0, first=True)
                up_slot(name, S + 5)
                up_slot(name, S + 6)
                down(S + 7, 1)
                with pe.Fori(0, 4) as i:
                    c.enter(i, h_ready=4, mm_done=6)
                    for k in (0, 3):
                        up_slot(name, S + 8 + k, i)
                        up_slot(name, S + 9 + k, i)
                        down(S + 10 + k, k // 3, i=i)
                    c.leave(4)
                used[0] += 3 * 4
                down(S + 32, 0, last=True, each=True)

            def ple(l):
                S = START[f"ple{l}"]
                assert used[0] == BANK[f"ple{l}"]
                c.wait("pe_ready", 2)
                ins = down_slot(S, 6, True, True, added=8 * (1 + 3 * l))
                c.up(ins, "mm_done")
                for g in range(4):
                    up_slot(f"ple{l}", S + g + 1, fresh=(g == 0))
                    if g == 0:
                        rms()

            def head_stats(n, sq_r, half_r, banks):
                c.wait("hn_sq")
                c.wait("hn_lo")
                if n >= 2:
                    c.wait("hn_ln")
                MM(banks[n % 2], half_r, sq_r[:, 0], start=True, stop=False, skip_group_check=True)
                c.up(MM(banks[n % 2], half_r, sq_r[:, 1], start=False, stop=True, skip_group_check=True), "hn_ssq")

            def transposes(n, abuf, per):
                nk = n % 2 + 1
                c.wait("probs")
                if n >= 2:
                    c.wait("at_sb", per)
                for j in range(per):
                    for k in range(nk):
                        o = 4 // per * j + k
                        ins = nc.tensor.transpose(up[n % 2][:, o // 2, (o % 2) * P:(o % 2 + 1) * P],
                                                  abuf[:, n % 2, j * T + k * P:j * T + (k + 1) * P], ident)
                c.up(ins, "at_ps")

            def head_values(h, o, v, at, rows):
                MM(o[:, 0:T], v[:, 0], at[:, 0:T], start=True, stop=False, skip_group_check=True)
                return MM(o[:, P:T], v[:, 1], at[:, T + P:2 * T], start=False, stop=True, skip_group_check=True)

            ffn(0, "ffn0")
            ple(0)

            S = START["kvq"]
            assert used[0] == BANK["kvq"]
            token_slot("kv", S, fresh=True)
            rms(True)
            token_slot("kv", S + 1)
            pe.wait_ge(dma["bias_oh"], 16)
            c.wait("rstd_tok")
            c.up(MM(aux[0][0:HEADS, 0:384], d_oh[:, 384:384 + HEADS], d_oh[:, 0:384], start=True, stop=True), "bias_ps")
            token_slot("kv", S + 2)
            token_slot("kv", S + 3)
            c.wait("hi_ready", 8)
            c.wait("lo_ready", 8)
            c.wait("half_r")
            def diff_scores(n):
                h, qb = n // 2, n % 2
                if n >= 2:
                    c.wait("scores_read")
                for e in range(2):
                    r = slice(HD * e, HD * e + HD)
                    ins = MM(acc[:, 2 * (n % 2) + e, 0:P * (qb + 1)], d_q[r, h, qb * P:(qb + 1) * P],
                             d_k[r, h, 0:P * (qb + 1)], start=True, stop=True)
                c.up(ins, "scores")

            for n in range(8 + 1):
                if n < 8:
                    up_slot("kv" if n % 2 == 0 else "q", S + 4 + n)
                if n == 8:
                    c.wait("qk_ready", 6)
                    for k in range(2):
                        diff_scores(k)
                if n >= 1:
                    head_stats(n - 1, d_sq_r, d_half_r, [aux[0][:], aux[1][:]])

            def diff_values(h):
                pe.wait_ge(sem("at_sb"), 2 * h + 2)
                if h >= 2:
                    pe.wait_ge(sem("o_ln"), h - 1)
                ins = head_values(h, aux[h % 2], d_v[:, :, h * P:(h + 1) * P], d_at[:, h % 2], P)
                c.up(ins, "pv")

            for n in range(2 * HEADS + 7):
                if n == 2 * 6:
                    c.wait("qk_ready", 2)
                if 2 <= n < 2 * HEADS:
                    diff_scores(n)
                if n == 6:
                    c.wait("hn_ln", 2)
                if n == 19:
                    c.wait("at_sb", 2)
                    o = begin_slot(START["wo"])
                if 19 <= n < 23:
                    slot_part("diff", START["wo"], o, [n - 19])
                if 3 <= n < 2 * HEADS + 3:
                    transposes(n - 3, d_a, 1)
                if n % 2 == 0 and n >= 8:
                    h = n // 2 - 4
                    c.wait("o_sq")
                    c.up(MM(aux[h % 2][:, T:2 * T], ones, d_q[:, h], start=True, stop=True), "o_ssq")
                if n % 2 == 0 and 6 <= n < 2 * HEADS + 6:
                    diff_values(n // 2 - 3)
            c.wait("scores_read", 2)
            S = START["wo"]
            slot_part("diff", S, o, range(4, KT))
            for g in range(1, 4):
                up_slot("diff", S + g)

            ffn(1, "ffn1")
            ple(1)

            S = START["evin"]
            assert used[0] == BANK["evin"]
            token_slot("even", S, fresh=True)
            rms(True)
            banks = [aux[0][:], aux[1][:]]
            up_slot("even", S + 1)
            up_slot("even", S + 2)
            c.wait("half_r")
            head_stats(0, e_sq_r, e_half_r, banks)

            def index_scores(qb):
                c.wait("idx_relu" if qb else "idx_ready")
                for h in range(4):
                    r = slice(HD * (h % 2), HD * (h % 2) + HD)
                    ins = MM(acc[:, h, 0:P * (qb + 1)],
                             e_pl[r, 1 + h // 2, qb * P:(qb + 1) * P], e_pl[r, 0, 0:P * (qb + 1)],
                             start=True, stop=True)
                c.up(ins, "idx_ps")

            index_scores(0)
            up_slot("even", S + 3)
            index_scores(1)
            up_slot("even", S + 4)
            head_stats(1, e_sq_r, e_half_r, banks)
            up_slot("even", S + 5)
            up_slot("even", S + 6)
            head_stats(2, e_sq_r, e_half_r, banks)
            c.wait("hn_ln", 2)
            c.wait("idx_relu")
            c.wait("qk_ready", 3)
            pe.wait_ge(sem("up_free"), BANK["evout"])

            def even_scores(n):
                h, qb = n // 2, n % 2
                if n >= 2:
                    c.wait("scores_read")
                for e in range(2):
                    r = slice(HD * e, HD * e + HD)
                    ins = MM(acc[:, 2 * (n % 2) + e, 0:P * (qb + 1)], e_q[r, h, qb * P:(qb + 1) * P],
                             e_k[r, 0:P * (qb + 1)], start=True, stop=True)
                c.up(ins, "scores")

            at0 = 2 * HEADS
            for n in range(8 + 4):
                if n < 8:
                    even_scores(n)
                if 3 <= n < 11:
                    transposes(n - 3, e_a, 2)
                if n == 11:
                    c.wait("at_sb", 4)
                    o = begin_slot(START["evout"])
                    slot_part("mixed", START["evout"], o, range(2))
                if n >= 5 and n % 2:
                    h = (n - 5) // 2
                    pe.wait_ge(sem("at_sb"), at0 + 4 * (h + 1))
                    if h >= 2:
                        pe.wait_ge(sem("hi_ready"), KT * UNIT["mixed"] + h - 1)
                    for e in range(2):
                        v = aux[h % 2][HD * e:HD * e + HD]
                        at = e_at[:, 2 * (h % 2) + e]
                        MM(v[:, 0:T], e_v[:, 0, HD * e:HD * e + HD], at[:, 0:T], start=True, stop=False,
                           tile_position=(0, HD * e), skip_group_check=True)
                        ins = MM(v[:, P:T], e_v[:, 1, HD * e:HD * e + HD], at[:, T + P:2 * T], start=False, stop=True,
                                 tile_position=(0, HD * e), skip_group_check=True)
                    c.up(ins, "pv")
                if n == 9:
                    c.wait("scores_read", 2)
                    c.wait("pooled")
                    for m in range(4):
                        c.up(MM(acc[:, m, 0:T], e_pw[:, m], e_cnt[:, m], start=True, stop=True), "pool_ps")
            S = START["evout"]
            slot_part("mixed", S, o, range(2, KT))
            for g in range(1, 4):
                up_slot("mixed", S + g)

            ffn(2, "ffn2")

            S = START["qkv"]
            assert used[0] == BANK["qkv"]
            token_slot("odd", S, fresh=True)
            rms(True)
            token_slot("odd", S + 1)
            token_slot("odd", S + 2)
            token_slot("odd", S + 3)
            for n in range(8):
                up_slot("odd", S + 4 + n)
            pe.wait_ge(dma["stickmask"], 32)
            c.wait("stick_qk", 8)
            first = begin_slot(START["out"])
            for n in range(STICKS + 4):
                for h in ((0, 1) if n == 0 else (n + 1,)):
                    if h < STICKS:
                        m, r = h // 2, slice(HD * (h % 2), HD * (h % 2) + HD)
                        if h >= 2:
                            c.wait("z_sb")
                        MM(acc[:, h % 2, 0:T], k_k[r, m, 0:P], k_q[r, m, 0:T], start=True, stop=True)
                        c.up(MM(acc[:, h % 2, T:T + P], k_k[r, m, P:T], k_q[r, m, P:T], start=True, stop=True), "z_ps")
                if n >= 8 and n % 2 == 0:
                    slot_part("stick", START["out"], first, [n // 2 - 4])
                if 2 <= n < STICKS + 2:
                    h = n - 2
                    c.wait("brk")
                    if h >= 2:
                        c.wait("log_a")
                    o, b = acc[:, 2 + h % 2], k_b[:, h % 2]
                    MM(o[:, 0:T], k_tri, b[:, 0:T], start=True, stop=False, skip_group_check=True)
                    MM(o[:, P:T], ones, b[:, T:T + P], start=False, stop=False, skip_group_check=True)
                    c.up(MM(o[:, T:T + P], k_tri, b[:, T:T + P], start=False, stop=True, skip_group_check=True),
                         "remain")
                if n >= 4:
                    h = n - 4
                    m, r = h // 2, HD * (h % 2)
                    c.wait("a_sb")
                    if h % 2 == 0 and m >= 2:
                        pe.wait_ge(sem("hi_ready"), KT * UNIT["stick"] + m - 1)
                    o = aux[m % 2][r:r + HD]
                    MM(o[:, 0:T], k_v[:, 0, h * HD:(h + 1) * HD], k_a[:, h % 2, 0:T], start=True, stop=False,
                       tile_position=(0, r), skip_group_check=True)
                    ins = MM(o[:, P:T], k_v[:, 1, h * HD:(h + 1) * HD], k_a[:, h % 2, T:T + P], start=False,
                             stop=True, tile_position=(0, r), skip_group_check=True)
                    c.up(ins, "stick_pv")
            S = START["out"]
            slot_part("stick", S, first, range(6, KT))
            for g in range(1, 4):
                up_slot("stick", S + g)
            ffn(3, "ffn3")


def _up(*cols):
    w = np.concatenate(cols, axis=1)
    if w.shape[1] < 256:
        w = np.pad(w, ((0, 0), (0, 256 - w.shape[1])))
    return w.reshape(KT, P, 256).transpose(1, 0, 2).reshape(P, 2048)


def _down(rows):
    return rows.reshape(2, P, D).transpose(1, 0, 2).reshape(P, 2048)


def _pieces(w, n=256):
    return [w[:, i:i + n] for i in range(0, w.shape[1], n)]


def _ffn_slots(gate, val, down):
    ups = [_up(gate[:, n * P:(n + 1) * P], val[:, n * P:(n + 1) * P]) for n in range(2 * STEPS)]
    downs = [_down(down[j * 256:(j + 1) * 256]) for j in range(STEPS)]
    out = ups[0:2]
    for j in range(1, STEPS):
        out += [ups[2 * j], ups[2 * j + 1], downs[j - 1]]
    return out + [downs[STEPS - 1]]


def _stream(i):
    s = [_up(c) for c in _pieces(i["ssm_w_in"][0])]
    glu = i["ssm_w_glu"][0]
    s += [_up(glu[:, m * P:(m + 1) * P], glu[:, D + m * P:D + (m + 1) * P]) for m in range(KT)]

    def ffn(l):
        w = i["ffn_w_up"][l]
        return _ffn_slots(w[:, :FF], w[:, FF:], i["ffn_w_down"][l])

    def ple(l):
        g = [_up(c) for c in _pieces(i["ple_w_gate"][l])]
        return [_down(i["ple_w_proj"][l])] + g

    def qk(k, q):
        return [_up(c) for pair in zip(_pieces(k), _pieces(q)) for c in pair]

    kv, wq = i["kv_w"], i["attn_w_q"][0]
    s += ffn(0) + ple(0)
    s += [_up(c) for c in _pieces(kv[:, D:])] + qk(kv[:, :D], wq)
    s += [_up(c) for c in _pieces(i["attn_w_o"][0])] + ffn(1) + ple(1)
    w = i["ev_w_in_2"][0]
    q, k, v, qi, ki, wi, u = (w[:, a:b] for a, b in [(0, 512), (512, 640), (640, 768), (768, 1024), (1024, 1088),
                                                     (1088, 1092), (1092, 1604)])
    q = np.concatenate([q[:, c * 64:(c + 1) * 64] for t in range(4) for c in (t, t + 4)], axis=1)
    s += [_up(v, wi), _up(k, ki, ki), _up(qi), _up(q[:, :256]), _up(q[:, 256:]), _up(u[:, :256]), _up(u[:, 256:])]
    w = i["ev_w_out_2"][0]
    w = np.concatenate([w[c * 64:(c + 1) * 64] for t in range(4) for c in (t, t + 4)] + [w[512:]], axis=0)
    s += [_up(c) for c in _pieces(w)]
    s += _ffn_slots(i["ffn_w1_2"][0], i["ffn_w3_2"][0], i["ffn_w2_2"][0])
    w = i["od_w_qkv_2"][0]
    s += [_up(c) for c in _pieces(w[:, 2 * D:])] + qk(w[:, D:2 * D], w[:, :D])
    s += [_up(c) for c in _pieces(i["od_w_out_2"][0])]
    s += _ffn_slots(i["ffn_w1_2"][1], i["ffn_w3_2"][1], i["ffn_w2_2"][1])
    assert len(s) == N_SLOTS
    return np.stack(s)


def _features(v):
    return np.moveaxis(v.reshape(v.shape[:-1] + (KT, P)), -1, 0)


def _bucket():
    n = 255 - np.arange(384)
    nf = np.maximum(n, 16).astype(np.float32)
    large = 16 + (np.log(nf / np.float32(16)) / np.float32(math.log(8.0)) * np.float32(16)).astype(np.int32)
    b = np.where(n < 16, n, np.minimum(large, 31))
    oh = np.zeros((33, 384), np.float32)
    for m in range(384):
        oh[b[m] if n[m] >= 0 else 32, m] = 1.0
    return oh


def _layout(i):
    f = np.float32
    i = {k: np.asarray(v) for k, v in i.items()}
    a = {"stream": _stream(i)}
    a["x"] = i["x"][0].T.reshape(KT, P, T).transpose(1, 0, 2)
    for l in range(2):
        a[f"p{l}"] = i["p"][l, 0].T.reshape(2, P, T).transpose(1, 0, 2)
    gains = np.stack([i["ssm_norm"][0], i["ffn_norm"][0], i["ple_norm"][0], i["kv_norm"], i["attn_norm"][0],
                      i["ffn_norm"][1], i["ple_norm"][1], i["norm_mix_g_2"][0], i["norm_ffn_g_2"][0],
                      i["norm_mix_g_2"][1], i["norm_ffn_g_2"][1]])
    cw = np.concatenate([i["ffn_conv_w"], i["ffn_conv_b"][:, None]], axis=1).reshape(2, 4, 2, 22, P)
    cw = cw.transpose(4, 0, 3, 2, 1).reshape(P, -1)
    col = lambda v: np.concatenate([v, v])[:, None]
    lam = np.zeros((P, 4), f)
    for j, n in enumerate(["lambda_q1", "lambda_q2", "lambda_k1", "lambda_k2"]):
        lam[:64, j] = i[n][0]
    a["par"] = np.concatenate([
        _features(gains).reshape(P, -1), cw, _features(i["ssm_d"][0]), col(i["k_norm"]), col(i["q_norm"][0]),
        i["subln"][0][:, None], col(i["ev_k_norm_g_2"][0]), col(i["ev_q_norm_g_2"][0]), lam,
        i["ev_pool_scale_2"][0].reshape(4, P).T, np.ones((P, P), f), np.eye(P, dtype=f)], axis=1)
    pairs = lambda v: v.reshape(PAIRS, P).T
    dt = np.repeat(i["ssm_log_dt"][0][:, None], STATE, axis=1)
    a["s5_par"] = np.stack([pairs(i["ssm_lambda_re"][0]), pairs(i["ssm_lambda_im"][0]), pairs(dt)], axis=1)
    b = np.zeros((4, 32, 2, KT, P), f)
    cc = np.zeros((P, 2, PAIRS, 32), f)
    for r, (nb, ncn) in enumerate([("ssm_b_re", "ssm_c_re"), ("ssm_b_im", "ssm_c_im")]):
        bb, c_ = i[nb][0], i[ncn][0]
        for g in range(GROUPS):
            pr, h = g // 2, g % 2
            b[pr % 4, h * 16:h * 16 + 16, r, pr // 4, h * 64:h * 64 + 64] = bb[g].T
            cc[h * 64:h * 64 + 64, r, pr, h * 16:h * 16 + 16] = c_[g].T
    a["s5_b"], a["s5_c"] = b.reshape(P, 2, KT, P), cc
    a["tmat"] = np.broadcast_to(np.arange(P, dtype=f), (P, P))
    wb = np.concatenate([i["rel_bias"], np.full((1, HEADS), NEG, f)])
    a["bias_oh"] = np.concatenate([_bucket(), wb], axis=1)
    q, k = np.arange(P)[:, None], np.arange(T)[None, :]
    a["causal"] = np.stack([np.where(k <= q + P * j, 0, NEG) for j in range(2)], axis=1).astype(f)
    cnt = np.stack([1.0 / np.minimum(np.arange(1, T + 1), w) for w in (2, 4, 8, 16)]).astype(f)
    a["count"] = np.broadcast_to(cnt, (P, 4, T))
    a["halves"] = np.kron(np.eye(2), np.ones((HD, HD))).astype(f)
    a["pool_w"] = i["ev_pool_w_2"][0].transpose(1, 0, 2)
    s_, q_ = np.arange(P)[:, None], np.arange(T)[None, :]
    a["stickmask"] = np.concatenate([np.where(s_ < q_, 0, NEG), np.where(s_ < q_[:, :P], 0, NEG)], axis=1).astype(f)
    a["tri"] = (np.arange(P)[:, None] >= np.arange(P)[None, :]).astype(f)
    return {k: np.ascontiguousarray(v) for k, v in a.items()}


def kernel(**inputs):
    import concourse.bacc as bacc
    from concourse.bass_utils import run_bass_kernel_spmd

    arrays = _layout(inputs)
    nc = bacc.Bacc("TRN2", target_bir_lowering=False, num_devices=1)
    f32 = mybir.dt.float32
    a = {k: nc.dram_tensor(f"in_{k}", v.shape, f32, kind="ExternalInput").ap() for k, v in arrays.items()}
    scratch = nc.dram_tensor("bias_rows", (HEADS * P * 384,), f32, kind="Internal").ap()
    a["scratch"] = scratch.rearrange("(h p m) -> h p m", h=HEADS, p=P)
    a["scratch_toeplitz"] = bass.AP(tensor=scratch.tensor, offset=P - 1, ap=[[383, P], [P * 384, HEADS], [1, T]])
    out = nc.dram_tensor("out_x", (KT, P, T), f32, kind="ExternalOutput").ap()
    program(nc, a, out)
    r = run_bass_kernel_spmd(nc, [{f"in_{k}": v for k, v in arrays.items()}], core_ids=[0])
    return r.results[0]["out_x"].reshape(D, T).T.reshape(1, T, D)
```
